# Optimizing a Trainium2 kernel written in Bass

```python
import jax, jax.numpy as jnp
from jax import lax
import numpy as np

D_MODEL = 1024
BATCH = 1
SEQ = 512
DEPTH = 1

MEM_LEN = 256
FOX_HEADS = 8
FOX_HEAD_DIM = 64
DSA_HEADS = 8
DSA_HEAD_DIM = 64
IDX_HEADS = 8
IDX_DIM = 64
MEM_HEADS = 4
MEM_HEAD_DIM = 128
BRANCH_WIDTH = 512
N_BRANCHES = 3
D_FF = 2816
ROPE_THETA = 10000.0
Q_BLOCK = 128
TOPK_MAX = 256
EPS = 1e-6

SPLIT_SIZES = (
    BRANCH_WIDTH, BRANCH_WIDTH, BRANCH_WIDTH,
    FOX_HEADS,
    BRANCH_WIDTH, DSA_HEAD_DIM, DSA_HEAD_DIM,
    IDX_HEADS * IDX_DIM, IDX_DIM, IDX_HEADS,
    BRANCH_WIDTH,
    N_BRANCHES * D_MODEL,
)
SPLIT_POINTS = tuple(int(v) for v in np.cumsum(SPLIT_SIZES)[:-1])
D_IN = int(sum(SPLIT_SIZES))


def rmsnorm(x, g):
    xf = x.astype(jnp.float32)
    y = xf * lax.rsqrt(jnp.mean(xf * xf, axis=-1, keepdims=True) + EPS)
    return (y * g.astype(jnp.float32)).astype(x.dtype)

def swiglu(x, w_gate, w_up, w_down):
    return (jax.nn.silu(x @ w_gate) * (x @ w_up)) @ w_down

def rope_tables(positions, dim, dtype):
    inv_freq = ROPE_THETA ** (-jnp.arange(0, dim, 2, dtype=jnp.float32) / dim)
    ang = positions.astype(jnp.float32)[..., None] * inv_freq
    return jnp.cos(ang)[:, :, None, :].astype(dtype), jnp.sin(ang)[:, :, None, :].astype(dtype)

def rope(x, cos, sin):
    x1, x2 = jnp.split(x, 2, axis=-1)
    return jnp.concatenate([x1 * cos - x2 * sin, x2 * cos + x1 * sin], axis=-1)

def to_blocks(a):
    B, S = a.shape[:2]
    return a.reshape((B, S // Q_BLOCK, Q_BLOCK) + a.shape[2:]).swapaxes(0, 1)

def from_blocks(a):
    nb, B, Q = a.shape[:3]
    return a.swapaxes(0, 1).reshape((B, nb * Q) + a.shape[3:])

def fox_attention(q, k, v, logf):
    B, S, H, hd = q.shape
    c = jnp.cumsum(logf, axis=1)
    c_keys = c.transpose(0, 2, 1)
    key_pos = jnp.arange(S)
    scale = hd ** -0.5

    def block(args):
        qi, ci, bi = args
        qpos = bi * Q_BLOCK + jnp.arange(Q_BLOCK)
        s = jnp.einsum('bqhd,bkhd->bhqk', qi, k).astype(jnp.float32) * scale
        s = s + ci.transpose(0, 2, 1)[..., None] - c_keys[:, :, None, :]
        s = jnp.where(key_pos[None, :] <= qpos[:, None], s, -jnp.inf)
        p = jax.nn.softmax(s, axis=-1)
        return jnp.einsum('bhqk,bkhd->bqhd', p.astype(v.dtype), v)

    out = lax.map(block, (to_blocks(q), to_blocks(c), jnp.arange(S // Q_BLOCK)))
    return from_blocks(out).reshape(B, S, H * hd)

def dsa_attention(q, k, v, iq, ik, iw, k_sel):
    B, S, H, hd = q.shape
    key_pos = jnp.arange(S)
    scale = hd ** -0.5
    gather = jax.vmap(lambda a, i: a[i])

    def block(args):
        qi, iqi, iwi, bi = args
        qpos = bi * Q_BLOCK + jnp.arange(Q_BLOCK)
        sc = jnp.einsum('bqhd,bkd->bqhk', iqi, ik).astype(jnp.float32)
        score = jnp.einsum('bqh,bqhk->bqk', iwi.astype(jnp.float32), jax.nn.relu(sc))
        score = jnp.where((key_pos[None, :] <= qpos[:, None])[None], score, -jnp.inf)
        _, idx = lax.top_k(score, k_sel)
        valid = idx <= qpos[None, :, None]
        ks = gather(k, idx)
        vs = gather(v, idx)
        s = jnp.einsum('bqhd,bqkd->bqhk', qi, ks).astype(jnp.float32) * scale
        s = jnp.where(valid[:, :, None, :], s, -jnp.inf)
        p = jax.nn.softmax(s, axis=-1)
        return jnp.einsum('bqhk,bqkd->bqhd', p.astype(vs.dtype), vs)

    out = lax.map(block, (to_blocks(q), to_blocks(iq), to_blocks(iw), jnp.arange(S // Q_BLOCK)))
    return from_blocks(out).reshape(B, S, H * hd)

def memory_attention(q, km, vm):
    B, S, H, hd = q.shape
    s = jnp.einsum('bshd,bmhd->bhsm', q, km).astype(jnp.float32) * hd ** -0.5
    p = jax.nn.softmax(s, axis=-1)
    return jnp.einsum('bhsm,bmhd->bshd', p.astype(vm.dtype), vm).reshape(B, S, H * hd)

def first_inputs(seed: int = 0) -> dict:
    key = jax.random.key(seed)
    ks = jax.random.split(key, 24)
    f32 = jnp.float32

    def w(k, shape, fan_in):
        return jax.random.normal(k, shape, f32) * fan_in ** -0.5

    def gain(k, shape):
        return 1.0 + 0.02 * jax.random.normal(k, shape, f32)

    L = DEPTH
    return {
        "x": jax.random.normal(ks[0], (BATCH, SEQ, D_MODEL), f32),
        "mem": jax.random.normal(ks[1], (BATCH, MEM_LEN, D_MODEL), f32),
        "positions": jnp.broadcast_to(jnp.arange(SEQ, dtype=jnp.int32), (BATCH, SEQ)),
        "ffn1_norm": gain(ks[2], (L, D_MODEL)),
        "ffn1_w_gate": w(ks[3], (L, D_MODEL, D_FF), D_MODEL),
        "ffn1_w_up": w(ks[4], (L, D_MODEL, D_FF), D_MODEL),
        "ffn1_w_down": w(ks[5], (L, D_FF, D_MODEL), D_FF),
        "mix_norm": gain(ks[6], (L, D_MODEL)),
        "mem_norm": gain(ks[7], (L, D_MODEL)),
        "w_in": w(ks[8], (L, D_MODEL, D_IN), D_MODEL),
        "b_forget": 3.0 + 0.5 * jax.random.normal(ks[9], (L, FOX_HEADS), f32),
        "fox_q_norm": gain(ks[10], (L, FOX_HEAD_DIM)),
        "fox_k_norm": gain(ks[11], (L, FOX_HEAD_DIM)),
        "dsa_q_norm": gain(ks[12], (L, DSA_HEAD_DIM)),
        "dsa_k_norm": gain(ks[13], (L, DSA_HEAD_DIM)),
        "mem_q_norm": gain(ks[14], (L, MEM_HEAD_DIM)),
        "mem_k_norm": gain(ks[15], (L, MEM_HEAD_DIM)),
        "w_mem_kv": w(ks[16], (L, D_MODEL, 2 * BRANCH_WIDTH), D_MODEL),
        "w_branch": w(ks[17], (L, N_BRANCHES, BRANCH_WIDTH, D_MODEL), BRANCH_WIDTH),
        "w_out": w(ks[18], (L, D_MODEL, D_MODEL), D_MODEL),
        "ffn2_norm": gain(ks[19], (L, D_MODEL)),
        "ffn2_w_gate": w(ks[20], (L, D_MODEL, D_FF), D_MODEL),
        "ffn2_w_up": w(ks[21], (L, D_MODEL, D_FF), D_MODEL),
        "ffn2_w_down": w(ks[22], (L, D_FF, D_MODEL), D_FF),
    }

def first_block(x, mem, positions, ffn1_norm, ffn1_w_gate, ffn1_w_up, ffn1_w_down, mix_norm,
              mem_norm, w_in, b_forget, fox_q_norm, fox_k_norm, dsa_q_norm, dsa_k_norm,
              mem_q_norm, mem_k_norm, w_mem_kv, w_branch, w_out, ffn2_norm, ffn2_w_gate,
              ffn2_w_up, ffn2_w_down):
    B, S, D = x.shape
    M = mem.shape[1]
    k_sel = min(TOPK_MAX, S // 4)
    cos, sin = rope_tables(positions, DSA_HEAD_DIM, x.dtype)
    cos_i, sin_i = rope_tables(positions, IDX_DIM, x.dtype)
    h = x
    for l in range(DEPTH):
        h = h + 0.5 * swiglu(rmsnorm(h, ffn1_norm[l]), ffn1_w_gate[l], ffn1_w_up[l], ffn1_w_down[l])

        u = rmsnorm(h, mix_norm[l])
        (fq, fk, fv, ff, dq, dk, dv, iq, ik, iw, mq, g) = jnp.split(u @ w_in[l], SPLIT_POINTS, axis=-1)

        fq = rmsnorm(fq.reshape(B, S, FOX_HEADS, FOX_HEAD_DIM), fox_q_norm[l])
        fk = rmsnorm(fk.reshape(B, S, FOX_HEADS, FOX_HEAD_DIM), fox_k_norm[l])
        fv = fv.reshape(B, S, FOX_HEADS, FOX_HEAD_DIM)
        logf = jax.nn.log_sigmoid(ff.astype(jnp.float32) + b_forget[l].astype(jnp.float32))
        o_a = fox_attention(fq, fk, fv, logf)

        dq = rope(rmsnorm(dq.reshape(B, S, DSA_HEADS, DSA_HEAD_DIM), dsa_q_norm[l]), cos, sin)
        dk = rope(rmsnorm(dk[:, :, None, :], dsa_k_norm[l]), cos, sin)[:, :, 0, :]
        iq = rope(iq.reshape(B, S, IDX_HEADS, IDX_DIM), cos_i, sin_i)
        ik = rope(ik[:, :, None, :], cos_i, sin_i)[:, :, 0, :]
        iw = iw * (IDX_HEADS ** -0.5 * IDX_DIM ** -0.5)
        o_b = dsa_attention(dq, dk, dv, iq, ik, iw, k_sel)

        km, vm = jnp.split(rmsnorm(mem, mem_norm[l]) @ w_mem_kv[l], 2, axis=-1)
        km = rmsnorm(km.reshape(B, M, MEM_HEADS, MEM_HEAD_DIM), mem_k_norm[l])
        vm = vm.reshape(B, M, MEM_HEADS, MEM_HEAD_DIM)
        mq = rmsnorm(mq.reshape(B, S, MEM_HEADS, MEM_HEAD_DIM), mem_q_norm[l])
        o_c = memory_attention(mq, km, vm)

        branches = jnp.stack([o_a, o_b, o_c], axis=2)
        proj = jnp.einsum('bsnw,nwd->bsnd', branches, w_branch[l])
        gates = jax.nn.sigmoid(g.reshape(B, S, N_BRANCHES, D))
        h = h + jnp.sum(gates * proj, axis=2) @ w_out[l]

        h = h + 0.5 * swiglu(rmsnorm(h, ffn2_norm[l]), ffn2_w_gate[l], ffn2_w_up[l], ffn2_w_down[l])
    return h


HEAD_DIM = 64
N_HEADS_A = 8
N_KV_A = 2
N_HEADS_B = 8
N_KV_B = 2
WIDTH_A = N_HEADS_A * HEAD_DIM
WIDTH_B = N_HEADS_B * HEAD_DIM
MIX_WIDTH = WIDTH_A + WIDTH_B
WINDOW = 128
GRID_W = 64
D_FF_2 = ((8 * D_MODEL + 3 * 256 - 1) // (3 * 256)) * 256
IN_COLS = (N_HEADS_A + 2 * N_KV_A + N_HEADS_B + 2 * N_KV_B) * HEAD_DIM
SPLITS = tuple(int(s) for s in np.cumsum([WIDTH_A, N_KV_A * HEAD_DIM, N_KV_A * HEAD_DIM,
                                           WIDTH_B, N_KV_B * HEAD_DIM])[:])


def rms_norm(x, g):
    xf = x.astype(jnp.float32)
    y = xf * lax.rsqrt(jnp.mean(xf * xf, axis=-1, keepdims=True) + EPS)
    return (y * g.astype(jnp.float32)).astype(x.dtype)

def apply_rope(x, ang):
    cos = jnp.cos(ang)[None, :, None, :].astype(x.dtype)
    sin = jnp.sin(ang)[None, :, None, :].astype(x.dtype)
    x1, x2 = jnp.split(x, 2, axis=-1)
    return jnp.concatenate([x1 * cos - x2 * sin, x2 * cos + x1 * sin], axis=-1)

def global_attention(q, k, v):
    B, S, Hq, D = q.shape
    Hkv = k.shape[2]
    G = Hq // Hkv
    nb = S // Q_BLOCK
    qb = q.reshape(B, nb, Q_BLOCK, Hkv, G, D).transpose(1, 0, 2, 3, 4, 5)
    scale = D ** -0.5

    def one_block(qi):
        s = jnp.einsum('bqkgd,bskd->bkgqs', qi, k).astype(jnp.float32) * scale
        p = jax.nn.softmax(s, axis=-1).astype(v.dtype)
        return jnp.einsum('bkgqs,bskd->bqkgd', p, v)

    o = lax.map(one_block, qb)
    return o.transpose(1, 0, 2, 3, 4, 5).reshape(B, S, Hq * D)

def window_attention(q, k, v, sink):
    B, S, Hq, D = q.shape
    Hkv = k.shape[2]
    G = Hq // Hkv
    nb = S // Q_BLOCK
    C = 3 * Q_BLOCK
    qb = q.reshape(B, nb, Q_BLOCK, Hkv, G, D)
    pad = ((0, 0), (Q_BLOCK, Q_BLOCK), (0, 0), (0, 0))
    kp = jnp.pad(k, pad).reshape(B, nb + 2, Q_BLOCK, Hkv, D)
    vp = jnp.pad(v, pad).reshape(B, nb + 2, Q_BLOCK, Hkv, D)
    kb = jnp.concatenate([kp[:, :-2], kp[:, 1:-1], kp[:, 2:]], axis=2)
    vb = jnp.concatenate([vp[:, :-2], vp[:, 1:-1], vp[:, 2:]], axis=2)
    scale = D ** -0.5
    s = jnp.einsum('bnqkgd,bnckd->bnkgqc', qb, kb).astype(jnp.float32) * scale
    blk = jnp.arange(nb)[:, None, None]
    qpos = blk * Q_BLOCK + jnp.arange(Q_BLOCK)[None, :, None]
    kpos = (blk - 1) * Q_BLOCK + jnp.arange(C)[None, None, :]
    valid = (jnp.abs(kpos - qpos) <= WINDOW) & (kpos >= 0) & (kpos < S)
    s = jnp.where(valid[None, :, None, None], s, -jnp.inf)
    sink_l = sink.astype(jnp.float32).reshape(1, 1, Hkv, G, 1, 1)
    m = jnp.maximum(jnp.max(s, axis=-1, keepdims=True), sink_l)
    e = jnp.exp(s - m)
    den = jnp.sum(e, axis=-1, keepdims=True) + jnp.exp(sink_l - m)
    p = (e / den).astype(v.dtype)
    o = jnp.einsum('bnkgqc,bnckd->bnqkgd', p, vb)
    return o.reshape(B, S, Hq * D)

def second_inputs(seed: int = 0) -> dict:
    key = jax.random.key(seed)
    ks = jax.random.split(key, 16)
    f32 = jnp.float32

    def gain(k, n):
        return 1.0 + 0.05 * jax.random.normal(k, (DEPTH, n), f32)

    def dense(k, fan_in, fan_out):
        return jax.random.normal(k, (DEPTH, fan_in, fan_out), f32) * fan_in ** -0.5

    return {
        "x": jax.random.normal(ks[0], (BATCH, SEQ, D_MODEL), f32),
        "norm_mix_pre": gain(ks[1], D_MODEL),
        "w_in": dense(ks[2], D_MODEL, IN_COLS),
        "q_norm_a": gain(ks[3], HEAD_DIM),
        "k_norm_a": gain(ks[4], HEAD_DIM),
        "sink_b": 0.5 * jax.random.normal(ks[5], (DEPTH, N_HEADS_B), f32),
        "group_norm_a": gain(ks[6], WIDTH_A),
        "group_norm_b": gain(ks[7], WIDTH_B),
        "w_out": dense(ks[8], MIX_WIDTH, D_MODEL),
        "norm_mix_post": gain(ks[9], D_MODEL),
        "norm_ffn_pre": gain(ks[10], D_MODEL),
        "w_gate": dense(ks[11], D_MODEL, D_FF_2),
        "w_up": dense(ks[12], D_MODEL, D_FF_2),
        "w_down": dense(ks[13], D_FF_2, D_MODEL),
        "norm_ffn_post": gain(ks[14], D_MODEL),
    }

def second_block(x, norm_mix_pre, w_in, q_norm_a, k_norm_a, sink_b, group_norm_a, group_norm_b,
              w_out, norm_mix_post, norm_ffn_pre, w_gate, w_up, w_down, norm_ffn_post):
    B, S, _ = x.shape
    rows = S // GRID_W
    t = jnp.arange(S, dtype=jnp.float32)
    row = jnp.broadcast_to(jnp.arange(rows, dtype=jnp.float32)[:, None], (rows, GRID_W)).reshape(S)
    col = jnp.broadcast_to(jnp.arange(GRID_W, dtype=jnp.float32)[None, :], (rows, GRID_W)).reshape(S)
    ax_pairs = HEAD_DIM // 4
    freq_ax = ROPE_THETA ** (-jnp.arange(ax_pairs, dtype=jnp.float32) / ax_pairs)
    ang_axial = jnp.concatenate([row[:, None] * freq_ax[None, :], col[:, None] * freq_ax[None, :]], axis=-1)
    n_pairs = HEAD_DIM // 2
    freq_1d = ROPE_THETA ** (-jnp.arange(n_pairs, dtype=jnp.float32) / n_pairs)
    ang_1d = t[:, None] * freq_1d[None, :]

    for l in range(DEPTH):
        h = rms_norm(x, norm_mix_pre[l])
        proj = h @ w_in[l]
        qa, ka, va, qb, kb, vb = jnp.split(proj, SPLITS, axis=-1)

        qa = apply_rope(rms_norm(qa.reshape(B, S, N_HEADS_A, HEAD_DIM), q_norm_a[l]), ang_axial)
        ka = apply_rope(rms_norm(ka.reshape(B, S, N_KV_A, HEAD_DIM), k_norm_a[l]), ang_axial)
        va = va.reshape(B, S, N_KV_A, HEAD_DIM)
        out_a = global_attention(qa, ka, va)

        qb = apply_rope(qb.reshape(B, S, N_HEADS_B, HEAD_DIM), ang_1d)
        kb = apply_rope(kb.reshape(B, S, N_KV_B, HEAD_DIM), ang_1d)
        vb = vb.reshape(B, S, N_KV_B, HEAD_DIM)
        out_b = window_attention(qb, kb, vb, sink_b[l])

        mixed = jnp.concatenate([rms_norm(out_a, group_norm_a[l]),
                                 rms_norm(out_b, group_norm_b[l])], axis=-1) @ w_out[l]
        x = x + rms_norm(mixed, norm_mix_post[l])

        h = rms_norm(x, norm_ffn_pre[l])
        f = (jax.nn.silu(h @ w_gate[l]) * (h @ w_up[l])) @ w_down[l]
        x = x + rms_norm(f, norm_ffn_post[l])
    return x


def setup_inputs(seed=0):
    out = dict(first_inputs(seed))
    for name, value in second_inputs(seed + 1).items():
        if name != "x":
            out[name + "_2"] = value
    return out


def reference(
    x, mem, positions, ffn1_norm, ffn1_w_gate, ffn1_w_up, ffn1_w_down, mix_norm, mem_norm, w_in,
    b_forget, fox_q_norm, fox_k_norm, dsa_q_norm, dsa_k_norm, mem_q_norm, mem_k_norm, w_mem_kv,
    w_branch, w_out, ffn2_norm, ffn2_w_gate, ffn2_w_up, ffn2_w_down, norm_mix_pre_2, w_in_2,
    q_norm_a_2, k_norm_a_2, sink_b_2, group_norm_a_2, group_norm_b_2, w_out_2, norm_mix_post_2,
    norm_ffn_pre_2, w_gate_2, w_up_2, w_down_2, norm_ffn_post_2,
):
    x = first_block(
        x, mem, positions, ffn1_norm, ffn1_w_gate, ffn1_w_up, ffn1_w_down, mix_norm, mem_norm,
        w_in, b_forget, fox_q_norm, fox_k_norm, dsa_q_norm, dsa_k_norm, mem_q_norm, mem_k_norm,
        w_mem_kv, w_branch, w_out, ffn2_norm, ffn2_w_gate, ffn2_w_up, ffn2_w_down,
    )
    return second_block(
        x, norm_mix_pre_2, w_in_2, q_norm_a_2, k_norm_a_2, sink_b_2, group_norm_a_2,
        group_norm_b_2, w_out_2, norm_mix_post_2, norm_ffn_pre_2, w_gate_2, w_up_2, w_down_2,
        norm_ffn_post_2,
    )


_drawn_inputs = setup_inputs


def setup_inputs(seed=0):
    import zlib

    import numpy as np

    out = dict(_drawn_inputs(seed))
    spreads = {}
    factors = {'ffn1_norm': 3.6,
     'mix_norm': 3.261,
     'mem_norm': 8.0,
     'fox_q_norm': 8.0,
     'fox_k_norm': 8.0,
     'dsa_q_norm': 8.0,
     'dsa_k_norm': 8.0,
     'mem_q_norm': 8.0,
     'mem_k_norm': 8.0,
     'ffn2_norm': 5.041,
     'sink_b_2': 64.0,
     'norm_mix_pre_2': 7.77,
     'q_norm_a_2': 8.0,
     'k_norm_a_2': 8.0,
     'group_norm_a_2': 8.0,
     'group_norm_b_2': 8.0,
     'norm_mix_post_2': 8.0,
     'norm_ffn_pre_2': 8.0,
     'norm_ffn_post_2': 8.0}
    for name, (base, spread) in spreads.items():
        noise = np.random.default_rng([zlib.crc32(name.encode()), seed]).standard_normal(out[name].shape)
        drawn = base * np.exp(spread * noise) if base else spread * noise
        out[name] = __import__('jax').numpy.asarray(drawn.astype(out[name].dtype))
    for name, factor in factors.items():
        out[name] = (out[name] * factor).astype(out[name].dtype)
    return out
```

```python
from contextlib import ExitStack

import concourse.bass as bass
from concourse import mybir

ALU = mybir.AluOpType
ACT = mybir.ActivationFunctionType
AX = mybir.AxisListType
F32 = mybir.dt.float32
F32R = mybir.dt.float32r
I32 = mybir.dt.int32

P = 128
D = 1024
S = 512
MEM = 256
FF = 2816
HD = 64
KC = D // P
FT = FF // P
TT = S // P
MT = MEM // P
TOPK = 128
TOP_ROUNDS = TOPK // 8
N_ANGLE = 17
EPS = 1e-6
NEG = -1e30
TAKEN = -3e38
BW = 512
HEADS = 8

SIZES = (BW, BW, BW, HEADS, BW, HD, HD, BW, HD, HEADS, BW, 3 * D)
OFF = [sum(SIZES[:i]) for i in range(len(SIZES))]
FQ, FK, FV, FG, DQ, DK, DV, IQ, IK, IW, MQ, GT = OFF
D_IN = sum(SIZES)
QA, KA, VA, QB, KB, VB = 0, 512, 640, 768, 1280, 1408
D_IN2 = 1536

(G_F1, G_MIX, G_MEM, G_F2, G_PRE2, G_GN, G_POST2, G_FPRE2, G_FPOST2) = range(0, 72, 8)
G_FQ, G_FK, G_DQ, G_DK, G_MQ, G_MK, G_QA, G_KA, G_BF = range(72, 81)
N_GAIN = 82

C_ID, C_ONE, C_BLK, C_ROT, C_CAUSAL, C_UP, C_LOW, C_FREQ, C_SIGN = (
    0, 128, 256, 384, 512, 640, 768, 896, 897)
N_CONST = 898

U_GU1 = 0
U_DN1 = U_GU1 + 2 * FT
U_PREP = U_DN1 + FT
U_MEM = U_PREP + 4
U_FOX = U_MEM + 16
U_GATE = U_FOX + 16
U_BR = U_GATE + 24
U_WO = U_BR + 12
U_GU2 = U_WO + 8
U_DN2 = U_GU2 + 2 * FT
U_B2 = U_DN2 + FT
U_WO2 = U_B2 + 16
U_GU3 = U_WO2 + 8
U_DN3 = U_GU3 + 2 * FT
N_UNITS = U_DN3 + FT
RAW = 4
SPL = 2


def two_blocks(nc, t, out):
    ctx = ExitStack()
    with ctx:
        def sem(name):
            return ctx.enter_context(nc.semaphore(name))

        top = [(nc.sbuf_base + 63) // 64 * 64]

        def at(name, shape, addr, dt=F32):
            return nc.alloc_sbuf_tensor_at(name, shape, dt, offset=addr)

        def size(shape):
            n = 4
            for s in shape[1:]:
                n *= s
            return n

        def place(name, shape, dt=F32):
            a = top[0]
            top[0] += (size(shape) + 31) // 32 * 32
            return at(name, shape, a, dt)

        raw = place("raw", [P, RAW, D])
        w_hi = place("w_hi", [P, SPL, D], F32R)
        w_lo = place("w_lo", [P, SPL, D], F32R)
        hT = place("hT", [P, KC, S])
        const = place("const", [P, N_CONST + 2])
        ident_r = place("ident_r", [P, P], F32R)
        masks_r = place("masks_r", [P, 3, P], F32R)
        gain = place("gain", [P, N_GAIN + 2])
        cos1 = place("cos1", [P, S])
        sin1 = place("sin1", [P, S])
        iw_tok = place("iw_tok", [P, TT, HEADS])
        negmax = place("negmax", [P, 8])
        rowsum = place("rowsum", [P, 8])
        rowinv = place("rowinv", [P, 8])
        sink = place("sink", [P, HEADS])
        sinkexp = place("sinkexp", [P, 8])
        best8 = place("best8", [P, TT, 8])
        work = place("work", [P, 10, S])
        W = [work[:, i, :] for i in range(10)]
        ident = const[:, C_ID:C_ID + P]
        ones = const[:, C_ONE:C_ONE + P]
        blk64 = const[:, C_BLK:C_BLK + P]
        rot = const[:, C_ROT:C_ROT + P]

        base = top[0]
        u_at = base
        u_hi = at("u_hi", [P, KC, S], u_at, F32R)
        u_lo = at("u_lo", [P, KC, S], u_at + 16384, F32R)
        o_at = u_at + 32768
        x_at = o_at + 24576
        s_at = x_at + 24576
        assert s_at + 49152 <= nc.sbuf_usable_end, (s_at + 49152, nc.sbuf_usable_end)
        a_at = o_at
        x_tok = at("x_tok", [P, TT, D], a_at)
        gain_rows = at("gain_rows", [N_GAIN, P], a_at + 16384)
        pos_i = at("pos_i", [P, S], a_at + FT * 4096, I32)
        hid_hi = at("hid_hi", [P, FT, S], a_at, F32R)
        hid_lo = at("hid_lo", [P, FT, S], a_at + FT * 2048, F32R)

        oT = at("oT", [P, 12, S], o_at)
        score = at("score", [P, TT, S], o_at + 4 * 2048)
        iq = at("iq", [P, 4, S], x_at)
        topmask = at("topmask", [P, TT, S], x_at, F32R)
        dq = at("dq", [P, 4, S], x_at + 8192)
        ik = at("ik", [P, S], x_at + 16384)
        dk = at("dk", [P, S], x_at + 18432)
        dvT = at("dvT", [P, S], x_at + 20480)
        c_sum = at("c_sum", [32 + HEADS, S], x_at + 22528, F32R)
        m_tok = at("m_tok", [P, MT, D], s_at)
        mT = at("mT", [P, KC, MEM], s_at + 8192)
        m_hi = at("m_hi", [P, KC, MEM], s_at + 16384, F32R)
        m_lo = at("m_lo", [P, KC, MEM], s_at + 24576, F32R)

        def staging(tag, a, nk, ncol):
            kw = nk * P
            names = (("qh", [P, S]), ("ql", [P, S]), ("kh", [P, kw]), ("kl", [P, kw]),
                     ("vh", [P, nk, ncol]), ("vl", [P, nk, ncol]),
                     ("ph", [P, nk, S]), ("pl", [P, nk, S]))
            d = {}
            for n, shape in names:
                d[n] = at(tag + n, shape, a, F32R)
                a += size(shape)
            return d, a

        mst, e_at = staging("m_", s_at + 32768, MT, P)
        assert e_at <= s_at + 49152
        fst, e_at = staging("f_", s_at, TT, P)
        c_q = at("c_q", [4, 2, S], e_at, F32R)
        c_k = at("c_k", [4, 2, S], e_at + 4096, F32R)
        assert e_at + 8192 <= s_at + 49152
        ist = {n: at("i_" + n, [P, S], s_at + 2048 * i, F32R) for i, n in enumerate(("qh", "ql", "kh", "kl"))}
        sig = at("sig", [P, 24, S], s_at)
        dst, e_at = staging("d_", u_at, TT, P)
        assert e_at <= o_at
        o_hi = at("o_hi", [P, 12, S], u_at, F32R)
        o_lo = at("o_lo", [P, 12, S], x_at, F32R)
        mix_lo = at("mix_lo", [P, KC, S], u_at + 24576, F32R)
        mix_hi = at("mix_hi", [P, KC, S], u_at + 24576 + 16384, F32R)
        o2T = at("o2T", [P, KC, S], a_at)
        tab2 = at("tab2", [P, 4, S], a_at + 16384)
        b2a = a_at + 24576
        ast, b2a = staging("a_", b2a, TT, P)
        bst = {}
        for n, shape in (("kh", [P, S]), ("kl", [P, S]), ("vh", [P, TT, P]), ("vl", [P, TT, P])):
            bst[n] = at("b_" + n, shape, b2a, F32R)
            b2a += size(shape)
        bst["ph"], bst["pl"] = ast["ph"], ast["pl"]
        q2 = []
        for i in range(4):
            q2.append((at(f"q2h{i}", [P, S], b2a, F32R), at(f"q2l{i}", [P, S], b2a + 2048, F32R)))
            b2a += 4096
        rtmp = at("rtmp", [P, 10, S], b2a)
        assert b2a + 10 * 2048 <= nc.sbuf_usable_end
        fT = at("fT", [P, KC, S], u_at)
        mo = at("mo", [P, KC, S], a_at + 16384)
        out_tok = at("out_tok", [P, 2, D], a_at)

        c_dram = nc.dram_tensor("forget_sums", (2, HEADS, S), F32, kind="Internal").ap()
        bank = [ctx.enter_context(nc.psum_tensor(f"bank{i}", [P, S], F32)) for i in range(8)]

        raw_loaded = [sem(f"raw_loaded{i}") for i in range(RAW)]
        c_stored = sem("c_stored")
        part_loaded = sem("part_loaded")
        hi_done = sem("hi_done")
        split_ready = sem("split_ready")
        unit_done = sem("unit_done")
        ld_const, ld_gain, ld_x, ld_pos, ld_mem, ld_tab, ld_sink, ld_c = (
            sem(n) for n in ("ld_const", "ld_gain", "ld_x", "ld_pos", "ld_mem", "ld_tab", "ld_sink",
                             "ld_c"))
        stored = [sem("stored0"), sem("stored1")]
        gain_zero, gain_t, gain_ready, const_r, xt_done, x_ready, trig, trig_a = (
            sem(n) for n in ("gain_zero", "gain_t", "gain_ready", "const_r", "xt_done", "x_ready", "trig",
                             "trig_a"))
        n_sq, n_acc, n_std, n_rec, n_t, n_hi, n_lo = (
            sem("n_" + n) for n in ("sq", "acc", "std", "rec", "t", "hi", "lo"))
        f_silu, f_prod, f_hi, f_lo, f_out = (sem("f_" + n) for n in ("silu", "prod", "hi", "lo", "out"))
        h_sq, h_raw, h_sum, h_std, h_rec, h_out = (
            sem("h_" + n) for n in ("sq", "raw", "sum", "std", "rec", "out"))
        r_raw, r_rot, r_cos, r_sin, r_out = (sem("r_" + n) for n in ("raw", "rot", "cos", "sin", "out"))
        s_hi, s_lo = sem("s_hi"), sem("s_lo")
        v_raw, v_t = sem("v_raw"), sem("v_t")
        a_s, a_max, a_exp, a_rec, a_p, a_t, a_ph, a_pl, a_pv, a_o = (
            sem("a_" + n) for n in ("s", "max", "exp", "rec", "p", "t", "ph", "pl", "pv", "o"))
        a_sink, a_den = sem("a_sink"), sem("a_den")
        iw_t, iw_ready, fg, fg_a, c_ready, c_one = (
            sem(n) for n in ("iw_t", "iw_ready", "fg", "fg_a", "c_ready", "c_one"))
        ix_s, ix_relu, ix_acc, tk_max, tk_rep, tk_mask = (
            sem(n) for n in ("ix_s", "ix_relu", "ix_acc", "tk_max", "tk_rep", "tk_mask"))
        g_sig, o_split_hi, o_split, b_mul, b_add, b_hi, b_lo, res = (
            sem(n) for n in ("g_sig", "o_split_hi", "o_split", "b_mul", "b_add", "b_hi", "b_lo", "res"))
        mt_done, m_ready, ot_done, o_ready_a, o_ready_b = (
            sem(n) for n in ("mt_done", "m_ready", "ot_done", "o_ready_a", "o_ready_b"))

        block = ctx.enter_context(nc.Block())

        def cols(w, a, n=P):
            return w.rearrange("(c p) n -> p c n", p=P)[:, :, bass.ds(a, n)]

        def raw_as(slot, c):
            return raw[:, slot, :].rearrange("p (c n) -> p c n", c=c)

        @block.sync
        def _(sp):
            wait_value = sp.alloc_register("wait_value")

            def value(v):
                if isinstance(v, int):
                    return v
                sp.reg_mov(wait_value, v)
                return wait_value

            def unit(u, slot, dst, src):
                if not (isinstance(u, int) and u < RAW):
                    free = value(u - RAW + 1)
                    sp.wait_ge(split_ready, 1)
                    sp.wait_ge(split_ready, free)
                sp.dma_start(dst, src).then_inc(raw_loaded[slot], 16)

            def panel(u, slot, w, a):
                unit(u, slot, raw_as(slot, KC), cols(w, a))

            def halves(u, slot, w, one, two, n):
                dst = raw_as(slot, KC)
                free = value(u - RAW + 1)
                sp.wait_ge(split_ready, 1)
                sp.wait_ge(split_ready, free)
                sp.dma_start(dst[:, :, one[0]:one[0] + n], cols(w, one[1], n)).then_inc(part_loaded, 16)
                first = value(16 * (part_count(u) + 1))
                sp.wait_ge(split_ready, 1)
                sp.wait_ge(part_loaded, first)
                sp.dma_start(dst[:, :, two[0]:two[0] + n], cols(w, two[1], n)).then_inc(raw_loaded[slot], 16)

            def twice(u, slot, w, a):
                halves(u, slot, w, (0, a), (HD, a), HD)

            def ffn(u0, gate, up, down):
                def four(i):
                    for k in range(4):
                        panel(u0 + 4 * i + k, (u0 + k) % RAW, (gate, up)[k % 2], (2 * i + k // 2) * P)
                start = 0
                if u0 == 0:
                    four(0)
                    start = 1
                with sp.Fori(start, FT // 2) as i:
                    four(i)
                d0 = u0 + 2 * FT

                def rows(j, k):
                    slot = (d0 + k) % RAW
                    unit(d0 + j, slot, raw[:, slot, :], down[bass.ds(j * P, P), :])
                with sp.Fori(0, FT // 4) as i:
                    for k in range(4):
                        rows(4 * i + k, k)
                for k in range(FT % 4):
                    rows(FT // 4 * 4 + k, k)

            def part_count(u):
                if isinstance(u, int):
                    return u - U_PREP
                return parts_before[0]

            parts_before = [0]
            ffn(U_GU1, t["ffn1_w_gate"][0], t["ffn1_w_up"][0], t["ffn1_w_down"][0])
            w_in = t["w_in"][0]
            slot = U_PREP % RAW
            halves(U_PREP, slot, w_in, (0, FG), (32, IW), HEADS)
            for k, a in enumerate((IK, DK, DV)):
                twice(U_PREP + 1 + k, (U_PREP + 1 + k) % RAW, w_in, a)
            kv = t["w_mem_kv"][0]
            with sp.Fori(0, 4) as i:
                for k, (w, a) in enumerate(((w_in, MQ), (kv, 0), (kv, BW), (w_in, IQ))):
                    panel(U_MEM + 4 * i + k, (U_MEM + k) % RAW, w, a + i * P)
            with sp.Fori(0, 4) as i:
                for k, a in enumerate((FQ, FK, FV, DQ)):
                    panel(U_FOX + 4 * i + k, (U_FOX + k) % RAW, w_in, a + i * P)
            with sp.Fori(0, 6) as i:
                for k in range(4):
                    panel(U_GATE + 4 * i + k, (U_GATE + k) % RAW, w_in, GT + (4 * i + k) * P)
            for mp in range(4):
                for n in range(3):
                    k = 3 * mp + n
                    slot = (U_BR + k) % RAW
                    unit(U_BR + k, slot, raw_as(slot, 4), cols(t["w_branch"][0, n], mp * 2 * P, 2 * P))

            def w_out(u0, w):
                with sp.Fori(0, 2) as i:
                    for k in range(4):
                        panel(u0 + 4 * i + k, (u0 + k) % RAW, w, (4 * i + k) * P)
            w_out(U_WO, t["w_out"][0])
            ffn(U_GU2, t["ffn2_w_gate"][0], t["ffn2_w_up"][0], t["ffn2_w_down"][0])
            w2 = t["w_in_2"][0]
            with sp.Fori(0, 2) as i:
                u = U_B2 + 8 * i
                for k, a in enumerate((KA, VA, KB, VB)):
                    parts_before[0] = 4 + 4 * i + k
                    twice(u + k, (U_B2 + k) % RAW, w2, a + i * HD)
                for k, a in enumerate((QA, QB, QA + P, QB + P)):
                    panel(u + 4 + k, (U_B2 + k) % RAW, w2, a + i * 2 * P)
            w_out(U_WO2, t["w_out_2"][0])
            ffn(U_GU3, t["w_gate_2"][0], t["w_up_2"][0], t["w_down_2"][0])
            for i in range(TT):
                sp.wait_ge(o_ready_a, i + 1)
                sp.wait_ge(o_ready_b, i + 1)
                sp.dma_start(out[0, i * P:(i + 1) * P, :], out_tok[:, i % 2, :]).then_inc(stored[i % 2], 16)
            for s in stored:
                sp.wait_ge(s, 16 * TT // 2)

        @block.gpsimd
        def _(pool):
            loaded_value, used_value = pool.alloc_register("loaded_value"), pool.alloc_register("used_value")

            def value(reg, v):
                if isinstance(v, int):
                    return v
                pool.reg_mov(reg, v)
                return reg

            def split(u, i, k):
                first = isinstance(u, int) and u < SPL
                loaded = value(loaded_value, 16 * (i + 1))
                used = value(used_value, u - SPL + 1)
                pool.wait_ge(raw_loaded[k], 16)
                pool.wait_ge(raw_loaded[k], loaded)
                if not first:
                    pool.wait_ge(unit_done, used)
                s = k % SPL
                pool.tensor_scalar(w_hi[:, s, :], raw[:, k, :], 1.0, 1.0, ALU.mult, ALU.mult).then_inc(hi_done, 1)
                pool.wait_ge(hi_done, u + 1)
                pool.tensor_tensor(w_lo[:, s, :], raw[:, k, :], w_hi[:, s, :].bitcast(F32),
                                   ALU.subtract).then_inc(split_ready, 1)
            for k in range(RAW):
                split(k, 0, k)
            with pool.Fori(1, N_UNITS // RAW) as i:
                for k in range(RAW):
                    split(4 * i + k, i, k)
            for k in range(N_UNITS % RAW):
                split(N_UNITS // RAW * RAW + k, N_UNITS // RAW, k)

        N_F1, N_MIX, N_MEM, N_F2, N_PRE, N_GRP, N_POST, N_FPRE, N_FPOST = range(9)
        SPLITS = {N_F1: 0, N_MIX: 1, N_MEM: 2, N_F2: 3, N_PRE: 4, N_GRP: 5, N_FPRE: 6}
        H_PREP, H_MEM, H_FOX, H_B2 = 0, 1, 9, 21
        R_PREP, R_MEM, R_FOX, R_B2 = 0, 2, 6, 10
        RR_PREP, RR_MEM, RR_B2 = 0, 2, 6
        S_MEM, S_FOX, S_IDX, S_DSA, S_B2 = 0, 12, 24, 29, 35
        VR_PREP, VR_MEM, VR_FOX, VR_B2 = 0, 1, 5, 9
        VT_MEM, VT_FOX, VT_DSA, VT_B2 = 0, 4, 8, 9
        A_MEM, A_FOX, A_DSA, A_B2 = (0, 0, 0), (16, 4, 8), (48, 12, 40), (80, 20, 72)

        def causal(qt):
            return 0, qt + 1

        def window(qt):
            return max(0, qt - 1), min(TT, qt + 2)

        def whole(qt):
            return 0, TT

        def memory(qt):
            return 0, MT

        def q_blocks(keys, kb):
            q = [i for i in range(TT) if keys(i)[0] <= kb < keys(i)[1]]
            return q[0], q[-1] + 1

        @block.tensor
        def _(pe):
            def unit_mm(u, outs, rhs_hi, rhs_lo, n=S, per=None, before=None):
                slot = per[0] if per else 0
                pe.wait_ge(split_ready, u + 1)
                for c in range(KC):
                    if before:
                        before(c)
                    wh = w_hi[:, slot, c * P:(c + 1) * P]
                    wl = w_lo[:, slot, c * P:(c + 1) * P]
                    pe.matmul(outs[:, 0:n], wh, rhs_hi[:, c, :], start=(c == 0), stop=False)
                    pe.matmul(outs[:, 0:n], wh, rhs_lo[:, c, :], start=False, stop=False)
                    last = pe.matmul(outs[:, 0:n], wl, rhs_hi[:, c, :], start=False, stop=(c == KC - 1))
                last.then_inc(unit_done, 1)

            def panel(u, slot, b, rhs, before=None):
                unit_mm(u, bank[b], rhs[0], rhs[1], per=(slot,), before=before)

            U = (u_hi, u_lo)

            def norm_sum(ni, n=S, groups=1):
                per = KC // groups
                for c in range(KC):
                    pe.wait_ge(n_sq, ni * KC + c + 1)
                    pe.matmul(bank[c // per][:, 0:n], ones, W[c % 2][:, 0:n], start=(c % per == 0),
                              stop=(c % per == per - 1)).then_inc(n_acc, 1)

            def norm_wait(ni):
                def before(c):
                    pe.wait_ge(n_lo, SPLITS[ni] * KC + c + 1)
                return before

            def ffn(fi, u0, ni):
                def two(it, first):
                    for k in range(2):
                        f = 2 * it + k
                        u = u0 + 4 * it + 2 * k
                        if not first:
                            pe.wait_ge(f_silu, fi * FT + f - 1)
                        panel(u, 0, 2 * k, U, norm_wait(ni) if first and k == 0 else None)
                        if not first:
                            pe.wait_ge(f_prod, fi * FT + f - 1)
                        panel(u + 1, 1, 2 * k + 1, U)
                two(0, True)
                with pe.Fori(1, FT // 2) as it:
                    two(it, False)
                d0 = u0 + 2 * FT

                def down(j, slot, start, stop):
                    pe.wait_ge(split_ready, d0 + j + 1)
                    pe.wait_ge(f_lo, fi * FT + j + 1)
                    for m in (4, 5, 6, 7, 0, 1, 2, 3):
                        if start and m == 0:
                            pe.wait_ge(f_prod, fi * FT + FT)
                        wh = w_hi[:, slot, m * P:(m + 1) * P]
                        wl = w_lo[:, slot, m * P:(m + 1) * P]
                        pe.matmul(bank[m][:], wh, hid_hi[:, j, :], start=start, stop=False)
                        pe.matmul(bank[m][:], wh, hid_lo[:, j, :], start=False, stop=False)
                        last = pe.matmul(bank[m][:], wl, hid_hi[:, j, :], start=False, stop=stop)
                    last.then_inc(unit_done, 1)
                down(0, 0, True, False)
                down(1, 1, False, False)
                with pe.Fori(1, FT // 2 - 1) as it:
                    for k in range(2):
                        down(2 * it + k, k, False, False)
                down(FT - 2, 0, False, False)
                down(FT - 1, 1, False, True)

            def head_sum(i, b, sq, m, n=S):
                pe.wait_ge(h_sq, i + 1)
                pe.matmul(bank[b][:, 0:n], m, sq[:, 0:n], start=True, stop=True).then_inc(h_sum, 1)

            def rotate(b, src):
                pe.matmul(bank[b][:], rot, src, start=True, stop=True).then_inc(r_rot, 1)

            def values(i_raw, b, src, n=TT):
                pe.wait_ge(v_raw, i_raw + 1)
                for kb in range(n):
                    last = pe.transpose(bank[b][:, kb * P:(kb + 1) * P], src[:, kb * P:(kb + 1) * P], ident)
                last.then_inc(v_t, 1)

            def attend(done, st, keys, heads, rows, kT, q=None, extra=None, o_banks=(6, 7), wait_o=True):
                t0, h0, e0 = done
                qh, ql = q or (st["qh"], st["ql"])
                kh, kl = kT
                nk = max(keys(i)[1] for i in range(TT))
                nt = heads * TT

                def scores(n):
                    e, qt = n // TT, n % TT
                    lo, hi = keys(qt)
                    b = bank[n % 2][:, 0:(hi - lo) * P]
                    r0, r1 = (0, P) if rows == P else (e * rows, (e + 1) * rows)
                    if n >= 2 or not isinstance(t0, int) or t0 + n - 1 > 0:
                        pe.wait_ge(a_exp, t0 + n - 1)
                    q_cols = slice(qt * P, (qt + 1) * P)
                    k_cols = slice(lo * P, hi * P)
                    more = extra(e, qt, lo, hi) if extra else []
                    pe.matmul(b, qh[r0:r1, q_cols], kh[r0:r1, k_cols], start=True, stop=False)
                    for lhs, rhs, c0, c1 in more:
                        pe.matmul(bank[n % 2][:, c0:c1], lhs, rhs, start=False, stop=False)
                    pe.matmul(b, qh[r0:r1, q_cols], kl[r0:r1, k_cols], start=False, stop=False)
                    pe.matmul(b, ql[r0:r1, q_cols], kh[r0:r1, k_cols], start=False, stop=True).then_inc(a_s, 1)

                def transposes(n):
                    e, qt = n // TT, n % TT
                    lo, hi = keys(qt)
                    pe.wait_ge(a_p, t0 + n + 1)
                    if qt == 0 and e:
                        pe.wait_ge(a_pl, e0 + nk * e)
                    for kb in range(lo, hi):
                        last = pe.transpose(bank[2 + kb][:, qt * P:(qt + 1) * P],
                                            W[8 + n % 2][:, (kb - lo) * P:(kb - lo + 1) * P], ident)
                    last.then_inc(a_t, 1)

                def outputs(e):
                    pe.wait_ge(a_pl, e0 + nk * (e + 1))
                    if wait_o and not (isinstance(h0, int) and h0 + e - len(o_banks) + 1 <= 0):
                        pe.wait_ge(a_o, h0 + e - len(o_banks) + 1)
                    o = bank[o_banks[e % len(o_banks)]]
                    for g0, g1 in ((0, 2), (2, TT)) if keys is window else ((0, TT),):
                        some = [(kb, max(g0, q_blocks(keys, kb)[0]), min(g1, q_blocks(keys, kb)[1])) for kb in range(nk)]
                        some = [x for x in some if x[1] < x[2]]
                        full = [x for x in some if x[1:] == (g0, g1)][0]
                        steps = [(full, "vh", "ph")]
                        steps += [(x, v, p) for x in some if x != full
                                  for v, p in (("vh", "ph"), ("vh", "pl"), ("vl", "ph"))]
                        steps += [(full, "vh", "pl"), (full, "vl", "ph")]
                        for i, ((kb, q0, q1), v, p) in enumerate(steps):
                            c = slice(q0 * P, q1 * P)
                            last = pe.matmul(o[:, c], st[v][:, kb, :], st[p][:, kb, c], start=(i == 0),
                                             stop=(i == len(steps) - 1))
                    last.then_inc(a_pv, 1)

                scores(0)
                for n in range(1, nt):
                    scores(n)
                    if n > TT and n % TT == 1:
                        outputs(n // TT - 1)
                    transposes(n - 1)
                transposes(nt - 1)
                outputs(heads - 1)

            pe.wait_ge(ld_const, 16)
            pe.wait_ge(ld_gain, 16 * 25)
            pe.transpose(bank[7][:, 0:N_GAIN], gain_rows[:, :], ident[0:N_GAIN, 0:N_GAIN]).then_inc(gain_t, 1)
            pe.wait_ge(ld_x, 16)
            pe.wait_ge(gain_ready, 1)
            for c in range(KC):
                for i in range(TT):
                    last = pe.transpose(bank[c][:, i * P:(i + 1) * P], x_tok[:, i, c * P:(c + 1) * P], ident)
                last.then_inc(xt_done, 1)
            pe.wait_ge(x_ready, KC)

            norm_sum(N_F1)
            ffn(0, U_GU1, N_F1)

            pe.wait_ge(f_out, KC)
            norm_sum(N_MIX)
            for k in range(4):
                pe.wait_ge(n_std, N_MIX + 1)
                panel(U_PREP + k, k % SPL, k, U, norm_wait(N_MIX) if k == 0 else None)
            head_sum(H_PREP, 4, W[0], blk64)
            pe.wait_ge(r_raw, RR_PREP + 2)
            rotate(6, W[2])
            for i in range(TT):
                last = pe.transpose(bank[5][:, i * HD:(i + 1) * HD], W[7][0:HD, i * P:(i + 1) * P], ident[0:HD, 0:HD])
            last.then_inc(iw_t, 1)
            pe.wait_ge(h_out, H_PREP + 1)
            rotate(7, W[1])
            pe.wait_ge(ld_mem, 16)
            pe.wait_ge(r_out, R_PREP + 2)
            pe.wait_ge(iw_ready, 1)
            pe.wait_ge(v_raw, VR_PREP + 1)
            for c in range(KC):
                for i in range(MT):
                    last = pe.transpose(bank[c][:, i * P:(i + 1) * P], m_tok[:, i, c * P:(c + 1) * P], ident)
                last.then_inc(mt_done, 1)
            pe.wait_ge(m_ready, KC)
            norm_sum(N_MEM, MEM)
            pe.wait_ge(n_std, N_MEM + 1)

            def mem_head(i, first):
                u = U_MEM + 4 * i
                if not first:
                    pe.wait_ge(a_o, i)
                panel(u, 0, 2, U)
                unit_mm(u + 1, bank[3], m_hi, m_lo, n=MEM, per=(1,), before=norm_wait(N_MEM) if first else None)
                head_sum(H_MEM + 2 * i, 6, W[0], ones)
                unit_mm(u + 2, bank[4], m_hi, m_lo, n=MEM, per=(0,))
                head_sum(H_MEM + 2 * i + 1, 7, W[2], ones, MEM)
                panel(u + 3, 1, 5, U)
                values(VR_MEM + i, 1, W[4], MT)
                pe.wait_ge(h_std, H_MEM + 2 * i + 1)
                pe.wait_ge(r_raw, RR_MEM + i + 1)
                rotate(6, W[5])
                pe.wait_ge(s_lo, S_MEM + 3 * i + 3)
                pe.wait_ge(r_out, R_MEM + i + 1)
                attend((A_MEM[0] + 4 * i, A_MEM[1] + i, A_MEM[2] + 2 * i), mst, memory, 1, P,
                       (mst["kh"], mst["kl"]), o_banks=(6,), wait_o=False)
            mem_head(0, True)
            with pe.Fori(1, 4) as i:
                mem_head(i, False)

            def fox_pair(i, first):
                u = U_FOX + 4 * i
                pe.wait_ge(a_o, A_FOX[1] + 2 * i)
                panel(u, 0, 2, U)
                panel(u + 1, 1, 3, U)
                head_sum(H_FOX + 3 * i, 6, W[0], blk64)
                panel(u + 2, 0, 4, U)
                head_sum(H_FOX + 3 * i + 1, 7, W[2], blk64)
                panel(u + 3, 1, 5, U)
                values(VR_FOX + i, 1, W[6])
                head_sum(H_FOX + 3 * i + 2, 0, W[4], blk64)
                pe.wait_ge(h_out, H_FOX + 3 * i + 3)
                rotate(6, W[5])
                pe.wait_ge(s_lo, S_FOX + 3 * i + 3)
                pe.wait_ge(ld_c, 32 * (i + 1))
                pe.wait_ge(r_out, R_FOX + i + 1)

                def extra(e, qt, lo, hi):
                    return [(c_q[:, e, qt * P:(qt + 1) * P], c_k[:, e, lo * P:hi * P], 0, (hi - lo) * P),
                            (ident_r[:], masks_r[:, 0, :], qt * P, (qt + 1) * P)]
                attend((A_FOX[0] + 8 * i, A_FOX[1] + 2 * i, A_FOX[2] + 8 * i), fst, causal, 2, HD,
                       (fst["kh"], fst["kl"]), extra=extra)
            fox_pair(0, True)
            with pe.Fori(1, 4) as i:
                fox_pair(i, False)

            pe.wait_ge(a_o, A_DSA[1])
            pe.wait_ge(s_lo, S_IDX + 1)

            def index_pair(i, first):
                pe.wait_ge(s_lo, S_IDX + 2 + i)
                for k in range(6):
                    e, qt = k // 3, 1 + k % 3
                    n = (qt + 1) * P
                    r = slice(e * HD, (e + 1) * HD)
                    if not first or k >= 2:
                        pe.wait_ge(ix_relu, 6 * i + k - 1)
                    b = bank[k % 2][:, 0:n]
                    q = slice(qt * P, (qt + 1) * P)
                    pe.matmul(b, ist["qh"][r, q], ist["kh"][r, 0:n], start=True, stop=False)
                    pe.matmul(b, ist["qh"][r, q], ist["kl"][r, 0:n], start=False, stop=False)
                    pe.matmul(b, ist["ql"][r, q], ist["kh"][r, 0:n], start=False, stop=True).then_inc(ix_s, 1)
            index_pair(0, True)
            with pe.Fori(1, 4) as i:
                index_pair(i, False)

            def gates(i, first):
                for k in range(4):
                    if not first:
                        pe.wait_ge(g_sig, 4 * i + k - 3)
                    panel(U_GATE + 4 * i + k, k % SPL, 2 + k, U)
            gates(0, True)
            with pe.Fori(1, 6) as i:
                gates(i, False)

            pe.wait_ge(ix_relu, 24)
            pe.wait_ge(g_sig, 24)
            values(VR_PREP, 1, dvT)
            pe.wait_ge(s_lo, S_DSA + 2)
            pe.wait_ge(tk_mask, 3)

            def dsa_extra(e, qt, lo, hi):
                if qt == 0:
                    return [(ident_r[:], masks_r[:, 0, :], 0, P)]
                return [(ident_r[:], topmask[:, qt, 0:hi * P], 0, hi * P)]

            with pe.Fori(0, 4) as i:
                pe.wait_ge(s_lo, S_DSA + 3 + i)
                attend((A_DSA[0] + 8 * i, A_DSA[1] + 2 * i, A_DSA[2] + 8 * i), dst, causal, 2, HD,
                       (dst["kh"], dst["kl"]), extra=dsa_extra)

            pe.wait_ge(o_split, 3)
            pe.wait_ge(a_o, A_B2[1])

            def branches(it, first):
                for kk in range(6):
                    k = 6 * it + kk
                    n = kk % 3
                    slot = kk % SPL
                    if not first or kk >= 3:
                        pe.wait_ge(b_mul, 2 * k - 4)
                    pe.wait_ge(split_ready, U_BR + k + 1)
                    for half in range(2):
                        o = bank[2 * n + half][:]
                        for c in range(4):
                            a = c * 2 * P + half * P
                            oc = 4 * n + c
                            pe.matmul(o, w_hi[:, slot, a:a + P], o_hi[:, oc, :], start=(c == 0), stop=False)
                            pe.matmul(o, w_hi[:, slot, a:a + P], o_lo[:, oc, :], start=False, stop=False)
                            last = pe.matmul(o, w_lo[:, slot, a:a + P], o_hi[:, oc, :], start=False, stop=(c == 3))
                    last.then_inc(unit_done, 1)
            branches(0, True)
            with pe.Fori(1, 2) as it:
                branches(it, False)

            def w_out(u0, rhs, r0, before=None):
                for i in range(2):
                    for k in range(4):
                        if i:
                            pe.wait_ge(res, r0 + k + 1)
                        panel(u0 + 4 * i + k, k % SPL, k, rhs, before if i == 0 and k == 0 else None)
            pe.wait_ge(b_mul, 24)
            w_out(U_WO, (mix_hi, mix_lo), 0, lambda c: pe.wait_ge(b_lo, c + 1))

            pe.wait_ge(res, KC)
            norm_sum(N_F2)
            pe.wait_ge(n_std, N_F2 + 1)
            ffn(1, U_GU2, N_F2)

            pe.wait_ge(f_out, 2 * KC)
            norm_sum(N_PRE)
            pe.wait_ge(n_std, N_PRE + 1)

            def key_head(i, first):
                u = U_B2 + 8 * i
                h, r, rr, s, vr = H_B2 + 3 * i, R_B2 + 6 * i, RR_B2 + 3 * i, S_B2 + 8 * i, VR_B2 + 2 * i
                pe.wait_ge(a_o, A_B2[1] + 8 * i)
                panel(u, 0, 2, U, norm_wait(N_PRE) if first else None)
                panel(u + 1, 1, 3, U)
                head_sum(h, 6, W[0], blk64)
                panel(u + 2, 0, 4, U)
                values(vr, 0, W[2])
                panel(u + 3, 1, 5, U)
                pe.wait_ge(h_out, h + 1)
                rotate(7, W[1])
                panel(u + 4, 0, 2, U)
                values(vr + 1, 1, W[4])
                panel(u + 5, 1, 3, U)
                pe.wait_ge(r_raw, rr + 1)
                rotate(6, W[3])
                head_sum(h + 1, 4, W[5], blk64)
                panel(u + 6, 0, 5, U)
                pe.wait_ge(h_out, h + 2)
                pe.wait_ge(r_out, r + 1)
                rotate(7, W[6])
                panel(u + 7, 1, 2, U)
                pe.wait_ge(r_raw, rr + 2)
                pe.wait_ge(r_out, r + 2)
                rotate(6, W[7])
                head_sum(h + 2, 3, rtmp[:, 6, :], blk64)
                pe.wait_ge(h_out, h + 3)
                pe.wait_ge(r_out, r + 3)
                rotate(7, rtmp[:, 7, :])
                pe.wait_ge(r_raw, rr + 3)
                pe.wait_ge(r_out, r + 4)
                rotate(6, rtmp[:, 8, :])
                pe.wait_ge(s_lo, s + 8)

                def band(e, qt, lo, hi):
                    m = []
                    if lo < qt:
                        m.append((ident_r[:], masks_r[:, 2, :], 0, P))
                    if hi > qt + 1:
                        m.append((ident_r[:], masks_r[:, 1, :], (qt + 1 - lo) * P, (qt + 2 - lo) * P))
                    return m
                for k in range(4):
                    done = tuple(a + b * (4 * i + k) for a, b in zip(A_B2, (8, 2, 8)))
                    attend(done, (ast, bst)[k % 2], (whole, window)[k % 2], 2, HD,
                           ((ast if k % 2 == 0 else bst)["kh"], (ast if k % 2 == 0 else bst)["kl"]), q=q2[k],
                           extra=band if k % 2 else None)
            key_head(0, True)
            with pe.Fori(1, 2) as i:
                key_head(i, False)

            pe.wait_ge(a_o, A_B2[1] + 16)
            norm_sum(N_GRP, groups=2)
            pe.wait_ge(n_std, N_GRP + 2)
            w_out(U_WO2, U, 8, norm_wait(N_GRP))
            pe.wait_ge(res, 2 * KC)
            norm_sum(N_POST)
            pe.wait_ge(x_ready, 2 * KC)
            norm_sum(N_FPRE)
            pe.wait_ge(n_std, N_FPRE + 2)

            ffn(2, U_GU3, N_FPRE)
            pe.wait_ge(f_out, 3 * KC)
            norm_sum(N_FPOST)
            pe.wait_ge(n_std, N_FPOST + 2)
            pe.wait_ge(x_ready, 3 * KC)
            for i in range(TT):
                if i >= 2:
                    pe.wait_ge(o_ready_a, i - 1)
                    pe.wait_ge(o_ready_b, i - 1)
                for half in range(2):
                    for c in range(4):
                        last = pe.transpose(bank[2 * (i % 2) + half][:, c * P:(c + 1) * P],
                                            hT[:, 4 * half + c, i * P:(i + 1) * P], ident)
                    last.then_inc(ot_done, 1)

        @block.scalar
        def _(act):
            def copy(out_, in_, s, **kw):
                act.activation(out_, in_, ACT.Copy, **kw).then_inc(s, 1)

            def squares(ni, src, ready, n=S):
                for c in range(KC):
                    ready(c)
                    if ni * KC + c >= 2:
                        act.wait_ge(n_acc, ni * KC + c - 1)
                    act.activation(W[c % 2][:, 0:n], src[:, c, :], ACT.Square).then_inc(n_sq, 1)

            def norm_std(ni, n=S, groups=1, extra=0):
                act.wait_ge(n_acc, ni * KC + KC)
                for g in range(groups):
                    act.activation(W[2 + g][:, 0:n], bank[g][:, 0:n], ACT.Sqrt, scale=groups / D, bias=EPS).then_inc(n_std, 1)

            def norm_hi(ni, dst, n=S):
                for c in range(KC):
                    act.wait_ge(n_t, ni * KC + c + 1)
                    act.activation(dst[:, c, :], W[4 + c % 2][:, 0:n], ACT.Copy).then_inc(n_hi, 1)

            def ffn(fi, u0):
                def silu(f, k, u, first):
                    act.wait_ge(unit_done, u + 1)
                    if not first:
                        act.wait_ge(f_prod, fi * FT + f - 1)
                    act.activation(W[6 + k], bank[2 * k][:], ACT.Silu).then_inc(f_silu, 1)

                def high(f, k):
                    act.wait_ge(f_prod, fi * FT + f + 1)
                    act.activation(hid_hi[:, f, :], W[8 + k], ACT.Copy).then_inc(f_hi, 1)

                def two(it, first):
                    for k in range(2):
                        f = 2 * it + k
                        silu(f, k, u0 + 4 * it + 2 * k, first)
                        high(f, k)
                two(0, True)
                with act.Fori(1, FT // 2) as it:
                    two(it, False)

            def head_square(i, u, b, sq, rw, n=S):
                act.wait_ge(unit_done, u + 1)
                act.activation(sq[:, 0:n], bank[b][:, 0:n], ACT.Square).then_inc(h_sq, 1)
                copy(rw[:, 0:n], bank[b][:, 0:n], h_raw)

            def head_std(i, b, sq, width, n=S):
                act.wait_ge(h_sum, i + 1)
                act.activation(sq[:, 0:n], bank[b][:, 0:n], ACT.Sqrt, scale=1.0 / width, bias=EPS).then_inc(h_std, 1)

            def raw_copy(u, b, dst):
                act.wait_ge(unit_done, u + 1)
                copy(dst, bank[b][:], r_raw)

            def value_copy(u, b, dst, n=S):
                act.wait_ge(unit_done, u + 1)
                copy(dst[:, 0:n], bank[b][:, 0:n], v_raw)

            def attend(done, st, keys, heads, rows, put, sinks=None):
                t0, h0, e0 = done
                nk = max(keys(i)[1] for i in range(TT))
                nt = heads * TT

                def exps(n):
                    lo, hi = keys(n % TT)
                    w = (hi - lo) * P
                    act.wait_ge(a_max, t0 + n + 1)
                    if n >= 2 or not isinstance(t0, int) or t0 + n - 1 > 0:
                        act.wait_ge(a_t, t0 + n - 1)
                    act.activation(W[8 + n % 2][:, 0:w], bank[n % 2][:, 0:w], ACT.Exp, bias=negmax[:, n:n + 1],
                                   accum_out=rowsum[:, n:n + 1]).then_inc(a_exp, 1)
                    if sinks:
                        act.activation(sinkexp[:, n:n + 1], sinks(n // TT), ACT.Exp,
                                       bias=negmax[:, n:n + 1]).then_inc(a_sink, 1)

                def high(e):
                    act.wait_ge(a_t, t0 + TT * (e + 1))
                    if not isinstance(h0, int) or h0 + e > 0:
                        act.wait_ge(a_pv, h0 + e)
                    for kb in range(nk):
                        q0, q1 = q_blocks(keys, kb)
                        c = slice(q0 * P, q1 * P)
                        copy(st["ph"][:, kb, c], bank[2 + kb][:, c], a_ph)

                def output(e):
                    act.wait_ge(a_pv, h0 + e + 1)
                    r = slice(0, P) if rows == P else slice(e * rows, (e + 1) * rows)
                    copy(put(r), bank[6 + e][r, :], a_o)

                for n in range(nt):
                    exps(n)
                    if n >= TT and n % TT == 0:
                        high(n // TT - 1)
                    if n >= TT and n % TT == 1:
                        output(n // TT - 1)
                high(heads - 1)
                output(heads - 1)

            act.dma_start(const[:, 0:N_CONST], t["const"]).then_inc(ld_const, 16)
            act.dma_start(x_tok[:], t["x"][0].rearrange("(i p) d -> p i d", p=P)).then_inc(ld_x, 16)
            act.wait_ge(gain_zero, 1)
            for row, name in ((G_F1, "ffn1_norm"), (G_MIX, "mix_norm"), (G_MEM, "mem_norm"), (G_F2, "ffn2_norm"),
                              (G_PRE2, "norm_mix_pre_2"), (G_POST2, "norm_mix_post_2"),
                              (G_FPRE2, "norm_ffn_pre_2"), (G_FPOST2, "norm_ffn_post_2")):
                act.dma_start(gain_rows[row:row + KC, :], t[name][0].rearrange("(c p) -> c p", p=P)).then_inc(ld_gain, 16)
            for k, name in enumerate(("group_norm_a_2", "group_norm_b_2")):
                act.dma_start(gain_rows[G_GN + 4 * k:G_GN + 4 * k + 4, :],
                              t[name][0].rearrange("(c p) -> c p", p=P)).then_inc(ld_gain, 16)
            for row, name in ((G_FQ, "fox_q_norm"), (G_FK, "fox_k_norm"), (G_DQ, "dsa_q_norm"), (G_DK, "dsa_k_norm"),
                              (G_QA, "q_norm_a_2"), (G_KA, "k_norm_a_2")):
                for h in range(2):
                    act.dma_start(gain_rows[row:row + 1, h * HD:(h + 1) * HD], t[name]).then_inc(ld_gain, 16)
            act.dma_start(gain_rows[G_MQ:G_MQ + 1, :], t["mem_q_norm"]).then_inc(ld_gain, 16)
            act.dma_start(gain_rows[G_MK:G_MK + 1, :], t["mem_k_norm"]).then_inc(ld_gain, 16)
            act.dma_start(gain_rows[G_BF:G_BF + 1, 0:HEADS], t["b_forget"]).then_inc(ld_gain, 16)
            act.dma_start(pos_i[:], t["positions"].to_broadcast([P, S])).then_inc(ld_pos, 16)
            act.dma_start(sink[:], t["sink_b_2"].to_broadcast([P, HEADS])).then_inc(ld_sink, 16)

            def x_here(c):
                act.wait_ge(x_ready, c + 1)
            squares(N_F1, hT, x_here)
            norm_std(N_F1)
            norm_hi(N_F1, u_hi)
            ffn(0, U_GU1)
            act.wait_ge(trig, N_ANGLE)
            act.activation(sin1[:], W[0], ACT.Sin).then_inc(trig_a, 1)
            act.activation(cos1[:], W[1], ACT.Sin).then_inc(trig_a, 1)

            def f_here(fi):
                return lambda c: act.wait_ge(f_out, fi * KC + c + 1)
            squares(N_MIX, hT, f_here(0))
            act.dma_start(m_tok[:], t["mem"][0].rearrange("(i p) d -> p i d", p=P)).then_inc(ld_mem, 16)
            norm_std(N_MIX)
            norm_hi(N_MIX, u_hi)
            act.wait_ge(n_lo, (N_MIX + 1) * KC)
            act.wait_ge(unit_done, U_PREP + 1)
            copy(W[7][0:HD], bank[0][0:HD, :], r_raw)
            raw_copy(U_PREP + 1, 1, W[2])
            head_square(H_PREP, U_PREP + 2, 2, W[0], W[1])
            value_copy(U_PREP + 3, 3, dvT[:])
            head_std(H_PREP, 4, W[0], HD)
            act.wait_ge(iw_t, 1)
            act.activation(iw_tok[:], bank[5][:, 0:TT * HD].rearrange("p (i n) -> p i n", i=TT)[:, :, 32:32 + HEADS],
                           ACT.Copy, scale=float(HEADS ** -0.5 * HD ** -0.5)).then_inc(iw_ready, 1)
            act.wait_ge(fg, 3)
            act.activation(W[9][0:HEADS], W[9][0:HEADS], ACT.Exp).then_inc(fg_a, 1)
            act.wait_ge(fg_a, 1)
            act.activation(W[9][0:HEADS], W[9][0:HEADS], ACT.Ln, bias=1.0).then_inc(fg_a, 1)
            for c in range(KC):
                act.wait_ge(mt_done, c + 1)
                copy(mT[:, c, :], bank[c][:, 0:MEM], m_ready)
            act.wait_ge(c_ready, 2)
            for part in range(2):
                act.dma_start(c_dram[part], c_sum[32 * part:32 * part + HEADS, :].bitcast(F32)).then_inc(c_stored, 16)
            squares(N_MEM, mT, lambda c: act.wait_ge(m_ready, c + 1), MEM)
            norm_std(N_MEM, MEM)
            norm_hi(N_MEM, m_hi, MEM)
            act.wait_ge(n_lo, (N_MEM + 1) * KC)

            def mem_head(i, first):
                u, h = U_MEM + 4 * i, H_MEM + 2 * i
                head_square(h, u, 2, W[0], W[1])
                head_square(h + 1, u + 1, 3, W[2], W[3], MEM)
                head_std(h, 6, W[0], P)
                value_copy(u + 2, 4, W[4], MEM)
                head_std(h + 1, 7, W[2], P, MEM)
                raw_copy(u + 3, 5, W[5])
                act.wait_ge(h_out, h + 1)
                copy(mst["qh"][:], W[1], s_hi)
                act.wait_ge(h_out, h + 2)
                copy(mst["kh"][:], W[3][:, 0:MEM], s_hi)
                act.wait_ge(v_t, VT_MEM + i + 1)
                copy(mst["vh"][:], bank[1][:, 0:MEM].rearrange("p (k n) -> p k n", k=MT), s_hi)
                attend((A_MEM[0] + 4 * i, A_MEM[1] + i, A_MEM[2] + 2 * i), mst, memory, 1, P,
                       lambda r: oT[r, 8 + i, :])
            mem_head(0, True)
            with act.Fori(1, 4) as i:
                mem_head(i, False)

            def fox_pair(i, first):
                u, h = U_FOX + 4 * i, H_FOX + 3 * i
                if first:
                    act.wait_ge(c_one, 2)
                    act.wait_ge(c_stored, 32)
                for dst_, r in ((c_q, 0), (c_k, 2)):
                    act.dma_start(dst_[r:r + 2, :, :].bitcast(F32), c_dram[:, bass.ds(2 * i, 2), :]).then_inc(ld_c, 16)
                head_square(h, u, 2, W[0], W[1])
                head_square(h + 1, u + 1, 3, W[2], W[3])
                head_std(h, 6, W[0], HD)
                value_copy(u + 2, 4, W[6])
                head_std(h + 1, 7, W[2], HD)
                head_square(h + 2, u + 3, 5, W[4], W[5])
                act.wait_ge(h_out, h + 1)
                copy(fst["qh"][:], W[1], s_hi)
                act.wait_ge(h_out, h + 2)
                copy(fst["kh"][:], W[3], s_hi)
                act.wait_ge(v_t, VT_FOX + i + 1)
                copy(fst["vh"][:], bank[1][:].rearrange("p (k n) -> p k n", k=TT), s_hi)
                head_std(h + 2, 0, W[4], HD)
                attend((A_FOX[0] + 8 * i, A_FOX[1] + 2 * i, A_FOX[2] + 8 * i), fst, causal, 2, HD,
                       lambda r: oT[r, i, :])
            fox_pair(0, True)
            with act.Fori(1, 4) as i:
                fox_pair(i, False)

            act.wait_ge(a_pl, A_DSA[2])
            copy(ist["kh"][:], ik[:], s_hi)

            def index_pair(i, first):
                if not first:
                    act.wait_ge(ix_s, 6 * i)
                copy(ist["qh"][:], iq[:, i, :], s_hi)
                for k in range(6):
                    n = (2 + k % 3) * P
                    act.wait_ge(ix_s, 6 * i + k + 1)
                    if not first or k >= 2:
                        act.wait_ge(ix_acc, 6 * i + k - 1)
                    act.activation(W[k % 2][:, 0:n], bank[k % 2][:, 0:n], ACT.Relu).then_inc(ix_relu, 1)
            index_pair(0, True)
            with act.Fori(1, 4) as i:
                index_pair(i, False)

            act.wait_ge(ix_s, 24)
            with act.Fori(0, 6) as i:
                for k in range(4):
                    act.wait_ge(unit_done, U_GATE + 4 * i + k + 1)
                    act.activation(sig[:, 4 * i + k, :], bank[2 + k][:], ACT.Sigmoid).then_inc(g_sig, 1)

            copy(dst["kh"][:], dk[:], s_hi)
            act.wait_ge(v_t, VT_DSA + 1)
            copy(dst["vh"][:], bank[1][:].rearrange("p (k n) -> p k n", k=TT), s_hi)
            with act.Fori(0, 4) as i:
                act.wait_ge(a_s, A_DSA[0] + 8 * i)
                copy(dst["qh"][:], dq[:, i, :], s_hi)
                attend((A_DSA[0] + 8 * i, A_DSA[1] + 2 * i, A_DSA[2] + 8 * i), dst, causal, 2, HD,
                       lambda r: oT[r, 4 + i, :])

            act.wait_ge(a_o, A_B2[1])
            for n in range(3):
                copy(o_hi[:, 4 * n:4 * n + 4, :], oT[:, 4 * n:4 * n + 4, :], o_split_hi)
            act.wait_ge(o_split, 3)
            with act.Fori(0, 4) as i:
                for k in range(2):
                    m = 2 * i + k
                    act.wait_ge(b_add, 4 * i + 3 + k)
                    act.activation(mix_hi[:, m, :], W[3 * k], ACT.Copy).then_inc(b_hi, 1)

            squares(N_F2, hT, lambda c: act.wait_ge(res, c + 1))
            norm_std(N_F2)
            act.wait_ge(unit_done, U_GU2)
            norm_hi(N_F2, u_hi)
            ffn(1, U_GU2)

            squares(N_PRE, hT, f_here(1))
            act.dma_start(tab2[:], t["rope2"]).then_inc(ld_tab, 16)
            norm_std(N_PRE)
            norm_hi(N_PRE, u_hi)
            act.wait_ge(n_lo, (N_PRE + 1) * KC)

            def key_head(i, first):
                u = U_B2 + 8 * i
                h, r, s, vt = H_B2 + 3 * i, R_B2 + 6 * i, S_B2 + 8 * i, VT_B2 + 2 * i
                head_square(h, u, 2, W[0], W[1])
                value_copy(u + 1, 3, W[2])
                head_std(h, 6, W[0], HD)
                raw_copy(u + 2, 4, W[3])
                act.wait_ge(v_t, vt + 1)
                copy(ast["vh"][:], bank[0][:].rearrange("p (k n) -> p k n", k=TT), s_hi)
                value_copy(u + 3, 5, W[4])
                head_square(h + 1, u + 4, 2, W[5], W[6])
                raw_copy(u + 5, 3, W[7])
                act.wait_ge(v_t, vt + 2)
                copy(bst["vh"][:], bank[1][:].rearrange("p (k n) -> p k n", k=TT), s_hi)
                head_std(h + 1, 4, W[5], HD)
                head_square(h + 2, u + 6, 5, rtmp[:, 6, :], rtmp[:, 7, :])
                raw_copy(u + 7, 2, rtmp[:, 8, :])
                head_std(h + 2, 3, rtmp[:, 6, :], HD)
                for k in range(6):
                    act.wait_ge(r_out, r + k + 1)
                    dst_ = (ast["kh"], bst["kh"], q2[0][0], q2[1][0], q2[2][0], q2[3][0])[k]
                    copy(dst_[:], rtmp[:, k, :], s_hi, scale=(1.0 if k < 2 else HD ** -0.5) if k in (3, 5) else 1.0)
                for k in range(4):
                    done = tuple(a + b * (4 * i + k) for a, b in zip(A_B2, (8, 2, 8)))
                    attend(done, (ast, bst)[k % 2], (whole, window)[k % 2], 2, HD,
                           lambda rr, k=k: o2T[rr, (k % 2) * 4 + 2 * i + k // 2, :],
                           sinks=(lambda e, k=k: sink[:, bass.ds(4 * i + 2 * (k // 2) + e, 1)]) if k % 2 else None)
            act.wait_ge(ld_sink, 16)
            key_head(0, True)
            with act.Fori(1, 2) as i:
                key_head(i, False)

            squares(N_GRP, o2T, lambda c: act.wait_ge(a_o, A_B2[1] + 16))
            norm_std(N_GRP, groups=2)
            norm_hi(N_GRP, u_hi)
            act.wait_ge(unit_done, U_WO2 + 8)
            squares(N_POST, mo, lambda c: act.wait_ge(res, KC + c + 1))
            norm_std(N_POST)
            squares(N_FPRE, hT, lambda c: act.wait_ge(x_ready, KC + c + 1))
            norm_std(N_FPRE)
            norm_hi(N_FPRE, u_hi)
            ffn(2, U_GU3)
            squares(N_FPOST, fT, f_here(2))
            norm_std(N_FPOST)
            for i in range(TT):
                act.wait_ge(ot_done, 2 * i + 2)
                if i >= 2:
                    act.wait_ge(stored[i % 2], 16 * (i // 2))
                copy(out_tok[:, i % 2, 512:1024], bank[2 * (i % 2) + 1][:], o_ready_b)

        @block.vector
        def _(dve):
            def norm_recip(ni, std_no, n=S, groups=1, rec_no=None):
                for g in range(groups):
                    dve.wait_ge(n_std, std_no + g + 1)
                    dve.reciprocal(W[2 + g][:, 0:n], W[2 + g][:, 0:n]).then_inc(n_rec, 1)

            def norm_split(ni, std_no, src, g0, hi, lo, n=S, groups=1):
                norm_recip(ni, std_no, n, groups)
                per = KC // groups

                def low(c):
                    dve.wait_ge(n_hi, SPLITS[ni] * KC + c + 1)
                    dve.tensor_tensor(lo[:, c, :], W[4 + c % 2][:, 0:n], hi[:, c, :].bitcast(F32),
                                      ALU.subtract).then_inc(n_lo, 1)
                dve.wait_ge(n_rec, std_no + groups)
                for c in range(KC):
                    if c >= 2:
                        dve.wait_ge(n_lo, SPLITS[ni] * KC + c - 1)
                    dve.scalar_tensor_tensor(out=W[4 + c % 2][:, 0:n], in0=src[:, c, :], scalar=gain[:, g0 + c:g0 + c + 1],
                                             in1=W[2 + c // per][:, 0:n], op0=ALU.mult, op1=ALU.mult).then_inc(n_t, 1)
                    if c:
                        low(c - 1)
                low(KC - 1)

            def ffn(fi, u0, finish, between=None):
                def two(it, first):
                    for k in range(2):
                        f = 2 * it + k
                        if not first:
                            dve.wait_ge(f_lo, fi * FT + f - 1)
                        dve.wait_ge(f_silu, fi * FT + f + 1)
                        dve.wait_ge(unit_done, u0 + 4 * it + 2 * k + 2)
                        dve.tensor_tensor(W[8 + k], W[6 + k], bank[2 * k + 1][:], ALU.mult).then_inc(f_prod, 1)
                        dve.wait_ge(f_hi, fi * FT + f + 1)
                        dve.tensor_tensor(hid_lo[:, f, :], W[8 + k], hid_hi[:, f, :].bitcast(F32),
                                          ALU.subtract).then_inc(f_lo, 1)
                two(0, True)
                with dve.Fori(1, FT // 2) as it:
                    two(it, False)
                if between:
                    between()
                dve.wait_ge(unit_done, u0 + 3 * FT)
                for m in range(KC):
                    finish(m)

            def half_residual(m):
                dve.scalar_tensor_tensor(out=hT[:, m, :], in0=bank[m][:], scalar=0.5, in1=hT[:, m, :],
                                         op0=ALU.mult, op1=ALU.add).then_inc(f_out, 1)

            def head_norm(i, sq, rw, g, n=S):
                dve.wait_ge(h_std, i + 1)
                dve.reciprocal(sq[:, 0:n], sq[:, 0:n]).then_inc(h_rec, 1)
                dve.wait_ge(h_rec, i + 1)
                dve.scalar_tensor_tensor(out=rw[:, 0:n], in0=rw[:, 0:n], scalar=gain[:, g:g + 1], in1=sq[:, 0:n],
                                         op0=ALU.mult, op1=ALU.mult).then_inc(h_out, 1)

            def rope(j, src, b, cos, sin, tmp, dst_):
                dve.tensor_tensor(dst_, src, cos, ALU.mult).then_inc(r_cos, 1)
                if not isinstance(j, int) or j:
                    dve.wait_ge(r_out, j)
                dve.wait_ge(r_rot, j + 1)
                dve.tensor_tensor(tmp, bank[b][:], sin, ALU.mult).then_inc(r_sin, 1)
                dve.wait_ge(r_cos, j + 1)
                dve.wait_ge(r_sin, j + 1)
                dve.tensor_tensor(dst_, dst_, tmp, ALU.add).then_inc(r_out, 1)

            def low(i, dst_, src, hi):
                dve.wait_ge(s_hi, i + 1)
                dve.tensor_tensor(dst_, src, hi.bitcast(F32), ALU.subtract).then_inc(s_lo, 1)

            def attend(done, st, keys, heads, sinks=None, sink0=0, den0=0):
                t0, h0, e0 = done
                nk = max(keys(i)[1] for i in range(TT))
                nt = heads * TT

                def den_after_max(n):
                    return den0 + (1 if n == 0 else 2 * n)

                def den_after_probs(n):
                    return den0 + (2 * n + 3 if n < nt - 1 else 2 * nt)

                def maxes(n):
                    lo, hi = keys(n % TT)
                    row = bank[n % 2][:, 0:(hi - lo) * P]
                    dve.wait_ge(a_s, t0 + n + 1)
                    if sinks:
                        dve.tensor_reduce(rowinv[:, n:n + 1], row, AX.X, ALU.max).then_inc(a_den, 1)
                        dve.wait_ge(a_den, den_after_max(n))
                        dve.tensor_scalar(negmax[:, n:n + 1], rowinv[:, n:n + 1], sinks(n // TT), -1.0, ALU.max,
                                          ALU.mult).then_inc(a_max, 1)
                    else:
                        dve.tensor_reduce(negmax[:, n:n + 1], row, AX.X, ALU.max, negate=True).then_inc(a_max, 1)

                def probs(n):
                    lo, hi = keys(n % TT)
                    w = (hi - lo) * P
                    dve.wait_ge(a_exp, t0 + n + 1)
                    if sinks:
                        dve.wait_ge(a_sink, sink0 + n + 1)
                        dve.tensor_tensor(rowsum[:, n:n + 1], rowsum[:, n:n + 1], sinkexp[:, n:n + 1], ALU.add).then_inc(a_den, 1)
                        dve.wait_ge(a_den, den_after_probs(n))
                    dve.reciprocal(rowinv[:, n:n + 1], rowsum[:, n:n + 1]).then_inc(a_rec, 1)
                    dve.wait_ge(a_rec, t0 + n + 1)
                    p = W[8 + n % 2][:, 0:w]
                    dve.tensor_scalar(p, p, rowinv[:, n:n + 1], None, ALU.mult).then_inc(a_p, 1)

                def split(e):
                    for kb in range(nk):
                        q0, q1 = q_blocks(keys, kb)
                        c = slice(q0 * P, q1 * P)
                        dve.wait_ge(a_ph, e0 + nk * e + kb + 1)
                        dve.tensor_tensor(st["pl"][:, kb, c], bank[2 + kb][:, c], st["ph"][:, kb, c].bitcast(F32),
                                          ALU.subtract).then_inc(a_pl, 1)

                maxes(0)
                for n in range(1, nt):
                    maxes(n)
                    if n > TT and n % TT == 1:
                        split(n // TT - 1)
                    probs(n - 1)
                probs(nt - 1)
                split(heads - 1)

            def norm_add(ni, std_no, src, g0, x0):
                norm_recip(ni, std_no)
                dve.wait_ge(n_rec, std_no + 1)

                def add(c):
                    dve.wait_ge(n_t, ni * KC + c + 1)
                    dve.tensor_tensor(hT[:, c, :], hT[:, c, :], W[4 + c % 2], ALU.add).then_inc(x_ready, 1)
                for c in range(KC):
                    if c >= 2:
                        dve.wait_ge(x_ready, x0 + c - 1)
                    dve.scalar_tensor_tensor(out=W[4 + c % 2], in0=src[:, c, :], scalar=gain[:, g0 + c:g0 + c + 1],
                                             in1=W[2], op0=ALU.mult, op1=ALU.mult).then_inc(n_t, 1)
                    if c:
                        add(c - 1)
                add(KC - 1)

            dve.memset(gain_rows[:], 0.0).then_inc(gain_zero, 1)
            dve.wait_ge(ld_const, 16)
            dve.tensor_copy(ident_r[:], ident).then_inc(const_r, 1)
            dve.tensor_copy(masks_r[:], const[:, C_CAUSAL:C_CAUSAL + 3 * P].rearrange("p (m n) -> p m n", m=3)).then_inc(const_r, 1)
            dve.wait_ge(gain_t, 1)
            dve.tensor_copy(gain[:, 0:N_GAIN], bank[7][:, 0:N_GAIN]).then_inc(const_r, 1)
            dve.wait_ge(const_r, 3)
            for g, scale in ((G_FQ, HD ** -0.5), (G_DQ, HD ** -0.5), (G_QA, HD ** -0.5), (G_MQ, P ** -0.5)):
                last = dve.tensor_scalar(gain[:, g:g + 1], bank[7][:, g:g + 1], float(scale), None, ALU.mult)
            last.then_inc(gain_ready, 1)
            for c in range(KC):
                dve.wait_ge(xt_done, c + 1)
                dve.tensor_copy(hT[:, c, :], bank[c][:]).then_inc(x_ready, 1)
            dve.wait_ge(gain_ready, 1)

            norm_split(N_F1, N_F1, hT, G_F1, u_hi, u_lo)

            def angles():
                step = [0]

                def link(ins):
                    step[0] += 1
                    ins.then_inc(trig, 1)
                    dve.wait_ge(trig, step[0])
                ROUND = 12582912.0
                PI = 3.1415925
                TWO_PI = (6.28125, 0.0019350051879882812, 3.0199159819567e-07)
                a, n, m = W[2], W[3], W[4]
                dve.wait_ge(ld_pos, 16)
                link(dve.tensor_copy(a, pos_i[:]))
                link(dve.tensor_scalar(a, a, const[:, C_FREQ:C_FREQ + 1], None, ALU.mult))
                link(dve.tensor_scalar(n, a, 1.0 / 6.283185307179586, ROUND, ALU.mult, ALU.add))
                link(dve.tensor_scalar(n, n, ROUND, None, ALU.subtract))
                link(dve.tensor_scalar(m, a, 1.0 / 6.283185307179586, 0.25, ALU.mult, ALU.add))
                link(dve.tensor_scalar(m, m, ROUND, None, ALU.add))
                link(dve.tensor_scalar(m, m, ROUND, None, ALU.subtract))
                for dst_, turns, quarter in ((W[0], n, 0.0), (W[1], m, 1.5707963267948966)):
                    src = a
                    for part in TWO_PI:
                        link(dve.scalar_tensor_tensor(out=dst_, in0=turns, scalar=-part, in1=src,
                                                      op0=ALU.mult, op1=ALU.add))
                        src = dst_
                    link(dve.tensor_scalar(dst_, dst_, quarter, PI, ALU.add, ALU.min))
                    link(dve.tensor_scalar(dst_, dst_, -PI, None, ALU.max))
                assert step[0] == N_ANGLE
                dve.wait_ge(trig_a, 2)
                link(dve.tensor_scalar(sin1[:], sin1[:], const[:, C_SIGN:C_SIGN + 1], None, ALU.mult))

            ffn(0, U_GU1, half_residual, angles)

            norm_split(N_MIX, N_MIX, hT, G_MIX, u_hi, u_lo)
            dve.memset(W[6][0:HEADS], 1.0).then_inc(fg, 1)
            dve.wait_ge(r_raw, RR_PREP + 1)
            z, e = W[8][0:HEADS], W[9][0:HEADS]
            dve.tensor_scalar(z, W[7][0:HEADS], gain[0:HEADS, G_BF:G_BF + 1], None, ALU.add).then_inc(fg, 1)
            dve.wait_ge(fg, 2)
            dve.scalar_tensor_tensor(out=e, in0=z, scalar=-1.0, in1=z, op0=ALU.mult, op1=ALU.min).then_inc(fg, 1)
            head_norm(H_PREP, W[0], W[1], G_DK)
            rope(R_PREP, W[2], 6, cos1[:], sin1[:], W[4], ik[:])
            dve.wait_ge(h_out, H_PREP + 1)
            rope(R_PREP + 1, W[1], 7, cos1[:], sin1[:], W[5], dk[:])
            dve.wait_ge(fg_a, 2)
            dve.scalar_tensor_tensor(out=z, in0=z, scalar=0.0, in1=e, op0=ALU.min, op1=ALU.subtract).then_inc(fg, 1)
            dve.wait_ge(fg, 4)
            dve.tensor_tensor_scan(e, W[6][0:HEADS], z, 0.0, ALU.mult, ALU.add).then_inc(fg, 1)
            dve.wait_ge(fg, 5)
            dve.tensor_copy(c_sum[0:HEADS, :], e).then_inc(c_ready, 1)
            dve.wait_ge(c_ready, 1)
            dve.tensor_tensor(c_sum[32:32 + HEADS, :], e, c_sum[0:HEADS, :].bitcast(F32), ALU.subtract).then_inc(c_ready, 1)
            norm_split(N_MEM, N_MEM, mT, G_MEM, m_hi, m_lo, MEM)

            def mem_head(i):
                h, s = H_MEM + 2 * i, S_MEM + 3 * i
                head_norm(h, W[0], W[1], G_MQ)
                head_norm(h + 1, W[2], W[3], G_MK, MEM)
                low(s, mst["ql"][:], W[1], mst["qh"][:])
                low(s + 1, mst["kl"][:], W[3][:, 0:MEM], mst["kh"][:])
                low(s + 2, mst["vl"][:], bank[1][:, 0:MEM].rearrange("p (k n) -> p k n", k=MT), mst["vh"][:])
                rope(R_MEM + i, W[5], 6, cos1[:], sin1[:], W[6], iq[:, i, :])
                attend((A_MEM[0] + 4 * i, A_MEM[1] + i, A_MEM[2] + 2 * i), mst, memory, 1)
            with dve.Fori(0, 4) as i:
                mem_head(i)

            dve.memset(c_q[:].bitcast(F32), -1.0).then_inc(c_one, 1)
            dve.memset(c_k[:].bitcast(F32), 1.0).then_inc(c_one, 1)

            def fox_pair(i):
                h, s = H_FOX + 3 * i, S_FOX + 3 * i
                head_norm(h, W[0], W[1], G_FQ)
                head_norm(h + 1, W[2], W[3], G_FK)
                low(s, fst["ql"][:], W[1], fst["qh"][:])
                low(s + 1, fst["kl"][:], W[3], fst["kh"][:])
                low(s + 2, fst["vl"][:], bank[1][:].rearrange("p (k n) -> p k n", k=TT), fst["vh"][:])
                head_norm(h + 2, W[4], W[5], G_DQ)
                dve.wait_ge(h_out, h + 3)
                rope(R_FOX + i, W[5], 6, cos1[:], sin1[:], W[7], dq[:, i, :])
                attend((A_FOX[0] + 8 * i, A_FOX[1] + 2 * i, A_FOX[2] + 8 * i), fst, causal, 2)
            with dve.Fori(0, 4) as i:
                fox_pair(i)

            low(S_IDX, ist["kl"][:], ik[:], ist["kh"][:])

            def index_pair(i, first):
                low(S_IDX + 1 + i, ist["ql"][:], iq[:, i, :], ist["qh"][:])
                for k in range(6):
                    e, qt = k // 3, 1 + k % 3
                    n = (qt + 1) * P
                    sc, weight = score[:, qt, 0:n], iw_tok[:, qt, bass.ds(2 * i + e, 1)]
                    dve.wait_ge(ix_relu, 6 * i + k + 1)
                    if first and e == 0:
                        dve.tensor_scalar(sc, W[k % 2][:, 0:n], weight, None, ALU.mult).then_inc(ix_acc, 1)
                    else:
                        dve.wait_ge(ix_acc, 6 * i + k - 2)
                        dve.scalar_tensor_tensor(out=sc, in0=W[k % 2][:, 0:n], scalar=weight, in1=sc,
                                                 op0=ALU.mult, op1=ALU.add).then_inc(ix_acc, 1)
            index_pair(0, True)
            with dve.Fori(1, 4) as i:
                index_pair(i, False)
            dve.wait_ge(ix_acc, 24)
            for qt in range(1, TT):
                d = score[:, qt, qt * P:(qt + 1) * P]
                dve.tensor_tensor(d, d, const[:, C_CAUSAL:C_CAUSAL + P], ALU.add).then_inc(tk_rep, 1)
            dve.wait_ge(tk_rep, TT - 1)
            found = dve.alloc_register("found")
            with dve.Fori(0, TOP_ROUNDS) as r:
                for qt in range(1, TT):
                    dve.max(best8[:, qt, :], score[:, qt, 0:(qt + 1) * P]).then_inc(tk_max, 1)
                for qt in range(1, TT):
                    sc = score[:, qt, 0:(qt + 1) * P]
                    dve.reg_mov(found, (TT - 1) * r + qt)
                    dve.wait_ge(ix_acc, 24)
                    dve.wait_ge(tk_max, found)
                    dve.match_replace(sc, best8[:, qt, :], sc, TAKEN).then_inc(tk_rep, 1)
                dve.wait_ge(tk_rep, (TT - 1) * r + 2 * (TT - 1))
            for qt in range(1, TT):
                dve.tensor_scalar(topmask[:, qt, 0:(qt + 1) * P], score[:, qt, 0:(qt + 1) * P], TAKEN / 2, NEG,
                                  ALU.is_gt, ALU.mult).then_inc(tk_mask, 1)

            low(S_DSA, dst["kl"][:], dk[:], dst["kh"][:])
            low(S_DSA + 1, dst["vl"][:], bank[1][:].rearrange("p (k n) -> p k n", k=TT), dst["vh"][:])
            with dve.Fori(0, 4) as i:
                low(S_DSA + 2 + i, dst["ql"][:], dq[:, i, :], dst["qh"][:])
                attend((A_DSA[0] + 8 * i, A_DSA[1] + 2 * i, A_DSA[2] + 8 * i), dst, causal, 2)

            for n in range(3):
                c = slice(4 * n, 4 * n + 4)
                dve.wait_ge(o_split_hi, n + 1)
                dve.tensor_tensor(o_lo[:, c, :], oT[:, c, :], o_hi[:, c, :].bitcast(F32), ALU.subtract).then_inc(o_split, 1)

            def mixed(mp, first):
                if not first:
                    dve.wait_ge(b_lo, 2 * mp)
                for n in range(3):
                    dve.wait_ge(unit_done, U_BR + 3 * mp + n + 1)
                    for half in range(2):
                        dve.tensor_tensor(W[3 * half + n], bank[2 * n + half][:], sig[:, KC * n + 2 * mp + half, :],
                                          ALU.mult).then_inc(b_mul, 1)
                for half in range(2):
                    dve.wait_ge(b_mul, 6 * mp + 5 + half)
                    dve.tensor_tensor(W[3 * half], W[3 * half], W[3 * half + 1], ALU.add).then_inc(b_add, 1)
                for half in range(2):
                    dve.wait_ge(b_add, 4 * mp + 1 + half)
                    dve.tensor_tensor(W[3 * half], W[3 * half], W[3 * half + 2], ALU.add).then_inc(b_add, 1)
                for half in range(2):
                    dve.wait_ge(b_hi, 2 * mp + half + 1)
                    dve.tensor_tensor(mix_lo[:, 2 * mp + half, :], W[3 * half], mix_hi[:, 2 * mp + half, :].bitcast(F32),
                                      ALU.subtract).then_inc(b_lo, 1)
            mixed(0, True)
            with dve.Fori(1, 4) as mp:
                mixed(mp, False)
            for m in range(KC):
                dve.wait_ge(unit_done, U_WO + m + 1)
                dve.tensor_tensor(hT[:, m, :], bank[m % 4][:], hT[:, m, :], ALU.add).then_inc(res, 1)

            norm_split(N_F2, N_F2, hT, G_F2, u_hi, u_lo)
            ffn(1, U_GU2, half_residual)

            norm_split(N_PRE, N_PRE, hT, G_PRE2, u_hi, u_lo)
            dve.wait_ge(ld_tab, 16)
            dve.wait_ge(ld_sink, 16)

            def key_head(i):
                h, r, s = H_B2 + 3 * i, R_B2 + 6 * i, S_B2 + 8 * i
                tmp = rtmp[:, 9, :]

                def turn(k, src, b):
                    rope(r + k, src, b, tab2[:, 2 * (k % 2), :], tab2[:, 2 * (k % 2) + 1, :], tmp, rtmp[:, k, :])
                head_norm(h, W[0], W[1], G_KA)
                dve.wait_ge(h_out, h + 1)
                turn(0, W[1], 7)
                low(s, ast["vl"][:], bank[0][:].rearrange("p (k n) -> p k n", k=TT), ast["vh"][:])
                dve.wait_ge(r_raw, RR_B2 + 3 * i + 1)
                turn(1, W[3], 6)
                low(s + 1, bst["vl"][:], bank[1][:].rearrange("p (k n) -> p k n", k=TT), bst["vh"][:])
                head_norm(h + 1, W[5], W[6], G_QA)
                dve.wait_ge(h_out, h + 2)
                turn(2, W[6], 7)
                dve.wait_ge(r_raw, RR_B2 + 3 * i + 2)
                turn(3, W[7], 6)
                head_norm(h + 2, rtmp[:, 6, :], rtmp[:, 7, :], G_QA)
                dve.wait_ge(h_out, h + 3)
                turn(4, rtmp[:, 7, :], 7)
                dve.wait_ge(r_raw, RR_B2 + 3 * i + 3)
                turn(5, rtmp[:, 8, :], 6)
                for k in range(6):
                    hi, lo = ((ast["kh"], ast["kl"]), (bst["kh"], bst["kl"]), *q2)[k]
                    dve.wait_ge(s_hi, s + 3 + k)
                    if k in (3, 5):
                        dve.scalar_tensor_tensor(out=lo[:], in0=rtmp[:, k, :], scalar=float(HD ** -0.5),
                                                 in1=hi[:].bitcast(F32), op0=ALU.mult, op1=ALU.subtract).then_inc(s_lo, 1)
                    else:
                        dve.tensor_tensor(lo[:], rtmp[:, k, :], hi[:].bitcast(F32), ALU.subtract).then_inc(s_lo, 1)
                for k in range(4):
                    done = tuple(a + b * (4 * i + k) for a, b in zip(A_B2, (8, 2, 8)))
                    w = 2 * i + k // 2
                    attend(done, (ast, bst)[k % 2], (whole, window)[k % 2], 2,
                           sinks=(lambda e, k=k: sink[:, bass.ds(4 * i + 2 * (k // 2) + e, 1)]) if k % 2 else None,
                           sink0=8 * w, den0=16 * w)
            with dve.Fori(0, 2) as i:
                key_head(i)

            norm_split(N_GRP, N_GRP, o2T, G_GN, u_hi, u_lo, groups=2)
            for m in range(KC):
                dve.wait_ge(unit_done, U_WO2 + m + 1)
                dve.tensor_copy(mo[:, m, :], bank[m % 4][:]).then_inc(res, 1)
            norm_add(N_POST, N_POST + 1, mo, G_POST2, KC)

            norm_split(N_FPRE, N_FPRE + 1, hT, G_FPRE2, u_hi, u_lo)

            def to_fT(m):
                dve.tensor_copy(fT[:, m, :], bank[m][:]).then_inc(f_out, 1)
            ffn(2, U_GU3, to_fT)
            norm_add(N_FPOST, N_FPOST + 1, fT, G_FPOST2, 2 * KC)
            for i in range(TT):
                dve.wait_ge(ot_done, 2 * i + 1)
                if i >= 2:
                    dve.wait_ge(stored[i % 2], 16 * (i // 2))
                dve.tensor_copy(out_tok[:, i % 2, 0:512], bank[2 * (i % 2)][:]).then_inc(o_ready_a, 1)


def constants():
    import numpy as np

    c = np.zeros((P, N_CONST), np.float32)
    i = np.arange(P)
    c[:, C_ID:C_ID + P] = np.eye(P)
    c[:, C_ONE:C_ONE + P] = 1.0
    c[:, C_BLK:C_BLK + P] = i[:, None] // HD == i[None, :] // HD
    c[i, C_ROT + (i ^ 32)] = 1.0
    c[:, C_CAUSAL:C_CAUSAL + P] = np.where(i[None, :] > i[:, None], NEG, 0.0)
    c[:, C_UP:C_UP + P] = np.where(i[None, :] > i[:, None], NEG, 0.0)
    c[:, C_LOW:C_LOW + P] = np.where(i[None, :] < i[:, None], NEG, 0.0)
    pairs = np.arange(0, HD, 2, dtype=np.float32) / np.float32(HD)
    freq = np.power(np.float32(10000.0), -pairs).astype(np.float32)
    c[:, C_FREQ] = freq[i % 32]
    sign = np.where(i % HD < 32, -1.0, 1.0).astype(np.float32)
    c[:, C_SIGN] = sign
    t = np.arange(S)
    f16 = np.power(np.float32(10000.0), -(np.arange(16, dtype=np.float32) / np.float32(16))).astype(np.float32)
    axial = np.concatenate([(t // 64).astype(np.float32)[:, None] * f16, (t % 64).astype(np.float32)[:, None] * f16], 1)
    f32 = np.power(np.float32(10000.0), -(np.arange(32, dtype=np.float32) / np.float32(32))).astype(np.float32)
    token = t.astype(np.float32)[:, None] * f32
    rope2 = np.empty((P, 4, S), np.float32)
    for k, a in enumerate((axial, token)):
        rope2[:, 2 * k] = np.cos(a).T[i % 32]
        rope2[:, 2 * k + 1] = np.sin(a).T[i % 32] * sign[:, None]
    return {"const": c, "rope2": rope2}


_INS = [
    "x", "mem", "positions", "ffn1_norm", "ffn1_w_gate", "ffn1_w_up", "ffn1_w_down", "mix_norm", "mem_norm", "w_in",
    "b_forget", "fox_q_norm", "fox_k_norm", "dsa_q_norm", "dsa_k_norm", "mem_q_norm", "mem_k_norm", "w_mem_kv",
    "w_branch", "w_out", "ffn2_norm", "ffn2_w_gate", "ffn2_w_up", "ffn2_w_down", "norm_mix_pre_2", "w_in_2",
    "q_norm_a_2", "k_norm_a_2", "sink_b_2", "group_norm_a_2", "group_norm_b_2", "w_out_2", "norm_mix_post_2",
    "norm_ffn_pre_2", "w_gate_2", "w_up_2", "w_down_2", "norm_ffn_post_2",
]


def kernel(**inputs):
    import numpy as np
    import concourse.bacc as bacc
    from concourse.bass_utils import run_bass_kernel_spmd

    nc = bacc.Bacc("TRN2", target_bir_lowering=False, num_devices=1)
    arrays, args = {}, {}
    given = {name: np.ascontiguousarray(inputs[name]) for name in _INS}
    for name, a in {**given, **constants()}.items():
        arrays[f"in_{name}"] = a
        args[name] = nc.dram_tensor(f"in_{name}", a.shape, mybir.dt.from_np(a.dtype), kind="ExternalInput").ap()
    out = nc.dram_tensor("out_0", (1, S, D), F32, kind="ExternalOutput").ap()
    two_blocks(nc, args, out)
    r = run_bass_kernel_spmd(nc, [arrays], core_ids=[0])
    return r.results[0]["out_0"]
```

```python
from contextlib import ExitStack

import concourse.bass as bass
from concourse import mybir

ALU = mybir.AluOpType
ACT = mybir.ActivationFunctionType
AX = mybir.AxisListType
F32 = mybir.dt.float32
F32R = mybir.dt.float32r
I32 = mybir.dt.int32

P = 128
D = 1024
S = 512
MEM = 256
FF = 2816
HD = 64
KC = D // P
FT = FF // P
TT = S // P
MT = MEM // P
TOPK = 128
TOP_ROUNDS = TOPK // 8
N_ANGLE = 17
EPS = 1e-6
NEG = -1e30
TAKEN = -3e38
BW = 512
HEADS = 8

SIZES = (BW, BW, BW, HEADS, BW, HD, HD, BW, HD, HEADS, BW, 3 * D)
OFF = [sum(SIZES[:i]) for i in range(len(SIZES))]
FQ, FK, FV, FG, DQ, DK, DV, IQ, IK, IW, MQ, GT = OFF
D_IN = sum(SIZES)
QA, KA, VA, QB, KB, VB = 0, 512, 640, 768, 1280, 1408
D_IN2 = 1536

(G_F1, G_MIX, G_MEM, G_F2, G_PRE2, G_GN, G_POST2, G_FPRE2, G_FPOST2) = range(0, 72, 8)
G_FQ, G_FK, G_DQ, G_DK, G_MQ, G_MK, G_QA, G_KA, G_BF = range(72, 81)
N_GAIN = 82

C_ID, C_ONE, C_BLK, C_ROT, C_CAUSAL, C_UP, C_LOW, C_FREQ, C_SIGN = (
    0, 128, 256, 384, 512, 640, 768, 896, 897)
N_CONST = 898

U_GU1 = 0
U_DN1 = U_GU1 + 2 * FT
U_PREP = U_DN1 + FT
U_MEM = U_PREP + 4
U_FOX = U_MEM + 16
U_GATE = U_FOX + 16
U_BR = U_GATE + 24
U_WO = U_BR + 12
U_GU2 = U_WO + 8
U_DN2 = U_GU2 + 2 * FT
U_B2 = U_DN2 + FT
U_WO2 = U_B2 + 16
U_GU3 = U_WO2 + 8
U_DN3 = U_GU3 + 2 * FT
N_UNITS = U_DN3 + FT
RAW = 4
SPL = 2


def two_blocks(nc, t, out):
    ctx = ExitStack()
    with ctx:
        def sem(name):
            return ctx.enter_context(nc.semaphore(name))

        top = [(nc.sbuf_base + 63) // 64 * 64]

        def at(name, shape, addr, dt=F32):
            return nc.alloc_sbuf_tensor_at(name, shape, dt, offset=addr)

        def size(shape):
            n = 4
            for s in shape[1:]:
                n *= s
            return n

        def place(name, shape, dt=F32):
            a = top[0]
            top[0] += (size(shape) + 31) // 32 * 32
            return at(name, shape, a, dt)

        raw = place("raw", [P, RAW, D])
        w_hi = place("w_hi", [P, SPL, D], F32R)
        w_lo = place("w_lo", [P, SPL, D], F32R)
        hT = place("hT", [P, KC, S])
        const = place("const", [P, N_CONST + 2])
        ident_r = place("ident_r", [P, P], F32R)
        masks_r = place("masks_r", [P, 3, P], F32R)
        gain = place("gain", [P, N_GAIN + 2])
        cos1 = place("cos1", [P, S])
        sin1 = place("sin1", [P, S])
        iw_tok = place("iw_tok", [P, TT, HEADS])
        ones_r = place("ones_r", [P, P], F32R)
        zero_r = place("zero_r", [P, P], F32R)
        rowmax = place("rowmax", [P, 2, TT])
        negmax = place("negmax", [P, 2, TT])
        sink = place("sink", [P, HEADS])
        sink_now = place("sink_now", [P, 8])
        best8 = place("best8", [P, TT, 8])
        work_at = top[0]
        work = place("work", [P, 10, S])
        W = [work[:, i, :] for i in range(10)]
        shift = at("shift", [P, 2, S], work_at + 5 * 2048, F32R)
        q_second = (at("q_second_h", [P, S], work_at + 2048, F32R), at("q_second_l", [P, S], work_at + 2 * 2048, F32R))
        den, sink_e, inverse, prob = W[3], W[2], W[4], W[7:10]
        ident = const[:, C_ID:C_ID + P]
        ones = const[:, C_ONE:C_ONE + P]
        blk64 = const[:, C_BLK:C_BLK + P]
        rot = const[:, C_ROT:C_ROT + P]

        base = top[0]
        u_at = base
        u_hi = at("u_hi", [P, KC, S], u_at, F32R)
        u_lo = at("u_lo", [P, KC, S], u_at + 16384, F32R)
        o_at = u_at + 32768
        x_at = o_at + 24576
        s_at = x_at + 24576
        assert s_at + 49152 <= nc.sbuf_usable_end, (s_at + 49152, nc.sbuf_usable_end)
        a_at = o_at
        x_tok = at("x_tok", [P, TT, D], a_at)
        gain_rows = at("gain_rows", [N_GAIN, P], a_at + 16384)
        pos_i = at("pos_i", [P, S], a_at + FT * 4096, I32)
        hid_hi = at("hid_hi", [P, FT, S], a_at, F32R)
        hid_lo = at("hid_lo", [P, FT, S], a_at + FT * 2048, F32R)

        oT = at("oT", [P, 12, S], o_at)
        score = at("score", [P, TT, S], o_at + 4 * 2048)
        iq = at("iq", [P, 4, S], x_at)
        topmask = at("topmask", [P, TT, S], x_at, F32R)
        dq = at("dq", [P, 4, S], x_at + 8192)
        ik = at("ik", [P, S], x_at + 16384)
        dk = at("dk", [P, S], x_at + 18432)
        dvT = at("dvT", [P, S], x_at + 20480)
        c_sum = at("c_sum", [32 + HEADS, S], x_at + 22528, F32R)
        m_tok = at("m_tok", [P, MT, D], s_at)
        mT = at("mT", [P, KC, MEM], s_at + 8192)
        m_hi = at("m_hi", [P, KC, MEM], s_at + 16384, F32R)
        m_lo = at("m_lo", [P, KC, MEM], s_at + 24576, F32R)

        def staging(tag, a, nk, ncol, queries=True):
            kw = nk * P
            names = (("qh", [P, S]), ("ql", [P, S])) if queries else ()
            names += (("kh", [P, kw]), ("kl", [P, kw]),
                      ("vh", [P, nk, ncol]), ("vl", [P, nk, ncol]),
                      ("ph", [P, nk, S]), ("pl", [P, nk, S]))
            d = {}
            for n, shape in names:
                d[n] = at(tag + n, shape, a, F32R)
                a += size(shape)
            return d, a

        mst, e_at = staging("m_", s_at + 32768, MT, P)
        assert e_at <= s_at + 49152
        fst, e_at = staging("f_", s_at, TT, 3 * HD)
        c_q = at("c_q", [4, 2, S], e_at, F32R)
        c_k = at("c_k", [4, 2, S], e_at + 4096, F32R)
        assert e_at + 8192 <= s_at + 49152
        ist = {n: at("i_" + n, [P, S], s_at + 2048 * i, F32R) for i, n in enumerate(("qh", "ql", "kh", "kl"))}
        sig = at("sig", [P, 24, S], s_at)
        dst, e_at = staging("d_", u_at, TT, 3 * HD)
        assert e_at <= o_at
        o_hi = at("o_hi", [P, 12, S], u_at, F32R)
        o_lo = at("o_lo", [P, 12, S], x_at, F32R)
        mix_lo = at("mix_lo", [P, KC, S], u_at + 24576, F32R)
        mix_hi = at("mix_hi", [P, KC, S], u_at + 24576 + 16384, F32R)
        o2T = at("o2T", [P, KC, S], a_at)
        tab2 = at("tab2", [P, 4, S], a_at + 16384)
        b2a = a_at + 24576
        ast, b2a = staging("a_", b2a, TT, 3 * HD, queries=False)
        bst = {}
        for n, shape in (("kh", [P, S]), ("kl", [P, S]), ("vh", [P, TT, 3 * HD]), ("vl", [P, TT, 3 * HD])):
            bst[n] = at("b_" + n, shape, b2a, F32R)
            b2a += size(shape)
        bst["ph"], bst["pl"] = ast["ph"], ast["pl"]
        q2 = []
        for i in range(4):
            q2.append((at(f"q2h{i}", [P, S], b2a, F32R), at(f"q2l{i}", [P, S], b2a + 2048, F32R)))
            b2a += 4096
        rtmp = at("rtmp", [P, 9, S], b2a)
        assert b2a + 9 * 2048 <= nc.sbuf_usable_end
        fT = at("fT", [P, KC, S], u_at)
        mo = at("mo", [P, KC, S], a_at + 16384)
        out_tok = at("out_tok", [P, 2, D], a_at)

        c_dram = nc.dram_tensor("forget_sums", (2, HEADS, S), F32, kind="Internal").ap()
        bank = [ctx.enter_context(nc.psum_tensor(f"bank{i}", [P, S], F32)) for i in range(8)]

        raw_loaded = [sem(f"raw_loaded{i}") for i in range(RAW)]
        c_stored = sem("c_stored")
        part_loaded = sem("part_loaded")
        hi_done = sem("hi_done")
        split_ready = sem("split_ready")
        unit_done = sem("unit_done")
        ld_const, ld_gain, ld_x, ld_pos, ld_mem, ld_tab, ld_sink, ld_c = (
            sem(n) for n in ("ld_const", "ld_gain", "ld_x", "ld_pos", "ld_mem", "ld_tab", "ld_sink",
                             "ld_c"))
        stored = [sem("stored0"), sem("stored1")]
        gain_zero, gain_t, gain_ready, const_r, xt_done, x_ready, trig, trig_a = (
            sem(n) for n in ("gain_zero", "gain_t", "gain_ready", "const_r", "xt_done", "x_ready", "trig",
                             "trig_a"))
        n_sq, n_acc, n_std, n_rec, n_t, n_hi, n_lo = (
            sem("n_" + n) for n in ("sq", "acc", "std", "rec", "t", "hi", "lo"))
        f_silu, f_prod, f_hi, f_lo, f_out = (sem("f_" + n) for n in ("silu", "prod", "hi", "lo", "out"))
        h_sq, h_raw, h_sum, h_std, h_rec, h_out = (
            sem("h_" + n) for n in ("sq", "raw", "sum", "std", "rec", "out"))
        r_raw, r_rot, r_cos, r_sin, r_out = (sem("r_" + n) for n in ("raw", "rot", "cos", "sin", "out"))
        s_hi, s_lo = sem("s_hi"), sem("s_lo")
        v_raw, v_t = sem("v_raw"), sem("v_t")
        a_s, a_max, a_neg, a_shift, a_t, a_e, a_pl, a_pv, a_o, a_den, a_rec, a_out, a_sink = (
            sem("a_" + n) for n in ("s", "max", "neg", "shift", "t", "e", "pl", "pv", "o", "den", "rec", "out", "sink"))
        iw_t, iw_ready, fg, fg_a, c_ready, c_one = (
            sem(n) for n in ("iw_t", "iw_ready", "fg", "fg_a", "c_ready", "c_one"))
        ix_s, ix_relu, ix_acc, tk_max, tk_rep, tk_mask = (
            sem(n) for n in ("ix_s", "ix_relu", "ix_acc", "tk_max", "tk_rep", "tk_mask"))
        g_sig, o_split_hi, o_split, b_mul, b_add, b_hi, b_lo, res = (
            sem(n) for n in ("g_sig", "o_split_hi", "o_split", "b_mul", "b_add", "b_hi", "b_lo", "res"))
        mt_done, m_ready, ot_done, o_ready_a, o_ready_b = (
            sem(n) for n in ("mt_done", "m_ready", "ot_done", "o_ready_a", "o_ready_b"))

        block = ctx.enter_context(nc.Block())

        def cols(w, a, n=P):
            return w.rearrange("(c p) n -> p c n", p=P)[:, :, bass.ds(a, n)]

        def raw_as(slot, c):
            return raw[:, slot, :].rearrange("p (c n) -> p c n", c=c)

        @block.sync
        def _(sp):
            wait_value = sp.alloc_register("wait_value")

            def value(v):
                if isinstance(v, int):
                    return v
                sp.reg_mov(wait_value, v)
                return wait_value

            def unit(u, slot, dst, src):
                if not (isinstance(u, int) and u < RAW):
                    free = value(u - RAW + 1)
                    sp.wait_ge(split_ready, 1)
                    sp.wait_ge(split_ready, free)
                sp.dma_start(dst, src).then_inc(raw_loaded[slot], 16)

            def panel(u, slot, w, a):
                unit(u, slot, raw_as(slot, KC), cols(w, a))

            def halves(u, slot, w, one, two, n):
                dst = raw_as(slot, KC)
                free = value(u - RAW + 1)
                sp.wait_ge(split_ready, 1)
                sp.wait_ge(split_ready, free)
                sp.dma_start(dst[:, :, one[0]:one[0] + n], cols(w, one[1], n)).then_inc(part_loaded, 16)
                first = value(16 * (part_count(u) + 1))
                sp.wait_ge(split_ready, 1)
                sp.wait_ge(part_loaded, first)
                sp.dma_start(dst[:, :, two[0]:two[0] + n], cols(w, two[1], n)).then_inc(raw_loaded[slot], 16)

            def twice(u, slot, w, a):
                halves(u, slot, w, (0, a), (HD, a), HD)

            def ffn(u0, gate, up, down):
                def four(i):
                    for k in range(4):
                        panel(u0 + 4 * i + k, (u0 + k) % RAW, (gate, up)[k % 2], (2 * i + k // 2) * P)
                start = 0
                if u0 == 0:
                    four(0)
                    start = 1
                with sp.Fori(start, FT // 2) as i:
                    four(i)
                d0 = u0 + 2 * FT

                def rows(j, k):
                    slot = (d0 + k) % RAW
                    unit(d0 + j, slot, raw[:, slot, :], down[bass.ds(j * P, P), :])
                with sp.Fori(0, FT // 4) as i:
                    for k in range(4):
                        rows(4 * i + k, k)
                for k in range(FT % 4):
                    rows(FT // 4 * 4 + k, k)

            def part_count(u):
                if isinstance(u, int):
                    return u - U_PREP
                return parts_before[0]

            parts_before = [0]
            ffn(U_GU1, t["ffn1_w_gate"][0], t["ffn1_w_up"][0], t["ffn1_w_down"][0])
            w_in = t["w_in"][0]
            slot = U_PREP % RAW
            halves(U_PREP, slot, w_in, (0, FG), (32, IW), HEADS)
            for k, a in enumerate((IK, DK, DV)):
                twice(U_PREP + 1 + k, (U_PREP + 1 + k) % RAW, w_in, a)
            kv = t["w_mem_kv"][0]
            with sp.Fori(0, 4) as i:
                for k, (w, a) in enumerate(((w_in, MQ), (kv, 0), (kv, BW), (w_in, IQ))):
                    panel(U_MEM + 4 * i + k, (U_MEM + k) % RAW, w, a + i * P)
            with sp.Fori(0, 4) as i:
                for k, a in enumerate((FQ, FK, FV, DQ)):
                    panel(U_FOX + 4 * i + k, (U_FOX + k) % RAW, w_in, a + i * P)
            with sp.Fori(0, 6) as i:
                for k in range(4):
                    panel(U_GATE + 4 * i + k, (U_GATE + k) % RAW, w_in, GT + (4 * i + k) * P)
            for mp in range(4):
                for n in range(3):
                    k = 3 * mp + n
                    slot = (U_BR + k) % RAW
                    unit(U_BR + k, slot, raw_as(slot, 4), cols(t["w_branch"][0, n], mp * 2 * P, 2 * P))

            def w_out(u0, w):
                with sp.Fori(0, 2) as i:
                    for k in range(4):
                        panel(u0 + 4 * i + k, (u0 + k) % RAW, w, (4 * i + k) * P)
            w_out(U_WO, t["w_out"][0])
            ffn(U_GU2, t["ffn2_w_gate"][0], t["ffn2_w_up"][0], t["ffn2_w_down"][0])
            w2 = t["w_in_2"][0]
            with sp.Fori(0, 2) as i:
                u = U_B2 + 8 * i
                for k, (a, key, nth) in enumerate(((KA, True, 0), (QA, False, 0), (QA + P, False, 0), (KB, True, 1),
                                                   (QB, False, 0), (QB + P, False, 0), (VA, True, 2), (VB, True, 3))):
                    slot = (U_B2 + k) % RAW
                    if key:
                        parts_before[0] = 4 + 4 * i + nth
                        twice(u + k, slot, w2, a + i * HD)
                    else:
                        panel(u + k, slot, w2, a + i * 2 * P)
            w_out(U_WO2, t["w_out_2"][0])
            ffn(U_GU3, t["w_gate_2"][0], t["w_up_2"][0], t["w_down_2"][0])
            for i in range(TT):
                sp.wait_ge(o_ready_a, i + 1)
                sp.wait_ge(o_ready_b, i + 1)
                sp.dma_start(out[0, i * P:(i + 1) * P, :], out_tok[:, i % 2, :]).then_inc(stored[i % 2], 16)
            for s in stored:
                sp.wait_ge(s, 16 * TT // 2)

        @block.gpsimd
        def _(pool):
            loaded_value, used_value = pool.alloc_register("loaded_value"), pool.alloc_register("used_value")

            def value(reg, v):
                if isinstance(v, int):
                    return v
                pool.reg_mov(reg, v)
                return reg

            def split(u, i, k):
                first = isinstance(u, int) and u < SPL
                loaded = value(loaded_value, 16 * (i + 1))
                used = value(used_value, u - SPL + 1)
                pool.wait_ge(raw_loaded[k], 16)
                pool.wait_ge(raw_loaded[k], loaded)
                if not first:
                    pool.wait_ge(unit_done, used)
                s = k % SPL
                pool.tensor_scalar(w_hi[:, s, :], raw[:, k, :], 1.0, 1.0, ALU.mult, ALU.mult).then_inc(hi_done, 1)
                pool.wait_ge(hi_done, u + 1)
                pool.tensor_tensor(w_lo[:, s, :], raw[:, k, :], w_hi[:, s, :].bitcast(F32),
                                   ALU.subtract).then_inc(split_ready, 1)
            for k in range(RAW):
                split(k, 0, k)
            with pool.Fori(1, N_UNITS // RAW) as i:
                for k in range(RAW):
                    split(4 * i + k, i, k)
            for k in range(N_UNITS % RAW):
                split(N_UNITS // RAW * RAW + k, N_UNITS // RAW, k)

        N_F1, N_MIX, N_MEM, N_F2, N_PRE, N_GRP, N_POST, N_FPRE, N_FPOST = range(9)
        SPLITS = {N_F1: 0, N_MIX: 1, N_MEM: 2, N_F2: 3, N_PRE: 4, N_GRP: 5, N_FPRE: 6}
        H_PREP, H_MEM, H_FOX, H_DQ, H_B2 = 0, 1, 9, 17, 21
        R_PREP, R_IQ, R_DQ, R_B2 = 0, 2, 6, 10
        RR_PREP, RR_MEM, RR_FOX, RR_B2 = 0, 2, 6, 10
        S_MEM, S_FOX, S_IDX, S_DSA, S_B2 = 0, 12, 24, 29, 35
        VR_PREP, VR_MEM, VR_FOX, VR_B2 = 0, 1, 5, 9
        VT_MEM, VT_FOX, VT_DSA, VT_B2 = 0, 4, 8, 9
        A_MEM, A_FOX, A_DSA, A_B2 = (0, 0, 0, 0, 0), (16, 8, 8, 4, 4), (48, 40, 40, 12, 8), (80, 72, 72, 20, 12)

        def done_before(base, per, i):
            return tuple(a + b * i for a, b in zip(base, per))

        def causal(qt):
            return 0, qt + 1

        def window(qt):
            return max(0, qt - 1), min(TT, qt + 2)

        def whole(qt):
            return 0, TT

        def memory(qt):
            return 0, MT

        def q_blocks(keys, kb):
            q = [i for i in range(TT) if keys(i)[0] <= kb < keys(i)[1]]
            return q[0], q[-1] + 1

        def pair(st, keys, q=None, extra=None, extra_t=None, sinks=None):
            r = (slice(0, HD), slice(HD, P))
            return [{"st": st, "keys": keys, "q": q or (st["qh"], st["ql"]), "rows": r[e], "den": r[1 - e],
                     "v": slice(e * HD, e * HD + P), "e": e, "extra": extra, "extra_t": extra_t,
                     "sink": sinks + e if sinks is not None else None} for e in range(2)]

        def steps_of(heads):
            steps = []
            n = 0
            for h, job in enumerate(heads):
                nk = job["keys"](TT - 1)[1]
                for kb in range(nk):
                    steps.append((h, kb, kb, len(steps), n))
                    n += 1
                if job["sink"] is not None:
                    steps.append((h, nk, None, len(steps), n))
            return steps

        def last_step(steps, h):
            return max(x[3] for x in steps if x[0] == h and x[2] is not None)

        def last_block(steps, h):
            return max(x[4] for x in steps if x[0] == h and x[2] is not None) + 1

        def fox_extra(e, qt, lo, hi):
            return [(ident_r[:], masks_r[:, 0, :], qt * P, (qt + 1) * P),
                    (c_q[:, e, qt * P:(qt + 1) * P], c_k[:, e, lo * P:hi * P], 0, (hi - lo) * P)]

        def fox_extra_t(e, kb, q0, q1):
            return [(c_k[:, e, kb * P:(kb + 1) * P], c_q[:, e, q0 * P:q1 * P], 0, (q1 - q0) * P),
                    (masks_r[:, 0, :], ident_r[:], 0, P)]

        def dsa_extra(e, qt, lo, hi):
            if qt == 0:
                return [(ident_r[:], masks_r[:, 0, :], 0, P)]
            return [(ident_r[:], topmask[:, qt, 0:hi * P], 0, hi * P)]

        def dsa_extra_t(e, kb, q0, q1):
            return [(topmask[:, qt, kb * P:(kb + 1) * P] if qt else masks_r[:, 0, :], ident_r[:],
                     (qt - q0) * P, (qt - q0 + 1) * P) for qt in range(q0, q1)]

        def band(q, e, qt, lo, hi):
            m = []
            if lo < qt:
                m.append((ident_r[:], masks_r[:, 2, :], 0, P))
            if hi > qt + 1:
                m.append((ident_r[:], masks_r[:, 1, :], (qt + 1 - lo) * P, (qt + 2 - lo) * P))
            r = slice(e * HD, (e + 1) * HD)
            return m + [(q[r, qt * P:(qt + 1) * P], bst["kl"][r, lo * P:hi * P], 0, (hi - lo) * P)]

        def band_t(e, kb, q0, q1):
            m = []
            if kb > q0:
                m.append((masks_r[:, 1, :], ident_r[:], 0, P))
            if kb < q1 - 1:
                m.append((masks_r[:, 2, :], ident_r[:], (kb + 1 - q0) * P, (kb + 2 - q0) * P))
            return m

        mem_heads = [{"st": mst, "keys": memory, "q": (mst["qh"], mst["ql"]), "rows": slice(0, P), "den": None,
                      "v": slice(0, P), "e": 0, "extra": None, "extra_t": None, "sink": None}]
        fox_heads = pair(fst, causal, extra=fox_extra, extra_t=fox_extra_t)
        dsa_heads = (pair(dst, causal, extra=dsa_extra, extra_t=dsa_extra_t)
                     + pair(dst, causal, q=q_second, extra=dsa_extra, extra_t=dsa_extra_t))
        b2_heads = []
        for k in range(2):
            b2_heads += pair(ast, whole, q=q2[2 * k])
            b2_heads += pair(bst, window, q=q2[2 * k + 1], extra=lambda *a, k=k: band(q2[2 * k + 1][0], *a),
                             extra_t=band_t, sinks=2 * k)
        S_BANKS, T_BANKS, O_BANKS, DEN_BANK = (0, 1), (2, 3, 4), (6, 7), 5
        PV_LAG = 2

        @block.tensor
        def _(pe):
            def unit_mm(u, outs, rhs_hi, rhs_lo, n=S, per=None, before=None):
                slot = per[0] if per else 0
                pe.wait_ge(split_ready, u + 1)
                for c in range(KC):
                    if before:
                        before(c)
                    wh = w_hi[:, slot, c * P:(c + 1) * P]
                    wl = w_lo[:, slot, c * P:(c + 1) * P]
                    pe.matmul(outs[:, 0:n], wh, rhs_hi[:, c, :], start=(c == 0), stop=False)
                    pe.matmul(outs[:, 0:n], wh, rhs_lo[:, c, :], start=False, stop=False)
                    last = pe.matmul(outs[:, 0:n], wl, rhs_hi[:, c, :], start=False, stop=(c == KC - 1))
                last.then_inc(unit_done, 1)

            def panel(u, slot, b, rhs, before=None):
                unit_mm(u, bank[b], rhs[0], rhs[1], per=(slot,), before=before)

            def amid(c0, *steps):
                def before(c):
                    if c == c0:
                        for step in steps:
                            step()
                return before

            U = (u_hi, u_lo)

            def norm_sum(ni, n=S, groups=1):
                per = KC // groups
                for c in range(KC):
                    pe.wait_ge(n_sq, ni * KC + c + 1)
                    pe.matmul(bank[c // per][:, 0:n], ones, W[c % 2][:, 0:n], start=(c % per == 0),
                              stop=(c % per == per - 1)).then_inc(n_acc, 1)

            def norm_wait(ni):
                def before(c):
                    pe.wait_ge(n_lo, SPLITS[ni] * KC + c + 1)
                return before

            def ffn(fi, u0, ni):
                def two(it, first):
                    for k in range(2):
                        f = 2 * it + k
                        u = u0 + 4 * it + 2 * k
                        if not first:
                            pe.wait_ge(f_silu, fi * FT + f - 1)
                        panel(u, 0, 2 * k, U, norm_wait(ni) if first and k == 0 else None)
                        if not first:
                            pe.wait_ge(f_prod, fi * FT + f - 1)
                        panel(u + 1, 1, 2 * k + 1, U)
                two(0, True)
                with pe.Fori(1, FT // 2) as it:
                    two(it, False)
                d0 = u0 + 2 * FT

                def down(j, slot, start, stop):
                    pe.wait_ge(split_ready, d0 + j + 1)
                    pe.wait_ge(f_lo, fi * FT + j + 1)
                    for m in (4, 5, 6, 7, 0, 1, 2, 3):
                        if start and m == 0:
                            pe.wait_ge(f_prod, fi * FT + FT)
                        wh = w_hi[:, slot, m * P:(m + 1) * P]
                        wl = w_lo[:, slot, m * P:(m + 1) * P]
                        pe.matmul(bank[m][:], wh, hid_hi[:, j, :], start=start, stop=False)
                        pe.matmul(bank[m][:], wh, hid_lo[:, j, :], start=False, stop=False)
                        last = pe.matmul(bank[m][:], wl, hid_hi[:, j, :], start=False, stop=stop)
                    last.then_inc(unit_done, 1)
                down(0, 0, True, False)
                down(1, 1, False, False)
                with pe.Fori(1, FT // 2 - 1) as it:
                    for k in range(2):
                        down(2 * it + k, k, False, False)
                down(FT - 2, 0, False, False)
                down(FT - 1, 1, False, True)

            def head_sum(i, b, sq, m, n=S):
                pe.wait_ge(h_sq, i + 1)
                pe.matmul(bank[b][:, 0:n], m, sq[:, 0:n], start=True, stop=True).then_inc(h_sum, 1)

            def rotate(b, src):
                pe.matmul(bank[b][:], rot, src, start=True, stop=True).then_inc(r_rot, 1)

            def values(i_raw, b, src, n=TT):
                pe.wait_ge(v_raw, i_raw + 1)
                for kb in range(n):
                    last = pe.transpose(bank[b][:, kb * P:(kb + 1) * P], src[:, kb * P:(kb + 1) * P], ident)
                last.then_inc(v_t, 1)

            def attend(done, heads):
                s0, t0, b0, h0 = done[:4]
                steps = steps_of(heads)

                def scores(h, qt):
                    job = heads[h]
                    n = h * TT + qt
                    lo, hi = job["keys"](qt)
                    o = bank[S_BANKS[n % 2]]
                    if n >= 2:
                        pe.wait_ge(a_max, s0 + n - 1)
                    r, q, k = job["rows"], slice(qt * P, (qt + 1) * P), slice(lo * P, hi * P)
                    sums = [(job["q"][0][r, q], job["st"]["kh"][r, k], 0, (hi - lo) * P)]
                    if job["extra"]:
                        sums += job["extra"](job["e"], qt, lo, hi)
                    for i, (lhs, rhs, c0, c1) in enumerate(sums):
                        last = pe.matmul(o[:, c0:c1], lhs, rhs, start=i == 0, stop=i == len(sums) - 1)
                    last.then_inc(a_s, 1)

                def scores_t(h, i, kb, t):
                    job = heads[h]
                    q0, q1 = q_blocks(job["keys"], kb) if kb is not None else (0, TT)
                    n = (q1 - q0) * P
                    o = bank[T_BANKS[t % 3]][:, 0:n]
                    if t >= 3:
                        pe.wait_ge(a_e, t0 + t - 2)
                    if kb is not None:
                        r, k, q = job["rows"], slice(kb * P, (kb + 1) * P), slice(q0 * P, q1 * P)
                        (qh, ql), kh, kl = job["q"], job["st"]["kh"], job["st"]["kl"]
                        pe.matmul(o, kh[r, k], qh[r, q], start=True, stop=False)
                        if job["extra_t"]:
                            for lhs, rhs, c0, c1 in job["extra_t"](job["e"], kb, q0, q1):
                                pe.matmul(bank[T_BANKS[t % 3]][:, c0:c1], lhs, rhs, start=False, stop=False)
                        pe.matmul(o, kh[r, k], ql[r, q], start=False, stop=False)
                        pe.matmul(o, kl[r, k], qh[r, q], start=False, stop=False)
                    if i == 0:
                        pe.wait_ge(a_shift, h0 + h + 1)
                    pe.matmul(o, ones_r[:], shift[:, h % 2, q0 * P:q1 * P], start=kb is None, stop=True).then_inc(a_t, 1)

                def values_mm(h, i, kb, b):
                    job = heads[h]
                    st, keys = job["st"], job["keys"]
                    nk = keys(TT - 1)[1]
                    q0, q1 = q_blocks(keys, kb)
                    c = slice(q0 * P, q1 * P)
                    o = bank[O_BANKS[h % 2]]
                    if kb == 0 and h >= 2:
                        pe.wait_ge(a_o, h0 + h - 1)
                    pe.wait_ge(a_pl, b0 + b + 1)
                    slot = b % nk
                    ph, pl = st["ph"][:, slot, c], st["pl"][:, slot, c]
                    vh, vl = st["vh"][:, kb, job["v"]], st["vl"][:, kb, job["v"]]
                    ragged_first, ragged_last = kb == 0 and q1 < TT, kb == nk - 1 and q0 > 0
                    if ragged_first:
                        pe.matmul(o[:], zero_r[:], st["kh"][:], start=True, stop=False)
                    pe.matmul(o[:, c], vh, ph, start=kb == 0 and not ragged_first, stop=False)
                    pe.matmul(o[:, c], vh, pl, start=False, stop=False)
                    last = pe.matmul(o[:, c], vl, ph, start=False, stop=kb == nk - 1 and not ragged_last)
                    if ragged_last:
                        last = pe.matmul(o[:], zero_r[:], st["kh"][:], start=False, stop=True)
                    if job["den"] is None:
                        pe.matmul(bank[DEN_BANK][:], ones_r[:], ph, start=kb == 0, stop=False)
                        last = pe.matmul(bank[DEN_BANK][:], ones_r[:], pl, start=False, stop=kb == nk - 1)
                    last.then_inc(a_pv, 1)

                for qt in range(TT):
                    scores(0, qt)
                for x, (h, i, kb, t, b) in enumerate(steps):
                    scores_t(h, i, kb, t)
                    if h + 1 < len(heads) and i < TT // 2:
                        scores(h + 1, 2 * i)
                        scores(h + 1, 2 * i + 1)
                    if x >= PV_LAG and steps[x - PV_LAG][2] is not None:
                        h_, i_, kb_, t_, b_ = steps[x - PV_LAG]
                        values_mm(h_, i_, kb_, b_)
                for h, i, kb, t, b in steps[-PV_LAG:]:
                    if kb is not None:
                        values_mm(h, i, kb, b)

            pe.wait_ge(ld_const, 16)
            pe.wait_ge(ld_gain, 16 * 25)
            pe.transpose(bank[7][:, 0:N_GAIN], gain_rows[:, :], ident[0:N_GAIN, 0:N_GAIN]).then_inc(gain_t, 1)
            pe.wait_ge(ld_x, 16)
            pe.wait_ge(gain_ready, 1)
            for c in range(KC):
                for i in range(TT):
                    last = pe.transpose(bank[c][:, i * P:(i + 1) * P], x_tok[:, i, c * P:(c + 1) * P], ident)
                last.then_inc(xt_done, 1)
            pe.wait_ge(x_ready, KC)

            norm_sum(N_F1)
            ffn(0, U_GU1, N_F1)

            pe.wait_ge(f_out, KC)
            norm_sum(N_MIX)
            for k in range(4):
                pe.wait_ge(n_std, N_MIX + 1)
                panel(U_PREP + k, k % SPL, k, U, norm_wait(N_MIX) if k == 0 else None)
            head_sum(H_PREP, 4, W[0], blk64)
            pe.wait_ge(r_raw, RR_PREP + 2)
            rotate(6, W[2])
            for i in range(TT):
                last = pe.transpose(bank[5][:, i * HD:(i + 1) * HD], W[7][0:HD, i * P:(i + 1) * P], ident[0:HD, 0:HD])
            last.then_inc(iw_t, 1)
            pe.wait_ge(h_out, H_PREP + 1)
            rotate(7, W[1])
            pe.wait_ge(ld_mem, 16)
            pe.wait_ge(r_out, R_PREP + 2)
            pe.wait_ge(iw_ready, 1)
            pe.wait_ge(v_raw, VR_PREP + 1)
            for c in range(KC):
                for i in range(MT):
                    last = pe.transpose(bank[c][:, i * P:(i + 1) * P], m_tok[:, i, c * P:(c + 1) * P], ident)
                last.then_inc(mt_done, 1)
            pe.wait_ge(m_ready, KC)
            norm_sum(N_MEM, MEM)
            pe.wait_ge(n_std, N_MEM + 1)

            def mem_head(i, first):
                u, h = U_MEM + 4 * i, H_MEM + 2 * i
                if not first:
                    pe.wait_ge(a_o, i)
                panel(u, 0, 2, U)

                def km_hook(c):
                    if first:
                        norm_wait(N_MEM)(c)
                    if c == 5:
                        head_sum(h, 6, W[0], ones)
                unit_mm(u + 1, bank[3], m_hi, m_lo, n=MEM, per=(1,), before=km_hook)
                unit_mm(u + 2, bank[4], m_hi, m_lo, n=MEM, per=(0,),
                        before=amid(6, lambda: head_sum(h + 1, 7, W[2], ones, MEM)))
                panel(u + 3, 1, 5, U, amid(3, lambda: values(VR_MEM + i, 1, W[4], MT)))
                pe.wait_ge(r_raw, RR_MEM + i + 1)
                pe.wait_ge(s_lo, S_MEM + 3 * i + 3)
                attend(done_before(A_MEM, (4, 2, 2, 1, 1), i), mem_heads)
            mem_head(0, True)
            with pe.Fori(1, 4) as i:
                mem_head(i, False)

            def fox_pair(i, first):
                u, h = U_FOX + 4 * i, H_FOX + 2 * i
                pe.wait_ge(a_o, A_FOX[3] + 2 * i)
                rotate(0, iq[:, bass.ds(i, 1), :].rearrange("p a n -> p (a n)"))
                panel(u, 0, 2, U)
                panel(u + 1, 1, 3, U, amid(3, lambda: head_sum(h, 6, W[0], blk64)))
                panel(u + 2, 0, 4, U, amid(3, lambda: head_sum(h + 1, 7, W[2], blk64)))
                panel(u + 3, 1, 5, U, amid(3, lambda: values(VR_FOX + i, 1, W[6])))
                pe.wait_ge(s_lo, S_FOX + 3 * i + 3)
                pe.wait_ge(ld_c, 32 * (i + 1))
                pe.wait_ge(r_out, R_IQ + i + 1)
                attend(done_before(A_FOX, (8, 8, 8, 2, 1), i), fox_heads)
            fox_pair(0, True)
            with pe.Fori(1, 4) as i:
                fox_pair(i, False)

            pe.wait_ge(a_o, A_DSA[3])
            pe.wait_ge(s_lo, S_IDX + 1)

            def index_pair(i, first):
                pe.wait_ge(s_lo, S_IDX + 2 + i)
                for k in range(6):
                    e, qt = k // 3, 1 + k % 3
                    n = (qt + 1) * P
                    r = slice(e * HD, (e + 1) * HD)
                    if not first or k >= 2:
                        pe.wait_ge(ix_relu, 6 * i + k - 1)
                    b = bank[k % 2][:, 0:n]
                    q = slice(qt * P, (qt + 1) * P)
                    pe.matmul(b, ist["qh"][r, q], ist["kh"][r, 0:n], start=True, stop=False)
                    pe.matmul(b, ist["qh"][r, q], ist["kl"][r, 0:n], start=False, stop=False)
                    pe.matmul(b, ist["ql"][r, q], ist["kh"][r, 0:n], start=False, stop=True).then_inc(ix_s, 1)
            index_pair(0, True)
            with pe.Fori(1, 4) as i:
                index_pair(i, False)

            def gates(i, first, hooks=(None,) * 4):
                for k in range(4):
                    if not first:
                        pe.wait_ge(g_sig, 4 * i + k - 3)
                    panel(U_GATE + 4 * i + k, k % SPL, 2 + k, U, hooks[k])
            gates(0, True)
            gates(1, False)
            with pe.Fori(2, 6) as i:
                gates(i, False, (None, amid(3, lambda: head_sum(H_DQ + i - 2, 6, W[4], blk64)), None, None))
                pe.wait_ge(h_out, H_DQ + i - 1)
                pe.wait_ge(r_out, R_DQ + i - 2)
                rotate(7, dq[:, bass.ds(i - 2, 1), :].rearrange("p a n -> p (a n)"))

            pe.wait_ge(ix_relu, 24)
            pe.wait_ge(g_sig, 24)
            values(VR_PREP, 1, dvT)
            pe.wait_ge(s_lo, S_DSA + 2)
            pe.wait_ge(tk_mask, 3)

            with pe.Fori(0, 2) as i:
                pe.wait_ge(a_o, A_DSA[3] + 4 * i)
                pe.wait_ge(s_lo, S_DSA + 4 + 2 * i)
                attend(done_before(A_DSA, (16, 16, 16, 4, 2), i), dsa_heads)

            pe.wait_ge(o_split, 3)
            pe.wait_ge(a_o, A_B2[3])

            def branches(it, first):
                for kk in range(6):
                    k = 6 * it + kk
                    n = kk % 3
                    slot = kk % SPL
                    if not first or kk >= 3:
                        pe.wait_ge(b_mul, 2 * k - 4)
                    pe.wait_ge(split_ready, U_BR + k + 1)
                    for half in range(2):
                        o = bank[2 * n + half][:]
                        for c in range(4):
                            a = c * 2 * P + half * P
                            oc = 4 * n + c
                            pe.matmul(o, w_hi[:, slot, a:a + P], o_hi[:, oc, :], start=(c == 0), stop=False)
                            pe.matmul(o, w_hi[:, slot, a:a + P], o_lo[:, oc, :], start=False, stop=False)
                            last = pe.matmul(o, w_lo[:, slot, a:a + P], o_hi[:, oc, :], start=False, stop=(c == 3))
                    last.then_inc(unit_done, 1)
            branches(0, True)
            with pe.Fori(1, 2) as it:
                branches(it, False)

            def w_out(u0, rhs, r0, before=None):
                for i in range(2):
                    for k in range(4):
                        if i:
                            pe.wait_ge(res, r0 + k + 1)
                        panel(u0 + 4 * i + k, k % SPL, k, rhs, before if i == 0 and k == 0 else None)
            pe.wait_ge(b_mul, 24)
            w_out(U_WO, (mix_hi, mix_lo), 0, lambda c: pe.wait_ge(b_lo, c + 1))

            pe.wait_ge(res, KC)
            norm_sum(N_F2)
            pe.wait_ge(n_std, N_F2 + 1)
            ffn(1, U_GU2, N_F2)

            pe.wait_ge(f_out, 2 * KC)
            norm_sum(N_PRE)
            pe.wait_ge(n_std, N_PRE + 1)

            def key_head(i, first):
                u = U_B2 + 8 * i
                h, r, rr, s, vr = H_B2 + 3 * i, R_B2 + 6 * i, RR_B2 + 3 * i, S_B2 + 8 * i, VR_B2 + 2 * i
                pe.wait_ge(a_o, A_B2[3] + 8 * i)
                panel(u, 0, 2, U, norm_wait(N_PRE) if first else None)
                panel(u + 1, 1, 3, U, amid(3, lambda: head_sum(h, 6, W[0], blk64)))
                panel(u + 2, 0, 4, U, amid(3, lambda: head_sum(h + 1, 7, W[5], blk64)))

                def turn_ka():
                    pe.wait_ge(h_out, h + 1)
                    rotate(1, W[1])
                panel(u + 3, 1, 5, U, amid(3, lambda: head_sum(h + 2, 0, rtmp[:, 6, :], blk64), turn_ka))

                def turn_kb():
                    pe.wait_ge(r_raw, rr + 1)
                    rotate(6, W[3])
                panel(u + 4, 0, 2, U, amid(3, turn_kb))

                def turn_qa():
                    pe.wait_ge(h_out, h + 2)
                    rotate(7, W[6])
                panel(u + 5, 1, 3, U, amid(3, turn_qa))

                def turn_qb():
                    pe.wait_ge(h_std, h + 3)
                    pe.wait_ge(r_raw, rr + 2)
                    rotate(0, W[7])
                panel(u + 6, 0, 4, U, amid(3, turn_qb))

                def turn_second():
                    pe.wait_ge(h_out, h + 3)
                    pe.wait_ge(r_out, r + 1)
                    rotate(1, rtmp[:, 7, :])
                    pe.wait_ge(r_raw, rr + 3)
                    pe.wait_ge(r_out, r + 2)
                    rotate(6, rtmp[:, 8, :])
                panel(u + 7, 1, 5, U, amid(4, turn_second))
                pe.wait_ge(r_out, r + 4)
                values(vr, 7, W[2])
                values(vr + 1, 0, W[4])
                pe.wait_ge(s_lo, s + 8)
                attend(done_before(A_B2, (32, 36, 32, 8, 4), i), b2_heads)
            key_head(0, True)
            with pe.Fori(1, 2) as i:
                key_head(i, False)

            pe.wait_ge(a_o, A_B2[3] + 16)
            norm_sum(N_GRP, groups=2)
            pe.wait_ge(n_std, N_GRP + 2)
            w_out(U_WO2, U, 8, norm_wait(N_GRP))
            pe.wait_ge(res, 2 * KC)
            norm_sum(N_POST)
            pe.wait_ge(x_ready, 2 * KC)
            norm_sum(N_FPRE)
            pe.wait_ge(n_std, N_FPRE + 2)

            ffn(2, U_GU3, N_FPRE)
            pe.wait_ge(f_out, 3 * KC)
            norm_sum(N_FPOST)
            pe.wait_ge(n_std, N_FPOST + 2)
            pe.wait_ge(x_ready, 3 * KC)
            for i in range(TT):
                if i >= 2:
                    pe.wait_ge(o_ready_a, i - 1)
                    pe.wait_ge(o_ready_b, i - 1)
                for half in range(2):
                    for c in range(4):
                        last = pe.transpose(bank[2 * (i % 2) + half][:, c * P:(c + 1) * P],
                                            hT[:, 4 * half + c, i * P:(i + 1) * P], ident)
                    last.then_inc(ot_done, 1)

        @block.scalar
        def _(act):
            def copy(out_, in_, s, **kw):
                act.activation(out_, in_, ACT.Copy, **kw).then_inc(s, 1)

            def squares(ni, src, ready, n=S):
                for c in range(KC):
                    ready(c)
                    if ni * KC + c >= 2:
                        act.wait_ge(n_acc, ni * KC + c - 1)
                    act.activation(W[c % 2][:, 0:n], src[:, c, :], ACT.Square).then_inc(n_sq, 1)

            def norm_std(ni, n=S, groups=1, extra=0):
                act.wait_ge(n_acc, ni * KC + KC)
                for g in range(groups):
                    act.activation(W[2 + g][:, 0:n], bank[g][:, 0:n], ACT.Sqrt, scale=groups / D, bias=EPS).then_inc(n_std, 1)

            def norm_hi(ni, dst, n=S):
                for c in range(KC):
                    act.wait_ge(n_t, ni * KC + c + 1)
                    act.activation(dst[:, c, :], W[4 + c % 2][:, 0:n], ACT.Copy).then_inc(n_hi, 1)

            def ffn(fi, u0):
                def silu(f, k, u, first):
                    act.wait_ge(unit_done, u + 1)
                    if not first:
                        act.wait_ge(f_prod, fi * FT + f - 1)
                    act.activation(W[6 + k], bank[2 * k][:], ACT.Silu).then_inc(f_silu, 1)

                def high(f, k):
                    act.wait_ge(f_prod, fi * FT + f + 1)
                    act.activation(hid_hi[:, f, :], W[8 + k], ACT.Copy).then_inc(f_hi, 1)

                def two(it, first):
                    for k in range(2):
                        f = 2 * it + k
                        silu(f, k, u0 + 4 * it + 2 * k, first)
                        high(f, k)
                two(0, True)
                with act.Fori(1, FT // 2) as it:
                    two(it, False)

            def head_square(i, u, b, sq, rw, n=S):
                act.wait_ge(unit_done, u + 1)
                act.activation(sq[:, 0:n], bank[b][:, 0:n], ACT.Square).then_inc(h_sq, 1)
                copy(rw[:, 0:n], bank[b][:, 0:n], h_raw)

            def head_std(i, b, sq, width, n=S):
                act.wait_ge(h_sum, i + 1)
                act.activation(sq[:, 0:n], bank[b][:, 0:n], ACT.Sqrt, scale=1.0 / width, bias=EPS).then_inc(h_std, 1)

            def raw_copy(u, b, dst):
                act.wait_ge(unit_done, u + 1)
                copy(dst, bank[b][:], r_raw)

            def value_copy(u, b, dst, n=S):
                act.wait_ge(unit_done, u + 1)
                copy(dst[:, 0:n], bank[b][:, 0:n], v_raw)

            def attend(done, heads, put):
                s0, t0, b0, h0, g0 = done
                steps = steps_of(heads)

                def exps(h, i, kb, t, b):
                    job = heads[h]
                    o = bank[T_BANKS[t % 3]]
                    act.wait_ge(a_t, t0 + t + 1)
                    if kb is None:
                        r, k = job["rows"], job["sink"]
                        act.activation(sink_e[r], o[r, :], ACT.Exp, bias=sink_now[r, k:k + 1]).then_inc(a_e, 1)
                        return
                    nk = job["keys"](TT - 1)[1]
                    q0, q1 = q_blocks(job["keys"], kb)
                    c = slice(q0 * P, q1 * P)
                    if b >= nk:
                        act.wait_ge(a_pv, b0 + b - nk + 1)
                    act.activation(job["st"]["ph"][:, b % nk, c], o[:, 0:(q1 - q0) * P], ACT.Exp)
                    if b >= 3:
                        act.wait_ge(a_pl, b0 + b - 2)
                    act.activation(prob[b % 3][:, c], o[:, 0:(q1 - q0) * P], ACT.Exp).then_inc(a_e, 1)

                def output(h):
                    job = heads[h]
                    r, o = job["rows"], bank[O_BANKS[h % 2]]
                    act.wait_ge(a_pv, b0 + last_block(steps, h))
                    if h % 2 == 0 and not (isinstance(g0, int) and g0 + h == 0):
                        act.wait_ge(a_rec, g0 + h // 2)
                    act.activation(put(r, h // 2), o[r, :], ACT.Copy)
                    act.activation(den[r], bank[DEN_BANK][:] if job["den"] is None else o[job["den"], :],
                                   ACT.Copy).then_inc(a_o, 1)

                ends = {last_step(steps, h): h for h in range(len(heads))}
                for x in range(len(steps) + PV_LAG + 1):
                    if x < len(steps):
                        exps(*steps[x])
                    if x - PV_LAG - 1 in ends:
                        output(ends[x - PV_LAG - 1])

            def value_high(vt, b, st):
                act.wait_ge(v_t, vt + 1)
                for e in range(2):
                    last = act.activation(st["vh"][:, :, 2 * e * HD:(2 * e + 1) * HD],
                                          bank[b][:].rearrange("p (k n) -> p k n", k=TT)[:, :, e * HD:(e + 1) * HD],
                                          ACT.Copy)
                last.then_inc(s_hi, 1)

            act.dma_start(const[:, 0:N_CONST], t["const"]).then_inc(ld_const, 16)
            act.dma_start(x_tok[:], t["x"][0].rearrange("(i p) d -> p i d", p=P)).then_inc(ld_x, 16)
            act.wait_ge(gain_zero, 1)
            for row, name in ((G_F1, "ffn1_norm"), (G_MIX, "mix_norm"), (G_MEM, "mem_norm"), (G_F2, "ffn2_norm"),
                              (G_PRE2, "norm_mix_pre_2"), (G_POST2, "norm_mix_post_2"),
                              (G_FPRE2, "norm_ffn_pre_2"), (G_FPOST2, "norm_ffn_post_2")):
                act.dma_start(gain_rows[row:row + KC, :], t[name][0].rearrange("(c p) -> c p", p=P)).then_inc(ld_gain, 16)
            for k, name in enumerate(("group_norm_a_2", "group_norm_b_2")):
                act.dma_start(gain_rows[G_GN + 4 * k:G_GN + 4 * k + 4, :],
                              t[name][0].rearrange("(c p) -> c p", p=P)).then_inc(ld_gain, 16)
            for row, name in ((G_FQ, "fox_q_norm"), (G_FK, "fox_k_norm"), (G_DQ, "dsa_q_norm"), (G_DK, "dsa_k_norm"),
                              (G_QA, "q_norm_a_2"), (G_KA, "k_norm_a_2")):
                for h in range(2):
                    act.dma_start(gain_rows[row:row + 1, h * HD:(h + 1) * HD], t[name]).then_inc(ld_gain, 16)
            act.dma_start(gain_rows[G_MQ:G_MQ + 1, :], t["mem_q_norm"]).then_inc(ld_gain, 16)
            act.dma_start(gain_rows[G_MK:G_MK + 1, :], t["mem_k_norm"]).then_inc(ld_gain, 16)
            act.dma_start(gain_rows[G_BF:G_BF + 1, 0:HEADS], t["b_forget"]).then_inc(ld_gain, 16)
            act.dma_start(pos_i[:], t["positions"].to_broadcast([P, S])).then_inc(ld_pos, 16)
            act.dma_start(sink[:], t["sink_b_2"].to_broadcast([P, HEADS])).then_inc(ld_sink, 16)

            def x_here(c):
                act.wait_ge(x_ready, c + 1)
            squares(N_F1, hT, x_here)
            norm_std(N_F1)
            norm_hi(N_F1, u_hi)
            ffn(0, U_GU1)
            act.wait_ge(trig, N_ANGLE)
            act.activation(sin1[:], W[0], ACT.Sin).then_inc(trig_a, 1)
            act.activation(cos1[:], W[1], ACT.Sin).then_inc(trig_a, 1)

            def f_here(fi):
                return lambda c: act.wait_ge(f_out, fi * KC + c + 1)
            squares(N_MIX, hT, f_here(0))
            act.dma_start(m_tok[:], t["mem"][0].rearrange("(i p) d -> p i d", p=P)).then_inc(ld_mem, 16)
            norm_std(N_MIX)
            norm_hi(N_MIX, u_hi)
            act.wait_ge(n_lo, (N_MIX + 1) * KC)
            act.wait_ge(unit_done, U_PREP + 1)
            copy(W[7][0:HD], bank[0][0:HD, :], r_raw)
            raw_copy(U_PREP + 1, 1, W[2])
            head_square(H_PREP, U_PREP + 2, 2, W[0], W[1])
            value_copy(U_PREP + 3, 3, dvT[:])
            head_std(H_PREP, 4, W[0], HD)
            act.wait_ge(iw_t, 1)
            act.activation(iw_tok[:], bank[5][:, 0:TT * HD].rearrange("p (i n) -> p i n", i=TT)[:, :, 32:32 + HEADS],
                           ACT.Copy, scale=float(HEADS ** -0.5 * HD ** -0.5)).then_inc(iw_ready, 1)
            act.wait_ge(fg, 3)
            act.activation(W[9][0:HEADS], W[9][0:HEADS], ACT.Exp).then_inc(fg_a, 1)
            act.wait_ge(fg_a, 1)
            act.activation(W[9][0:HEADS], W[9][0:HEADS], ACT.Ln, bias=1.0).then_inc(fg_a, 1)
            for c in range(KC):
                act.wait_ge(mt_done, c + 1)
                copy(mT[:, c, :], bank[c][:, 0:MEM], m_ready)
            act.wait_ge(c_ready, 2)
            for part in range(2):
                act.dma_start(c_dram[part], c_sum[32 * part:32 * part + HEADS, :].bitcast(F32)).then_inc(c_stored, 16)
            squares(N_MEM, mT, lambda c: act.wait_ge(m_ready, c + 1), MEM)
            norm_std(N_MEM, MEM)
            norm_hi(N_MEM, m_hi, MEM)
            act.wait_ge(n_lo, (N_MEM + 1) * KC)

            def mem_head(i, first):
                u, h = U_MEM + 4 * i, H_MEM + 2 * i
                head_square(h, u, 2, W[0], W[1])
                if not first:
                    act.wait_ge(a_out, i)
                head_square(h + 1, u + 1, 3, W[2], W[3], MEM)
                head_std(h, 6, W[0], P)
                value_copy(u + 2, 4, W[4], MEM)
                head_std(h + 1, 7, W[2], P, MEM)
                raw_copy(u + 3, 5, iq[:, bass.ds(i, 1), :].rearrange("p a n -> p (a n)"))
                act.wait_ge(h_out, h + 1)
                copy(mst["qh"][:], W[1], s_hi)
                act.wait_ge(h_out, h + 2)
                copy(mst["kh"][:], W[3][:, 0:MEM], s_hi)
                act.wait_ge(v_t, VT_MEM + i + 1)
                copy(mst["vh"][:], bank[1][:, 0:MEM].rearrange("p (k n) -> p k n", k=MT), s_hi)
                attend(done_before(A_MEM, (4, 2, 2, 1, 1), i), mem_heads, lambda r, g: oT[r, 8 + i, :])
            mem_head(0, True)
            with act.Fori(1, 4) as i:
                mem_head(i, False)

            def fox_pair(i, first):
                u, h = U_FOX + 4 * i, H_FOX + 2 * i
                if first:
                    act.wait_ge(c_one, 2)
                    act.wait_ge(c_stored, 32)
                for dst_, r in ((c_q, 0), (c_k, 2)):
                    act.dma_start(dst_[r:r + 2, :, :].bitcast(F32), c_dram[:, bass.ds(2 * i, 2), :]).then_inc(ld_c, 16)
                head_square(h, u, 2, W[0], W[1])
                act.wait_ge(a_out, A_FOX[4] + i)
                head_square(h + 1, u + 1, 3, W[2], W[3])
                head_std(h, 6, W[0], HD)
                value_copy(u + 2, 4, W[6])
                head_std(h + 1, 7, W[2], HD)
                act.wait_ge(h_out, h + 1)
                copy(fst["qh"][:], W[1], s_hi)
                act.wait_ge(h_out, h + 2)
                copy(fst["kh"][:], W[3], s_hi)
                value_high(VT_FOX + i, 1, fst)
                raw_copy(u + 3, 5, dq[:, bass.ds(i, 1), :].rearrange("p a n -> p (a n)"))
                attend(done_before(A_FOX, (8, 8, 8, 2, 1), i), fox_heads, lambda r, g: oT[r, i, :])
            fox_pair(0, True)
            with act.Fori(1, 4) as i:
                fox_pair(i, False)

            act.wait_ge(a_o, A_DSA[3])
            copy(ist["kh"][:], ik[:], s_hi)

            def index_pair(i, first):
                if not first:
                    act.wait_ge(ix_s, 6 * i)
                copy(ist["qh"][:], iq[:, i, :], s_hi)
                for k in range(6):
                    n = (2 + k % 3) * P
                    act.wait_ge(ix_s, 6 * i + k + 1)
                    if not first or k >= 2:
                        act.wait_ge(ix_acc, 6 * i + k - 1)
                    act.activation(W[k % 2][:, 0:n], bank[k % 2][:, 0:n], ACT.Relu).then_inc(ix_relu, 1)
            index_pair(0, True)
            with act.Fori(1, 4) as i:
                index_pair(i, False)

            act.wait_ge(ix_s, 24)

            def gate(i, k):
                act.wait_ge(unit_done, U_GATE + 4 * i + k + 1)
                act.activation(sig[:, 4 * i + k, :], bank[2 + k][:], ACT.Sigmoid).then_inc(g_sig, 1)
            with act.Fori(0, 2) as i:
                for k in range(4):
                    gate(i, k)
            act.wait_ge(a_out, A_DSA[4])
            with act.Fori(2, 6) as i:
                act.wait_ge(h_out, H_DQ + i - 2)
                act.activation(W[4], dq[:, bass.ds(i - 2, 1), :].rearrange("p a n -> p (a n)"), ACT.Square).then_inc(h_sq, 1)
                gate(i, 0)
                head_std(H_DQ + i - 2, 6, W[4], HD)
                for k in range(1, 4):
                    gate(i, k)

            act.wait_ge(r_out, R_DQ + 4)
            act.wait_ge(ix_acc, 24)
            copy(dst["kh"][:], dk[:], s_hi)
            value_high(VT_DSA, 1, dst)
            with act.Fori(0, 2) as i:
                act.wait_ge(a_t, A_DSA[1] + 16 * i)
                copy(dst["qh"][:], dq[:, bass.ds(2 * i, 1), :], s_hi)
                copy(q_second[0][:], dq[:, bass.ds(2 * i + 1, 1), :], s_hi)
                attend(done_before(A_DSA, (16, 16, 16, 4, 2), i), dsa_heads,
                       lambda r, g: oT[r, bass.ds(2 * i + 4 + g, 1), :])

            act.wait_ge(a_out, A_B2[4])
            for n in range(3):
                copy(o_hi[:, 4 * n:4 * n + 4, :], oT[:, 4 * n:4 * n + 4, :], o_split_hi)
            act.wait_ge(o_split, 3)
            with act.Fori(0, 4) as i:
                for k in range(2):
                    m = 2 * i + k
                    act.wait_ge(b_add, 4 * i + 3 + k)
                    act.activation(mix_hi[:, m, :], W[3 * k], ACT.Copy).then_inc(b_hi, 1)

            squares(N_F2, hT, lambda c: act.wait_ge(res, c + 1))
            norm_std(N_F2)
            act.wait_ge(unit_done, U_GU2)
            norm_hi(N_F2, u_hi)
            ffn(1, U_GU2)

            squares(N_PRE, hT, f_here(1))
            act.dma_start(tab2[:], t["rope2"]).then_inc(ld_tab, 16)
            norm_std(N_PRE)
            norm_hi(N_PRE, u_hi)
            act.wait_ge(n_lo, (N_PRE + 1) * KC)

            def key_head(i, first):
                u = U_B2 + 8 * i
                h, r, s, vt = H_B2 + 3 * i, R_B2 + 6 * i, S_B2 + 8 * i, VT_B2 + 2 * i
                head_square(h, u, 2, W[0], W[1])
                act.wait_ge(a_out, A_B2[4] + 4 * i)
                head_square(h + 1, u + 1, 3, W[5], W[6])
                head_std(h, 6, W[0], HD)
                head_square(h + 2, u + 2, 4, rtmp[:, 6, :], rtmp[:, 7, :])
                head_std(h + 1, 7, W[5], HD)
                raw_copy(u + 3, 5, W[3])
                head_std(h + 2, 0, rtmp[:, 6, :], HD)

                def high(k):
                    act.wait_ge(r_out, r + k + 1)
                    copy((ast["kh"], bst["kh"], *(q[0] for q in q2))[k][:], rtmp[:, k, :], s_hi,
                         scale=HD ** -0.5 if k in (3, 5) else 1.0)
                high(0)
                raw_copy(u + 4, 2, W[7])
                raw_copy(u + 5, 3, rtmp[:, 8, :])
                high(1)
                high(2)
                value_copy(u + 6, 4, W[2])
                high(3)
                value_copy(u + 7, 5, W[4])
                high(4)
                high(5)
                value_high(vt, 7, ast)
                value_high(vt + 1, 0, bst)
                copy(sink_now[:, 0:4], sink[:, bass.ds(4 * i, 4)], a_sink)
                attend(done_before(A_B2, (32, 36, 32, 8, 4), i), b2_heads,
                       lambda r, g: o2T[r, (g % 2) * 4 + 2 * i + g // 2, :])
            act.wait_ge(ld_sink, 16)
            key_head(0, True)
            with act.Fori(1, 2) as i:
                key_head(i, False)

            squares(N_GRP, o2T, lambda c: act.wait_ge(a_out, A_B2[4] + 8))
            norm_std(N_GRP, groups=2)
            norm_hi(N_GRP, u_hi)
            act.wait_ge(unit_done, U_WO2 + 8)
            squares(N_POST, mo, lambda c: act.wait_ge(res, KC + c + 1))
            norm_std(N_POST)
            squares(N_FPRE, hT, lambda c: act.wait_ge(x_ready, KC + c + 1))
            norm_std(N_FPRE)
            norm_hi(N_FPRE, u_hi)
            ffn(2, U_GU3)
            squares(N_FPOST, fT, f_here(2))
            norm_std(N_FPOST)
            for i in range(TT):
                act.wait_ge(ot_done, 2 * i + 2)
                if i >= 2:
                    act.wait_ge(stored[i % 2], 16 * (i // 2))
                copy(out_tok[:, i % 2, 512:1024], bank[2 * (i % 2) + 1][:], o_ready_b)

        @block.vector
        def _(dve):
            def norm_recip(ni, std_no, n=S, groups=1, rec_no=None):
                for g in range(groups):
                    dve.wait_ge(n_std, std_no + g + 1)
                    dve.reciprocal(W[2 + g][:, 0:n], W[2 + g][:, 0:n]).then_inc(n_rec, 1)

            def norm_split(ni, std_no, src, g0, hi, lo, n=S, groups=1):
                norm_recip(ni, std_no, n, groups)
                per = KC // groups

                def low(c):
                    dve.wait_ge(n_hi, SPLITS[ni] * KC + c + 1)
                    dve.tensor_tensor(lo[:, c, :], W[4 + c % 2][:, 0:n], hi[:, c, :].bitcast(F32),
                                      ALU.subtract).then_inc(n_lo, 1)
                dve.wait_ge(n_rec, std_no + groups)
                for c in range(KC):
                    if c >= 2:
                        dve.wait_ge(n_lo, SPLITS[ni] * KC + c - 1)
                    dve.scalar_tensor_tensor(out=W[4 + c % 2][:, 0:n], in0=src[:, c, :], scalar=gain[:, g0 + c:g0 + c + 1],
                                             in1=W[2 + c // per][:, 0:n], op0=ALU.mult, op1=ALU.mult).then_inc(n_t, 1)
                    if c:
                        low(c - 1)
                low(KC - 1)

            def ffn(fi, u0, finish, between=None):
                def two(it, first):
                    for k in range(2):
                        f = 2 * it + k
                        if not first:
                            dve.wait_ge(f_lo, fi * FT + f - 1)
                        dve.wait_ge(f_silu, fi * FT + f + 1)
                        dve.wait_ge(unit_done, u0 + 4 * it + 2 * k + 2)
                        dve.tensor_tensor(W[8 + k], W[6 + k], bank[2 * k + 1][:], ALU.mult).then_inc(f_prod, 1)
                        dve.wait_ge(f_hi, fi * FT + f + 1)
                        dve.tensor_tensor(hid_lo[:, f, :], W[8 + k], hid_hi[:, f, :].bitcast(F32),
                                          ALU.subtract).then_inc(f_lo, 1)
                two(0, True)
                with dve.Fori(1, FT // 2) as it:
                    two(it, False)
                if between:
                    between()
                dve.wait_ge(unit_done, u0 + 3 * FT)
                for m in range(KC):
                    finish(m)

            def half_residual(m):
                dve.scalar_tensor_tensor(out=hT[:, m, :], in0=bank[m][:], scalar=0.5, in1=hT[:, m, :],
                                         op0=ALU.mult, op1=ALU.add).then_inc(f_out, 1)

            def head_norm(i, sq, rw, g, n=S):
                dve.wait_ge(h_std, i + 1)
                dve.reciprocal(sq[:, 0:n], sq[:, 0:n]).then_inc(h_rec, 1)
                dve.wait_ge(h_rec, i + 1)
                dve.scalar_tensor_tensor(out=rw[:, 0:n], in0=rw[:, 0:n], scalar=gain[:, g:g + 1], in1=sq[:, 0:n],
                                         op0=ALU.mult, op1=ALU.mult).then_inc(h_out, 1)

            def rope(j, src, b, cos, sin, tmp, dst_):
                if src is dst_:
                    dve.wait_ge(r_rot, j + 1)
                dve.tensor_tensor(dst_, src, cos, ALU.mult).then_inc(r_cos, 1)
                if not isinstance(j, int) or j:
                    dve.wait_ge(r_out, j)
                dve.wait_ge(r_rot, j + 1)
                dve.tensor_tensor(tmp, bank[b][:], sin, ALU.mult).then_inc(r_sin, 1)
                dve.wait_ge(r_cos, j + 1)
                dve.wait_ge(r_sin, j + 1)
                dve.tensor_tensor(dst_, dst_, tmp, ALU.add).then_inc(r_out, 1)

            def low(i, dst_, src, hi):
                dve.wait_ge(s_hi, i + 1)
                dve.tensor_tensor(dst_, src, hi.bitcast(F32), ALU.subtract).then_inc(s_lo, 1)

            def attend(done, heads, put, sink0=0):
                s0, t0, b0, h0, g0 = done
                steps = steps_of(heads)
                sunk = [h for h, job in enumerate(heads) if job["sink"] is not None]

                def maxes(h, qt):
                    lo, hi = heads[h]["keys"](qt)
                    n = h * TT + qt
                    dve.wait_ge(a_s, s0 + n + 1)
                    dve.tensor_reduce(rowmax[:, h % 2, qt:qt + 1], bank[S_BANKS[n % 2]][:, 0:(hi - lo) * P], AX.X,
                                      ALU.max, negate=h not in sunk).then_inc(a_max, 1)

                def diagonal(h):
                    dve.wait_ge(a_max, s0 + TT * (h + 1))
                    neg = rowmax
                    if h in sunk:
                        neg = negmax
                        k = heads[h]["sink"]
                        dve.tensor_scalar(negmax[:, h % 2, :], rowmax[:, h % 2, :], sink_now[:, k:k + 1], -1.0, ALU.max,
                                          ALU.mult).then_inc(a_neg, 1)
                        dve.wait_ge(a_neg, 2 * sink0 + sunk.index(h) + 1)
                    for qt in range(TT):
                        last = dve.tensor_scalar(shift[:, h % 2, qt * P:(qt + 1) * P], ident, neg[:, h % 2, qt:qt + 1],
                                                 None, ALU.mult)
                    last.then_inc(a_shift, 1)

                def low_part(h, i, kb, t, b):
                    job = heads[h]
                    nk = job["keys"](TT - 1)[1]
                    q0, q1 = q_blocks(job["keys"], kb)
                    c = slice(q0 * P, q1 * P)
                    dve.wait_ge(a_e, t0 + t + 1)
                    dve.tensor_tensor(job["st"]["pl"][:, b % nk, c], prob[b % 3][:, c],
                                      job["st"]["ph"][:, b % nk, c].bitcast(F32), ALU.subtract).then_inc(a_pl, 1)

                def output(g):
                    last = min(2 * g + 1, len(heads) - 1)
                    dve.wait_ge(a_o, h0 + last + 1)
                    if last in sunk:
                        k = sink0 + sunk.index(last) // 2 + 1
                        dve.wait_ge(a_e, t0 + max(x[3] for x in steps if x[0] == last) + 1)
                        dve.tensor_tensor(den, den, sink_e, ALU.add).then_inc(a_den, 1)
                        dve.wait_ge(a_den, k)
                    dve.reciprocal(inverse, den).then_inc(a_rec, 1)
                    dve.wait_ge(a_rec, g0 + g + 1)
                    o = put(slice(0, P), g)
                    dve.tensor_tensor(o, o, inverse, ALU.mult).then_inc(a_out, 1)

                for qt in range(TT):
                    maxes(0, qt)
                diagonal(0)
                groups = (len(heads) + 1) // 2
                ends = {last_step(steps, min(2 * g + 1, len(heads) - 1)): g for g in range(groups)}
                for x in range(len(steps) + PV_LAG + 3):
                    h, i = steps[x][:2] if x < len(steps) else (len(heads), 0)
                    if h + 1 < len(heads) and i < TT // 2:
                        maxes(h + 1, 2 * i)
                        maxes(h + 1, 2 * i + 1)
                    if h + 1 < len(heads) and i == TT // 2:
                        diagonal(h + 1)
                    if 1 <= x <= len(steps) and steps[x - 1][2] is not None:
                        low_part(*steps[x - 1])
                    if x - PV_LAG - 2 in ends:
                        output(ends[x - PV_LAG - 2])

            def value_low(i, st, b):
                dve.wait_ge(s_hi, i + 1)
                for e in range(2):
                    c = slice(2 * e * HD, (2 * e + 1) * HD)
                    last = dve.tensor_tensor(st["vl"][:, :, c],
                                             bank[b][:].rearrange("p (k n) -> p k n", k=TT)[:, :, e * HD:(e + 1) * HD],
                                             st["vh"][:, :, c].bitcast(F32), ALU.subtract)
                last.then_inc(s_lo, 1)

            def value_ones(st):
                dve.memset(st["vh"][:, :, HD:2 * HD].bitcast(F32), 1.0)
                dve.memset(st["vl"][:, :, HD:2 * HD].bitcast(F32), 0.0)

            def norm_add(ni, std_no, src, g0, x0):
                norm_recip(ni, std_no)
                dve.wait_ge(n_rec, std_no + 1)

                def add(c):
                    dve.wait_ge(n_t, ni * KC + c + 1)
                    dve.tensor_tensor(hT[:, c, :], hT[:, c, :], W[4 + c % 2], ALU.add).then_inc(x_ready, 1)
                for c in range(KC):
                    if c >= 2:
                        dve.wait_ge(x_ready, x0 + c - 1)
                    dve.scalar_tensor_tensor(out=W[4 + c % 2], in0=src[:, c, :], scalar=gain[:, g0 + c:g0 + c + 1],
                                             in1=W[2], op0=ALU.mult, op1=ALU.mult).then_inc(n_t, 1)
                    if c:
                        add(c - 1)
                add(KC - 1)

            dve.memset(gain_rows[:], 0.0).then_inc(gain_zero, 1)
            dve.wait_ge(ld_const, 16)
            dve.tensor_copy(ident_r[:], ident).then_inc(const_r, 1)
            dve.tensor_copy(ones_r[:], ones)
            dve.memset(zero_r[:].bitcast(F32), 0.0)
            dve.tensor_copy(masks_r[:], const[:, C_CAUSAL:C_CAUSAL + 3 * P].rearrange("p (m n) -> p m n", m=3)).then_inc(const_r, 1)
            dve.wait_ge(gain_t, 1)
            dve.tensor_copy(gain[:, 0:N_GAIN], bank[7][:, 0:N_GAIN]).then_inc(const_r, 1)
            dve.wait_ge(const_r, 3)
            for g, scale in ((G_FQ, HD ** -0.5), (G_DQ, HD ** -0.5), (G_QA, HD ** -0.5), (G_MQ, P ** -0.5)):
                last = dve.tensor_scalar(gain[:, g:g + 1], bank[7][:, g:g + 1], float(scale), None, ALU.mult)
            last.then_inc(gain_ready, 1)
            for c in range(KC):
                dve.wait_ge(xt_done, c + 1)
                dve.tensor_copy(hT[:, c, :], bank[c][:]).then_inc(x_ready, 1)
            dve.wait_ge(gain_ready, 1)

            norm_split(N_F1, N_F1, hT, G_F1, u_hi, u_lo)

            def angles():
                step = [0]

                def link(ins):
                    step[0] += 1
                    ins.then_inc(trig, 1)
                    dve.wait_ge(trig, step[0])
                ROUND = 12582912.0
                PI = 3.1415925
                TWO_PI = (6.28125, 0.0019350051879882812, 3.0199159819567e-07)
                a, n, m = W[2], W[3], W[4]
                dve.wait_ge(ld_pos, 16)
                link(dve.tensor_copy(a, pos_i[:]))
                link(dve.tensor_scalar(a, a, const[:, C_FREQ:C_FREQ + 1], None, ALU.mult))
                link(dve.tensor_scalar(n, a, 1.0 / 6.283185307179586, ROUND, ALU.mult, ALU.add))
                link(dve.tensor_scalar(n, n, ROUND, None, ALU.subtract))
                link(dve.tensor_scalar(m, a, 1.0 / 6.283185307179586, 0.25, ALU.mult, ALU.add))
                link(dve.tensor_scalar(m, m, ROUND, None, ALU.add))
                link(dve.tensor_scalar(m, m, ROUND, None, ALU.subtract))
                for dst_, turns, quarter in ((W[0], n, 0.0), (W[1], m, 1.5707963267948966)):
                    src = a
                    for part in TWO_PI:
                        link(dve.scalar_tensor_tensor(out=dst_, in0=turns, scalar=-part, in1=src,
                                                      op0=ALU.mult, op1=ALU.add))
                        src = dst_
                    link(dve.tensor_scalar(dst_, dst_, quarter, PI, ALU.add, ALU.min))
                    link(dve.tensor_scalar(dst_, dst_, -PI, None, ALU.max))
                assert step[0] == N_ANGLE
                dve.wait_ge(trig_a, 2)
                link(dve.tensor_scalar(sin1[:], sin1[:], const[:, C_SIGN:C_SIGN + 1], None, ALU.mult))

            ffn(0, U_GU1, half_residual, angles)

            norm_split(N_MIX, N_MIX, hT, G_MIX, u_hi, u_lo)
            dve.memset(W[6][0:HEADS], 1.0).then_inc(fg, 1)
            dve.wait_ge(r_raw, RR_PREP + 1)
            z, e = W[8][0:HEADS], W[9][0:HEADS]
            dve.tensor_scalar(z, W[7][0:HEADS], gain[0:HEADS, G_BF:G_BF + 1], None, ALU.add).then_inc(fg, 1)
            dve.wait_ge(fg, 2)
            dve.scalar_tensor_tensor(out=e, in0=z, scalar=-1.0, in1=z, op0=ALU.mult, op1=ALU.min).then_inc(fg, 1)
            head_norm(H_PREP, W[0], W[1], G_DK)
            rope(R_PREP, W[2], 6, cos1[:], sin1[:], W[4], ik[:])
            dve.wait_ge(h_out, H_PREP + 1)
            rope(R_PREP + 1, W[1], 7, cos1[:], sin1[:], W[5], dk[:])
            dve.wait_ge(fg_a, 2)
            dve.scalar_tensor_tensor(out=z, in0=z, scalar=0.0, in1=e, op0=ALU.min, op1=ALU.subtract).then_inc(fg, 1)
            dve.wait_ge(fg, 4)
            dve.tensor_tensor_scan(e, W[6][0:HEADS], z, 0.0, ALU.mult, ALU.add).then_inc(fg, 1)
            dve.wait_ge(fg, 5)
            dve.tensor_copy(c_sum[0:HEADS, :], e).then_inc(c_ready, 1)
            dve.wait_ge(c_ready, 1)
            dve.tensor_tensor(c_sum[32:32 + HEADS, :], e, c_sum[0:HEADS, :].bitcast(F32), ALU.subtract).then_inc(c_ready, 1)
            norm_split(N_MEM, N_MEM, mT, G_MEM, m_hi, m_lo, MEM)

            def mem_head(i):
                h, s = H_MEM + 2 * i, S_MEM + 3 * i
                head_norm(h, W[0], W[1], G_MQ)
                head_norm(h + 1, W[2], W[3], G_MK, MEM)
                low(s, mst["ql"][:], W[1], mst["qh"][:])
                low(s + 1, mst["kl"][:], W[3][:, 0:MEM], mst["kh"][:])
                low(s + 2, mst["vl"][:], bank[1][:, 0:MEM].rearrange("p (k n) -> p k n", k=MT), mst["vh"][:])
                attend(done_before(A_MEM, (4, 2, 2, 1, 1), i), mem_heads, lambda r, g: oT[r, 8 + i, :])
            with dve.Fori(0, 4) as i:
                mem_head(i)

            value_ones(fst)
            dve.memset(c_q[:].bitcast(F32), -1.0).then_inc(c_one, 1)
            dve.memset(c_k[:].bitcast(F32), 1.0).then_inc(c_one, 1)

            def fox_pair(i):
                h, s = H_FOX + 2 * i, S_FOX + 3 * i
                q = iq[:, bass.ds(i, 1), :].rearrange("p a n -> p (a n)")
                rope(R_IQ + i, q, 0, cos1[:], sin1[:], W[7], q)
                head_norm(h, W[0], W[1], G_FQ)
                head_norm(h + 1, W[2], W[3], G_FK)
                low(s, fst["ql"][:], W[1], fst["qh"][:])
                low(s + 1, fst["kl"][:], W[3], fst["kh"][:])
                value_low(s + 2, fst, 1)
                attend(done_before(A_FOX, (8, 8, 8, 2, 1), i), fox_heads, lambda r, g: oT[r, i, :])
            with dve.Fori(0, 4) as i:
                fox_pair(i)

            low(S_IDX, ist["kl"][:], ik[:], ist["kh"][:])

            def index_pair(i, first):
                low(S_IDX + 1 + i, ist["ql"][:], iq[:, i, :], ist["qh"][:])
                for k in range(6):
                    e, qt = k // 3, 1 + k % 3
                    n = (qt + 1) * P
                    sc, weight = score[:, qt, 0:n], iw_tok[:, qt, bass.ds(2 * i + e, 1)]
                    dve.wait_ge(ix_relu, 6 * i + k + 1)
                    if first and e == 0:
                        dve.tensor_scalar(sc, W[k % 2][:, 0:n], weight, None, ALU.mult).then_inc(ix_acc, 1)
                    else:
                        dve.wait_ge(ix_acc, 6 * i + k - 2)
                        dve.scalar_tensor_tensor(out=sc, in0=W[k % 2][:, 0:n], scalar=weight, in1=sc,
                                                 op0=ALU.mult, op1=ALU.add).then_inc(ix_acc, 1)
            index_pair(0, True)
            with dve.Fori(1, 4) as i:
                index_pair(i, False)
            dve.wait_ge(ix_acc, 24)
            for qt in range(1, TT):
                d = score[:, qt, qt * P:(qt + 1) * P]
                dve.tensor_tensor(d, d, const[:, C_CAUSAL:C_CAUSAL + P], ALU.add).then_inc(tk_rep, 1)
            dve.wait_ge(tk_rep, TT - 1)
            found = dve.alloc_register("found")
            with dve.Fori(0, TOP_ROUNDS) as r:
                for qt in range(1, TT):
                    dve.max(best8[:, qt, :], score[:, qt, 0:(qt + 1) * P]).then_inc(tk_max, 1)
                for qt in range(1, TT):
                    sc = score[:, qt, 0:(qt + 1) * P]
                    dve.reg_mov(found, (TT - 1) * r + qt)
                    dve.wait_ge(ix_acc, 24)
                    dve.wait_ge(tk_max, found)
                    dve.match_replace(sc, best8[:, qt, :], sc, TAKEN).then_inc(tk_rep, 1)
                dve.wait_ge(tk_rep, (TT - 1) * r + 2 * (TT - 1))
            for qt in range(1, TT):
                dve.tensor_scalar(topmask[:, qt, 0:(qt + 1) * P], score[:, qt, 0:(qt + 1) * P], TAKEN / 2, NEG,
                                  ALU.is_gt, ALU.mult).then_inc(tk_mask, 1)

            with dve.Fori(0, 4) as i:
                q = dq[:, bass.ds(i, 1), :].rearrange("p a n -> p (a n)")
                head_norm(H_DQ + i, W[4], q, G_DQ)
                dve.wait_ge(h_out, H_DQ + i + 1)
                rope(R_DQ + i, q, 7, cos1[:], sin1[:], W[5], q)

            low(S_DSA, dst["kl"][:], dk[:], dst["kh"][:])
            value_ones(dst)
            value_low(S_DSA + 1, dst, 1)
            with dve.Fori(0, 2) as i:
                low(S_DSA + 2 + 2 * i, dst["ql"][:], dq[:, bass.ds(2 * i, 1), :], dst["qh"][:])
                low(S_DSA + 3 + 2 * i, q_second[1][:], dq[:, bass.ds(2 * i + 1, 1), :], q_second[0][:])
                attend(done_before(A_DSA, (16, 16, 16, 4, 2), i), dsa_heads,
                       lambda r, g: oT[r, bass.ds(2 * i + 4 + g, 1), :])

            for n in range(3):
                c = slice(4 * n, 4 * n + 4)
                dve.wait_ge(o_split_hi, n + 1)
                dve.tensor_tensor(o_lo[:, c, :], oT[:, c, :], o_hi[:, c, :].bitcast(F32), ALU.subtract).then_inc(o_split, 1)

            def mixed(mp, first):
                if not first:
                    dve.wait_ge(b_lo, 2 * mp)
                for n in range(3):
                    dve.wait_ge(unit_done, U_BR + 3 * mp + n + 1)
                    for half in range(2):
                        dve.tensor_tensor(W[3 * half + n], bank[2 * n + half][:], sig[:, KC * n + 2 * mp + half, :],
                                          ALU.mult).then_inc(b_mul, 1)
                for half in range(2):
                    dve.wait_ge(b_mul, 6 * mp + 5 + half)
                    dve.tensor_tensor(W[3 * half], W[3 * half], W[3 * half + 1], ALU.add).then_inc(b_add, 1)
                for half in range(2):
                    dve.wait_ge(b_add, 4 * mp + 1 + half)
                    dve.tensor_tensor(W[3 * half], W[3 * half], W[3 * half + 2], ALU.add).then_inc(b_add, 1)
                for half in range(2):
                    dve.wait_ge(b_hi, 2 * mp + half + 1)
                    dve.tensor_tensor(mix_lo[:, 2 * mp + half, :], W[3 * half], mix_hi[:, 2 * mp + half, :].bitcast(F32),
                                      ALU.subtract).then_inc(b_lo, 1)
            mixed(0, True)
            with dve.Fori(1, 4) as mp:
                mixed(mp, False)
            for m in range(KC):
                dve.wait_ge(unit_done, U_WO + m + 1)
                dve.tensor_tensor(hT[:, m, :], bank[m % 4][:], hT[:, m, :], ALU.add).then_inc(res, 1)

            norm_split(N_F2, N_F2, hT, G_F2, u_hi, u_lo)
            ffn(1, U_GU2, half_residual)

            norm_split(N_PRE, N_PRE, hT, G_PRE2, u_hi, u_lo)
            dve.wait_ge(ld_tab, 16)
            value_ones(ast)
            value_ones(bst)

            def key_head(i):
                h, r, s = H_B2 + 3 * i, R_B2 + 6 * i, S_B2 + 8 * i
                tmp = W[8]

                def turn(k, src, b):
                    rope(r + k, src, b, tab2[:, 2 * (k % 2), :], tab2[:, 2 * (k % 2) + 1, :], tmp, rtmp[:, k, :])
                def low_of(k):
                    hi, lo = ((ast["kh"], ast["kl"]), (bst["kh"], bst["kl"]), *q2)[k]
                    dve.wait_ge(s_hi, s + k + 1)
                    if k in (3, 5):
                        dve.scalar_tensor_tensor(out=lo[:], in0=rtmp[:, k, :], scalar=float(HD ** -0.5),
                                                 in1=hi[:].bitcast(F32), op0=ALU.mult, op1=ALU.subtract).then_inc(s_lo, 1)
                    else:
                        dve.tensor_tensor(lo[:], rtmp[:, k, :], hi[:].bitcast(F32), ALU.subtract).then_inc(s_lo, 1)

                head_norm(h, W[0], W[1], G_KA)
                head_norm(h + 1, W[5], W[6], G_QA)
                dve.wait_ge(h_out, h + 1)
                turn(0, W[1], 1)
                dve.wait_ge(r_raw, RR_B2 + 3 * i + 1)
                turn(1, W[3], 6)
                low_of(0)
                head_norm(h + 2, rtmp[:, 6, :], rtmp[:, 7, :], G_QA)
                dve.wait_ge(h_out, h + 2)
                turn(2, W[6], 7)
                low_of(1)
                dve.wait_ge(r_raw, RR_B2 + 3 * i + 2)
                turn(3, W[7], 0)
                low_of(2)
                dve.wait_ge(h_out, h + 3)
                turn(4, rtmp[:, 7, :], 1)
                low_of(3)
                dve.wait_ge(r_raw, RR_B2 + 3 * i + 3)
                turn(5, rtmp[:, 8, :], 6)
                low_of(4)
                low_of(5)
                value_low(s + 6, ast, 7)
                value_low(s + 7, bst, 0)
                dve.wait_ge(a_sink, i + 1)
                attend(done_before(A_B2, (32, 36, 32, 8, 4), i), b2_heads, sink0=2 * i,
                       put=lambda r, g: o2T[r, (g % 2) * 4 + 2 * i + g // 2, :])
            with dve.Fori(0, 2) as i:
                key_head(i)

            norm_split(N_GRP, N_GRP, o2T, G_GN, u_hi, u_lo, groups=2)
            for m in range(KC):
                dve.wait_ge(unit_done, U_WO2 + m + 1)
                dve.tensor_copy(mo[:, m, :], bank[m % 4][:]).then_inc(res, 1)
            norm_add(N_POST, N_POST + 1, mo, G_POST2, KC)

            norm_split(N_FPRE, N_FPRE + 1, hT, G_FPRE2, u_hi, u_lo)

            def to_fT(m):
                dve.tensor_copy(fT[:, m, :], bank[m][:]).then_inc(f_out, 1)
            ffn(2, U_GU3, to_fT)
            norm_add(N_FPOST, N_FPOST + 1, fT, G_FPOST2, 2 * KC)
            for i in range(TT):
                dve.wait_ge(ot_done, 2 * i + 1)
                if i >= 2:
                    dve.wait_ge(stored[i % 2], 16 * (i // 2))
                dve.tensor_copy(out_tok[:, i % 2, 0:512], bank[2 * (i % 2)][:]).then_inc(o_ready_a, 1)


def constants():
    import numpy as np

    c = np.zeros((P, N_CONST), np.float32)
    i = np.arange(P)
    c[:, C_ID:C_ID + P] = np.eye(P)
    c[:, C_ONE:C_ONE + P] = 1.0
    c[:, C_BLK:C_BLK + P] = i[:, None] // HD == i[None, :] // HD
    c[i, C_ROT + (i ^ 32)] = 1.0
    c[:, C_CAUSAL:C_CAUSAL + P] = np.where(i[None, :] > i[:, None], NEG, 0.0)
    c[:, C_UP:C_UP + P] = np.where(i[None, :] > i[:, None], NEG, 0.0)
    c[:, C_LOW:C_LOW + P] = np.where(i[None, :] < i[:, None], NEG, 0.0)
    pairs = np.arange(0, HD, 2, dtype=np.float32) / np.float32(HD)
    freq = np.power(np.float32(10000.0), -pairs).astype(np.float32)
    c[:, C_FREQ] = freq[i % 32]
    sign = np.where(i % HD < 32, -1.0, 1.0).astype(np.float32)
    c[:, C_SIGN] = sign
    t = np.arange(S)
    f16 = np.power(np.float32(10000.0), -(np.arange(16, dtype=np.float32) / np.float32(16))).astype(np.float32)
    axial = np.concatenate([(t // 64).astype(np.float32)[:, None] * f16, (t % 64).astype(np.float32)[:, None] * f16], 1)
    f32 = np.power(np.float32(10000.0), -(np.arange(32, dtype=np.float32) / np.float32(32))).astype(np.float32)
    token = t.astype(np.float32)[:, None] * f32
    rope2 = np.empty((P, 4, S), np.float32)
    for k, a in enumerate((axial, token)):
        rope2[:, 2 * k] = np.cos(a).T[i % 32]
        rope2[:, 2 * k + 1] = np.sin(a).T[i % 32] * sign[:, None]
    return {"const": c, "rope2": rope2}


_INS = [
    "x", "mem", "positions", "ffn1_norm", "ffn1_w_gate", "ffn1_w_up", "ffn1_w_down", "mix_norm", "mem_norm", "w_in",
    "b_forget", "fox_q_norm", "fox_k_norm", "dsa_q_norm", "dsa_k_norm", "mem_q_norm", "mem_k_norm", "w_mem_kv",
    "w_branch", "w_out", "ffn2_norm", "ffn2_w_gate", "ffn2_w_up", "ffn2_w_down", "norm_mix_pre_2", "w_in_2",
    "q_norm_a_2", "k_norm_a_2", "sink_b_2", "group_norm_a_2", "group_norm_b_2", "w_out_2", "norm_mix_post_2",
    "norm_ffn_pre_2", "w_gate_2", "w_up_2", "w_down_2", "norm_ffn_post_2",
]


def kernel(**inputs):
    import numpy as np
    import concourse.bacc as bacc
    from concourse.bass_utils import run_bass_kernel_spmd

    nc = bacc.Bacc("TRN2", target_bir_lowering=False, num_devices=1)
    arrays, args = {}, {}
    given = {name: np.ascontiguousarray(inputs[name]) for name in _INS}
    for name, a in {**given, **constants()}.items():
        arrays[f"in_{name}"] = a
        args[name] = nc.dram_tensor(f"in_{name}", a.shape, mybir.dt.from_np(a.dtype), kind="ExternalInput").ap()
    out = nc.dram_tensor("out_0", (1, S, D), F32, kind="ExternalOutput").ap()
    two_blocks(nc, args, out)
    r = run_bass_kernel_spmd(nc, [arrays], core_ids=[0])
    return r.results[0]["out_0"]
```

```python
from contextlib import ExitStack

import concourse.bass as bass
from concourse import mybir

ALU = mybir.AluOpType
ACT = mybir.ActivationFunctionType
AX = mybir.AxisListType
F32 = mybir.dt.float32
F32R = mybir.dt.float32r
I32 = mybir.dt.int32

P = 128
D = 1024
S = 512
MEM = 256
FF = 2816
HD = 64
KC = D // P
FT = FF // P
TT = S // P
MT = MEM // P
TOPK = 128
TOP_ROUNDS = TOPK // 8
N_ANGLE = 17
EPS = 1e-6
NEG = -1e30
TAKEN = -3e38
BW = 512
HEADS = 8

SIZES = (BW, BW, BW, HEADS, BW, HD, HD, BW, HD, HEADS, BW, 3 * D)
OFF = [sum(SIZES[:i]) for i in range(len(SIZES))]
FQ, FK, FV, FG, DQ, DK, DV, IQ, IK, IW, MQ, GT = OFF
D_IN = sum(SIZES)
QA, KA, VA, QB, KB, VB = 0, 512, 640, 768, 1280, 1408
D_IN2 = 1536

(G_F1, G_MIX, G_MEM, G_F2, G_PRE2, G_GN, G_POST2, G_FPRE2, G_FPOST2) = range(0, 72, 8)
G_FQ, G_FK, G_DQ, G_DK, G_MQ, G_MK, G_QA, G_KA, G_BF = range(72, 81)
N_GAIN = 82

C_ID, C_ONE, C_BLK, C_ROT, C_CAUSAL, C_UP, C_LOW, C_FREQ, C_SIGN = (
    0, 128, 256, 384, 512, 640, 768, 896, 897)
N_CONST = 898

U_GU1 = 0
U_DN1 = U_GU1 + 2 * FT
U_PREP = U_DN1 + FT
U_MEM = U_PREP + 4
U_FOX = U_MEM + 16
U_GATE = U_FOX + 16
U_BR = U_GATE + 24
U_WO = U_BR + 12
U_GU2 = U_WO + 8
U_DN2 = U_GU2 + 2 * FT
U_B2 = U_DN2 + FT
U_WO2 = U_B2 + 16
U_GU3 = U_WO2 + 8
U_DN3 = U_GU3 + 2 * FT
N_UNITS = U_DN3 + FT
RAW = 4
SPL = 2


def two_blocks(nc, t, out):
    ctx = ExitStack()
    with ctx:
        def sem(name):
            return ctx.enter_context(nc.semaphore(name))

        top = [(nc.sbuf_base + 63) // 64 * 64]

        def at(name, shape, addr, dt=F32):
            return nc.alloc_sbuf_tensor_at(name, shape, dt, offset=addr)

        def size(shape):
            n = 4
            for s in shape[1:]:
                n *= s
            return n

        def place(name, shape, dt=F32):
            a = top[0]
            top[0] += (size(shape) + 31) // 32 * 32
            return at(name, shape, a, dt)

        raw = place("raw", [P, RAW, D])
        w_hi = place("w_hi", [P, SPL, D], F32R)
        w_lo = place("w_lo", [P, SPL, D], F32R)
        hT = place("hT", [P, KC, S])
        const = place("const", [P, N_CONST + 2])
        ident_r = place("ident_r", [P, P], F32R)
        masks_r = place("masks_r", [P, 3, P], F32R)
        gain = place("gain", [P, N_GAIN + 2])
        cos1 = place("cos1", [P, S])
        sin1 = place("sin1", [P, S])
        iw_tok = place("iw_tok", [P, TT, HEADS])
        ones_r = place("ones_r", [P, P], F32R)
        zero_r = place("zero_r", [P, P], F32R)
        rowmax = place("rowmax", [P, 2, TT])
        negmax = place("negmax", [P, 2, TT])
        sink = place("sink", [P, HEADS])
        sink_now = place("sink_now", [P, 8])
        best8 = place("best8", [P, TT, 8])
        work_at = top[0]
        work = place("work", [P, 10, S])
        W = [work[:, i, :] for i in range(10)]
        shift = at("shift", [P, 2, S], work_at + 5 * 2048, F32R)
        den, sink_e, inverse, prob = W[3], W[2], W[4], W[7:10]
        ident = const[:, C_ID:C_ID + P]
        ones = const[:, C_ONE:C_ONE + P]
        blk64 = const[:, C_BLK:C_BLK + P]
        rot = const[:, C_ROT:C_ROT + P]

        base = top[0]
        u_at = base
        u_hi = at("u_hi", [P, KC, S], u_at, F32R)
        u_lo = at("u_lo", [P, KC, S], u_at + 16384, F32R)
        o_at = u_at + 32768
        x_at = o_at + 24576
        s_at = x_at + 24576
        assert s_at + 49152 <= nc.sbuf_usable_end, (s_at + 49152, nc.sbuf_usable_end)
        a_at = o_at
        x_tok = at("x_tok", [P, TT, D], a_at)
        gain_rows = at("gain_rows", [N_GAIN, P], a_at + 16384)
        pos_i = at("pos_i", [P, S], a_at + FT * 4096, I32)
        hid_hi = at("hid_hi", [P, FT, S], a_at, F32R)
        hid_lo = at("hid_lo", [P, FT, S], a_at + FT * 2048, F32R)

        oT = at("oT", [P, 12, S], o_at)
        score = at("score", [P, TT, S], o_at + 4 * 2048)
        iq = at("iq", [P, 4, S], x_at)
        topmask = at("topmask", [P, TT, S], x_at, F32R)
        dq = at("dq", [P, 4, S], x_at + 8192)
        ik = at("ik", [P, S], x_at + 16384)
        dk = at("dk", [P, S], x_at + 18432)
        dvT = at("dvT", [P, S], x_at + 20480)
        c_sum = at("c_sum", [32 + HEADS, S], x_at + 22528, F32R)
        m_tok = at("m_tok", [P, MT, D], s_at)
        mT = at("mT", [P, KC, MEM], s_at + 8192)
        m_hi = at("m_hi", [P, KC, MEM], s_at + 16384, F32R)
        m_lo = at("m_lo", [P, KC, MEM], s_at + 24576, F32R)

        def staging(tag, a, nk, ncol, queries=True, share={}):
            kw = nk * P
            names = (("qh", [P, S]), ("ql", [P, S])) if queries else ()
            names += (("kh", [P, kw]), ("kl", [P, kw]),
                      ("vh", [P, nk, ncol]), ("vl", [P, nk, ncol]),
                      ("ph", [P, nk, S]), ("pl", [P, nk, S]))
            d = {}
            for n, shape in names:
                if n in share:
                    d[n] = share[n]
                    continue
                d[n] = at(tag + n, shape, a, F32R)
                a += size(shape)
            return d, a

        mst, e_at = staging("m_", s_at + 32768, MT, P)
        assert e_at <= s_at + 49152
        probs = {n: mst[n] for n in ("ph", "pl")}
        mst2, m_end = staging("m2_", s_at, MT, P, share=probs)
        assert m_end <= s_at + 8192
        fst, e_at = staging("f_", s_at, TT, 3 * HD)
        probs = {n: fst[n] for n in ("ph", "pl")}
        fst2, e_at = staging("f2_", e_at, TT, 3 * HD, share=probs)
        assert e_at <= s_at + 49152
        c_q = at("c_q", [36, 2, S], o_at + 8192, F32R)
        c_k = at("c_k", [36, 2, S], o_at + 8192 + 4096, F32R)
        sig = at("sig", [P, 24, S], s_at)
        i_at = s_at + 14 * 2048
        ist = {n: at("i_" + n, [P, S], i_at + 2048 * k, F32R) for k, n in enumerate(("kh", "kl"))}
        ist["qh"], ist["ql"] = (at("i_q" + n, [P, 4, S], i_at + 4096 + 8192 * k, F32R) for k, n in enumerate("hl"))
        q_later = [(at(f"d_qh{k}", [P, S], a, F32R), at(f"d_ql{k}", [P, S], b, F32R))
                   for k, a, b in ((1, work_at + 2048, work_at + 2 * 2048), (2, x_at + 16384, x_at + 20480),
                                   (3, x_at + 22528, work_at))]
        dst, e_at = staging("d_", u_at, TT, 3 * HD)
        assert e_at <= o_at
        o_hi = at("o_hi", [P, 12, S], u_at, F32R)
        o_lo = at("o_lo", [P, 12, S], x_at, F32R)
        mix_lo = at("mix_lo", [P, KC, S], u_at + 24576, F32R)
        mix_hi = at("mix_hi", [P, KC, S], u_at + 24576 + 16384, F32R)
        o2T = at("o2T", [P, KC, S], a_at)
        tab2 = at("tab2", [P, 4, S], a_at + 16384)
        b2a = a_at + 24576
        ast, b2a = staging("a_", b2a, TT, 3 * HD, queries=False)
        bst = {}
        for n, shape in (("kh", [P, S]), ("kl", [P, S]), ("vh", [P, TT, 3 * HD]), ("vl", [P, TT, 3 * HD])):
            bst[n] = at("b_" + n, shape, b2a, F32R)
            b2a += size(shape)
        bst["ph"], bst["pl"] = ast["ph"], ast["pl"]
        q2 = []
        for i in range(4):
            q2.append((at(f"q2h{i}", [P, S], b2a, F32R), at(f"q2l{i}", [P, S], b2a + 2048, F32R)))
            b2a += 4096
        rtmp = at("rtmp", [P, 9, S], b2a)
        assert b2a + 9 * 2048 <= nc.sbuf_usable_end
        fT = at("fT", [P, KC, S], u_at)
        mo = at("mo", [P, KC, S], a_at + 16384)
        out_tok = at("out_tok", [P, 2, D], a_at)

        c_dram = nc.dram_tensor("forget_sums", (2, HEADS, S), F32, kind="Internal").ap()
        bank = [ctx.enter_context(nc.psum_tensor(f"bank{i}", [P, S], F32)) for i in range(8)]

        raw_loaded = [sem(f"raw_loaded{i}") for i in range(RAW)]
        c_stored = sem("c_stored")
        part_loaded = sem("part_loaded")
        hi_done = sem("hi_done")
        split_ready = sem("split_ready")
        unit_done = sem("unit_done")
        ld_const, ld_gain, ld_x, ld_pos, ld_mem, ld_tab, ld_sink, ld_c = (
            sem(n) for n in ("ld_const", "ld_gain", "ld_x", "ld_pos", "ld_mem", "ld_tab", "ld_sink",
                             "ld_c"))
        stored = [sem("stored0"), sem("stored1")]
        gain_zero, gain_t, gain_ready, const_r, xt_done, x_ready, trig, trig_a = (
            sem(n) for n in ("gain_zero", "gain_t", "gain_ready", "const_r", "xt_done", "x_ready", "trig",
                             "trig_a"))
        n_sq, n_acc, n_std, n_rec, n_t, n_hi, n_lo = (
            sem("n_" + n) for n in ("sq", "acc", "std", "rec", "t", "hi", "lo"))
        f_gate, f_up, f_silu, f_prod, f_hi, f_lo, f_tile, f_out = (
            sem("f_" + n) for n in ("gate", "up", "silu", "prod", "hi", "lo", "tile", "out"))
        h_sq, h_raw, h_sum, h_std, h_rec, h_out = (
            sem("h_" + n) for n in ("sq", "raw", "sum", "std", "rec", "out"))
        r_raw, r_rot, r_cos, r_sin, r_out = (sem("r_" + n) for n in ("raw", "rot", "cos", "sin", "out"))
        s_hi, s_lo = sem("s_hi"), sem("s_lo")
        v_raw, v_t = sem("v_raw"), sem("v_t")
        a_s, a_max, a_neg, a_shift, a_t, a_e, a_pl, a_pv, a_o, a_den, a_rec, a_out, a_sink = (
            sem("a_" + n) for n in ("s", "max", "neg", "shift", "t", "e", "pl", "pv", "o", "den", "rec", "out", "sink"))
        iw_t, iw_ready, fg, fg_a, c_ready, c_one = (
            sem(n) for n in ("iw_t", "iw_ready", "fg", "fg_a", "c_ready", "c_one"))
        ix_s, ix_relu, ix_acc, tk_max, tk_rep, tk_mask = (
            sem(n) for n in ("ix_s", "ix_relu", "ix_acc", "tk_max", "tk_rep", "tk_mask"))
        g_sig, o_split_hi, o_split, b_mul, b_add, b_hi, b_lo, res = (
            sem(n) for n in ("g_sig", "o_split_hi", "o_split", "b_mul", "b_add", "b_hi", "b_lo", "res"))
        mt_done, m_ready, ot_done, o_ready_a, o_ready_b = (
            sem(n) for n in ("mt_done", "m_ready", "ot_done", "o_ready_a", "o_ready_b"))

        block = ctx.enter_context(nc.Block())

        def cols(w, a, n=P):
            return w.rearrange("(c p) n -> p c n", p=P)[:, :, bass.ds(a, n)]

        def raw_as(slot, c):
            return raw[:, slot, :].rearrange("p (c n) -> p c n", c=c)

        BRANCH_ORDER = 0, 2, 1

        @block.sync
        def _(sp):
            wait_value = sp.alloc_register("wait_value")

            def value(v):
                if isinstance(v, int):
                    return v
                sp.reg_mov(wait_value, v)
                return wait_value

            def unit(u, slot, dst, src):
                if not (isinstance(u, int) and u < RAW):
                    free = value(u - RAW + 1)
                    sp.wait_ge(split_ready, 1)
                    sp.wait_ge(split_ready, free)
                sp.dma_start(dst, src).then_inc(raw_loaded[slot], 16)

            def panel(u, slot, w, a):
                unit(u, slot, raw_as(slot, KC), cols(w, a))

            def halves(u, slot, w, one, two, n):
                dst = raw_as(slot, KC)
                free = value(u - RAW + 1)
                sp.wait_ge(split_ready, 1)
                sp.wait_ge(split_ready, free)
                sp.dma_start(dst[:, :, one[0]:one[0] + n], cols(w, one[1], n)).then_inc(part_loaded, 16)
                first = value(16 * (part_count(u) + 1))
                sp.wait_ge(split_ready, 1)
                sp.wait_ge(part_loaded, first)
                sp.dma_start(dst[:, :, two[0]:two[0] + n], cols(w, two[1], n)).then_inc(raw_loaded[slot], 16)

            def twice(u, slot, w, a):
                halves(u, slot, w, (0, a), (HD, a), HD)

            def ffn(u0, gate, up, down):
                def four(i):
                    for k in range(4):
                        panel(u0 + 4 * i + k, (u0 + k) % RAW, (gate, up)[k % 2], (2 * i + k // 2) * P)
                start = 0
                if u0 == 0:
                    four(0)
                    start = 1
                with sp.Fori(start, FT // 2) as i:
                    four(i)
                d0 = u0 + 2 * FT

                def rows(j, k):
                    slot = (d0 + k) % RAW
                    unit(d0 + j, slot, raw[:, slot, :], down[bass.ds(j * P, P), :])
                with sp.Fori(0, FT // 4) as i:
                    for k in range(4):
                        rows(4 * i + k, k)
                for k in range(FT % 4):
                    rows(FT // 4 * 4 + k, k)

            def part_count(u):
                if isinstance(u, int):
                    return u - U_PREP
                return parts_before[0]

            parts_before = [0]
            sp.wait_ge(ld_x, 16)
            ffn(U_GU1, t["ffn1_w_gate"][0], t["ffn1_w_up"][0], t["ffn1_w_down"][0])
            w_in = t["w_in"][0]
            slot = U_PREP % RAW
            halves(U_PREP, slot, w_in, (0, FG), (32, IW), HEADS)
            for k, a in enumerate((IK, DK, DV)):
                twice(U_PREP + 1 + k, (U_PREP + 1 + k) % RAW, w_in, a)
            kv = t["w_mem_kv"][0]
            with sp.Fori(0, 4) as i:
                for k, (w, a) in enumerate(((w_in, MQ), (kv, 0), (kv, BW), (w_in, IQ))):
                    panel(U_MEM + 4 * i + k, (U_MEM + k) % RAW, w, a + i * P)
            with sp.Fori(0, 4) as i:
                for k, a in enumerate((FQ, FK, FV, DQ)):
                    panel(U_FOX + 4 * i + k, (U_FOX + k) % RAW, w_in, a + i * P)
            with sp.Fori(0, 6) as i:
                for k in range(4):
                    panel(U_GATE + 4 * i + k, (U_GATE + k) % RAW, w_in, GT + (4 * i + k) * P)
            for mp in range(4):
                for place, n in enumerate(BRANCH_ORDER):
                    k = 3 * mp + place
                    slot = (U_BR + k) % RAW
                    unit(U_BR + k, slot, raw_as(slot, 4), cols(t["w_branch"][0, n], mp * 2 * P, 2 * P))

            def w_out(u0, w):
                with sp.Fori(0, 2) as i:
                    for k in range(4):
                        panel(u0 + 4 * i + k, (u0 + k) % RAW, w, (4 * i + k) * P)
            w_out(U_WO, t["w_out"][0])
            ffn(U_GU2, t["ffn2_w_gate"][0], t["ffn2_w_up"][0], t["ffn2_w_down"][0])
            w2 = t["w_in_2"][0]
            with sp.Fori(0, 2) as i:
                u = U_B2 + 8 * i
                for k, (a, key, nth) in enumerate(((KA, True, 0), (QA, False, 0), (QA + P, False, 0), (KB, True, 1),
                                                   (QB, False, 0), (QB + P, False, 0), (VA, True, 2), (VB, True, 3))):
                    slot = (U_B2 + k) % RAW
                    if key:
                        parts_before[0] = 4 + 4 * i + nth
                        twice(u + k, slot, w2, a + i * HD)
                    else:
                        panel(u + k, slot, w2, a + i * 2 * P)
            w_out(U_WO2, t["w_out_2"][0])
            ffn(U_GU3, t["w_gate_2"][0], t["w_up_2"][0], t["w_down_2"][0])
            for i in range(TT):
                sp.wait_ge(o_ready_a, i + 1)
                sp.wait_ge(o_ready_b, i + 1)
                sp.dma_start(out[0, i * P:(i + 1) * P, :], out_tok[:, i % 2, :]).then_inc(stored[i % 2], 16)
            for s in stored:
                sp.wait_ge(s, 16 * TT // 2)

        @block.gpsimd
        def _(pool):
            loaded_value, used_value = pool.alloc_register("loaded_value"), pool.alloc_register("used_value")

            def value(reg, v):
                if isinstance(v, int):
                    return v
                pool.reg_mov(reg, v)
                return reg

            def split(u, i, k):
                first = isinstance(u, int) and u < SPL
                loaded = value(loaded_value, 16 * (i + 1))
                used = value(used_value, u - SPL + 1)
                pool.wait_ge(raw_loaded[k], 16)
                pool.wait_ge(raw_loaded[k], loaded)
                if not first:
                    pool.wait_ge(unit_done, used)
                s = k % SPL
                pool.tensor_scalar(w_hi[:, s, :], raw[:, k, :], 1.0, 1.0, ALU.mult, ALU.mult).then_inc(hi_done, 1)
                pool.wait_ge(hi_done, u + 1)
                pool.tensor_tensor(w_lo[:, s, :], raw[:, k, :], w_hi[:, s, :].bitcast(F32),
                                   ALU.subtract).then_inc(split_ready, 1)
            for k in range(RAW):
                split(k, 0, k)
            with pool.Fori(1, N_UNITS // RAW) as i:
                for k in range(RAW):
                    split(4 * i + k, i, k)
            for k in range(N_UNITS % RAW):
                split(N_UNITS // RAW * RAW + k, N_UNITS // RAW, k)

        N_F1, N_MIX, N_MEM, N_F2, N_PRE, N_GRP, N_POST, N_FPRE, N_FPOST = range(9)
        SCALED = {N_MIX: 0, N_MEM: 1, N_PRE: 2, N_GRP: 3, N_POST: 4, N_FPOST: 5}
        SPLITS = {N_F1: 0, N_MIX: 1, N_MEM: 2, N_F2: 3, N_PRE: 4, N_GRP: 5, N_FPRE: 6}
        H_PREP, H_MEM, H_FOX, H_DQ, H_B2 = 0, 1, 9, 17, 21
        R_PREP, R_IQ, R_DQ, R_B2 = 0, 2, 6, 10
        RR_PREP, RR_MEM, RR_FOX, RR_B2 = 0, 2, 6, 10
        S_MEM, S_FOX, S_IDX, S_DSA, S_B2 = 0, 12, 24, 29, 35
        VR_PREP, VR_MEM, VR_FOX, VR_B2 = 0, 1, 5, 9
        VT_MEM, VT_FOX, VT_DSA, VT_B2 = 0, 4, 8, 9
        A_MEM, A_FOX, A_DSA, A_B2 = (0, 0, 0, 0, 0), (16, 8, 8, 4, 4), (48, 40, 40, 12, 8), (80, 72, 72, 20, 12)

        def done_before(base, per, i):
            return tuple(a + b * i for a, b in zip(base, per))

        def causal(qt):
            return 0, qt + 1

        def window(qt):
            return max(0, qt - 1), min(TT, qt + 2)

        def whole(qt):
            return 0, TT

        def memory(qt):
            return 0, MT

        def q_blocks(keys, kb):
            q = [i for i in range(TT) if keys(i)[0] <= kb < keys(i)[1]]
            return q[0], q[-1] + 1

        def pair(st, keys, q=None, extra=None, extra_t=None, sinks=None):
            r = (slice(0, HD), slice(HD, P))
            return [{"st": st, "keys": keys, "q": q or (st["qh"], st["ql"]), "rows": r[e], "den": r[1 - e],
                     "v": slice(e * HD, e * HD + P), "e": e, "extra": extra, "extra_t": extra_t,
                     "sink": sinks + e if sinks is not None else None} for e in range(2)]

        def group(heads):
            return 1 if heads[0]["den"] is None else 2

        def steps_of(heads):
            steps = []
            n = 0
            for h, job in enumerate(heads):
                nk = job["keys"](TT - 1)[1]
                for kb in range(nk):
                    steps.append((h, kb, kb, len(steps), n))
                    n += 1
                if job["sink"] is not None:
                    steps.append((h, nk, None, len(steps), n))
            return steps

        def last_step(steps, h):
            return max(x[3] for x in steps if x[0] == h and x[2] is not None)

        def last_block(steps, h):
            return max(x[4] for x in steps if x[0] == h and x[2] is not None) + 1

        def fox_extra(k, e, qt, lo, hi):
            return [(ident_r[:], masks_r[:, 0, :], qt * P, (qt + 1) * P),
                    (c_q[32 * k:32 * k + 4, e, qt * P:(qt + 1) * P], c_k[32 * k:32 * k + 4, e, lo * P:hi * P], 0, (hi - lo) * P)]

        def fox_extra_t(k, e, kb, q0, q1):
            return [(c_k[32 * k:32 * k + 4, e, kb * P:(kb + 1) * P], c_q[32 * k:32 * k + 4, e, q0 * P:q1 * P], 0, (q1 - q0) * P),
                    (masks_r[:, 0, :], ident_r[:], 0, P)]

        def dsa_extra(e, qt, lo, hi):
            if qt == 0:
                return [(ident_r[:], masks_r[:, 0, :], 0, P)]
            return [(ident_r[:], topmask[:, qt, 0:hi * P], 0, hi * P)]

        def dsa_extra_t(e, kb, q0, q1):
            return [(topmask[:, qt, kb * P:(kb + 1) * P] if qt else masks_r[:, 0, :], ident_r[:],
                     (qt - q0) * P, (qt - q0 + 1) * P) for qt in range(q0, q1)]

        def band(q, e, qt, lo, hi):
            m = []
            if lo < qt:
                m.append((ident_r[:], masks_r[:, 2, :], 0, P))
            if hi > qt + 1:
                m.append((ident_r[:], masks_r[:, 1, :], (qt + 1 - lo) * P, (qt + 2 - lo) * P))
            r = slice(e * HD, (e + 1) * HD)
            return m + [(q[r, qt * P:(qt + 1) * P], bst["kl"][r, lo * P:hi * P], 0, (hi - lo) * P)]

        def band_t(e, kb, q0, q1):
            m = []
            if kb > q0:
                m.append((masks_r[:, 1, :], ident_r[:], 0, P))
            if kb < q1 - 1:
                m.append((masks_r[:, 2, :], ident_r[:], (kb + 1 - q0) * P, (kb + 2 - q0) * P))
            return m

        mem_heads = [{"st": st, "keys": memory, "q": (st["qh"], st["ql"]), "rows": slice(0, P), "den": None,
                      "v": slice(0, P), "e": 0, "extra": None, "extra_t": None, "sink": None} for st in (mst, mst2)]
        fox_heads = []
        for k, st in enumerate((fst, fst2)):
            fox_heads += pair(st, causal, extra=lambda *a, k=k: fox_extra(k, *a),
                              extra_t=lambda *a, k=k: fox_extra_t(k, *a))
        dsa_heads = []
        for k in range(4):
            dsa_heads += pair(dst, causal, q=q_later[k - 1] if k else None, extra=dsa_extra, extra_t=dsa_extra_t)
        b2_heads = []
        for k in range(2):
            b2_heads += pair(ast, whole, q=q2[2 * k])
            b2_heads += pair(bst, window, q=q2[2 * k + 1], extra=lambda *a, k=k: band(q2[2 * k + 1][0], *a),
                             extra_t=band_t, sinks=2 * k)
        S_BANKS, T_BANKS, O_BANKS, DEN_BANK = (0, 1), (2, 3, 4), (6, 7), 5
        SUM_BANK = 4
        I_BANKS = 0, 1, 6
        PV_LAG = 2

        @block.tensor
        def _(pe):
            def unit_mm(u, outs, rhs_hi, rhs_lo, n=S, per=None, before=None):
                slot = per[0] if per else 0
                pe.wait_ge(split_ready, u + 1)
                for c in range(KC):
                    if before:
                        before(c)
                    wh = w_hi[:, slot, c * P:(c + 1) * P]
                    wl = w_lo[:, slot, c * P:(c + 1) * P]
                    pe.matmul(outs[:, 0:n], wh, rhs_hi[:, c, :], start=(c == 0), stop=False)
                    pe.matmul(outs[:, 0:n], wh, rhs_lo[:, c, :], start=False, stop=False)
                    last = pe.matmul(outs[:, 0:n], wl, rhs_hi[:, c, :], start=False, stop=(c == KC - 1))
                last.then_inc(unit_done, 1)

            def panel(u, slot, b, rhs, before=None):
                unit_mm(u, bank[b], rhs[0], rhs[1], per=(slot,), before=before)

            def amid(c0, *steps):
                def before(c):
                    if c == c0:
                        for step in steps:
                            step()
                return before

            U = (u_hi, u_lo)

            def sum_chunk(ni, c, b, n=S, per=KC):
                pe.wait_ge(n_sq, ni * KC + c + 1)
                pe.matmul(bank[b][:, 0:n], ones, W[c % 2][:, 0:n], start=(c % per == 0),
                          stop=(c % per == per - 1)).then_inc(n_acc, 1)

            def norm_sum(ni, n=S, groups=1):
                per = KC // groups
                for c in range(KC):
                    sum_chunk(ni, c, c // per, n, per)

            def norm_wait(ni):
                def before(c):
                    pe.wait_ge(n_lo, SPLITS[ni] * KC + c + 1)
                return before

            def ffn(fi, u0, ni):
                def two(it, first):
                    for k in range(2):
                        f = 2 * it + k
                        u = u0 + 4 * it + 2 * k
                        if not first:
                            pe.wait_ge(f_gate, fi * FT + f - 1)
                        panel(u, 0, 2 * k, U, norm_wait(ni) if first and k == 0 else None)
                        if not first:
                            pe.wait_ge(f_up, fi * FT + f - 1)
                        panel(u + 1, 1, 2 * k + 1, U, (lambda c: sum_chunk(ni, c, SUM_BANK)) if first and k == 0 else None)
                two(0, True)
                with pe.Fori(1, FT // 2) as it:
                    two(it, False)
                d0 = u0 + 2 * FT

                def down(j, slot, start, stop):
                    pe.wait_ge(split_ready, d0 + j + 1)
                    pe.wait_ge(f_lo, fi * FT + j + 1)
                    for m in (4, 5, 6, 7, 0, 1, 2, 3):
                        if start and m == 0:
                            pe.wait_ge(f_up, fi * FT + FT)
                        wh = w_hi[:, slot, m * P:(m + 1) * P]
                        wl = w_lo[:, slot, m * P:(m + 1) * P]
                        pe.matmul(bank[m][:], wh, hid_hi[:, j, :], start=start, stop=False)
                        pe.matmul(bank[m][:], wh, hid_lo[:, j, :], start=False, stop=False)
                        last = pe.matmul(bank[m][:], wl, hid_hi[:, j, :], start=False, stop=stop)
                    last.then_inc(unit_done, 1)
                down(0, 0, True, False)
                down(1, 1, False, False)
                with pe.Fori(1, FT // 2 - 1) as it:
                    for k in range(2):
                        down(2 * it + k, k, False, False)
                pe.wait_ge(split_ready, d0 + FT - 1)
                pe.wait_ge(f_lo, fi * FT + FT - 1)
                order = [(m, 0) for m in range(4, KC)] + [(m, k) for m in range(4) for k in range(2)]
                order += [(m, 1) for m in range(4, KC)]
                for m, k in order:
                    if (m, k) == (0, 1):
                        pe.wait_ge(split_ready, d0 + FT)
                        pe.wait_ge(f_lo, fi * FT + FT)
                    j = FT - 2 + k
                    wh = w_hi[:, k, m * P:(m + 1) * P]
                    wl = w_lo[:, k, m * P:(m + 1) * P]
                    pe.matmul(bank[m][:], wh, hid_hi[:, j, :], start=False, stop=False)
                    pe.matmul(bank[m][:], wh, hid_lo[:, j, :], start=False, stop=False)
                    last = pe.matmul(bank[m][:], wl, hid_hi[:, j, :], start=False, stop=k == 1)
                    if (m, k) == (3, 0) or (m, k) == (KC - 1, 1):
                        last.then_inc(unit_done, 1)
                    elif k:
                        last.then_inc(f_tile, 1)

            def head_sum(i, b, sq, m, n=S):
                pe.wait_ge(h_sq, i + 1)
                pe.matmul(bank[b][:, 0:n], m, sq[:, 0:n], start=True, stop=True).then_inc(h_sum, 1)

            def rotate(b, src):
                pe.matmul(bank[b][:], rot, src, start=True, stop=True).then_inc(r_rot, 1)

            def values(i_raw, b, src, n=TT):
                pe.wait_ge(v_raw, i_raw + 1)
                for kb in range(n):
                    last = pe.transpose(bank[b][:, kb * P:(kb + 1) * P], src[:, kb * P:(kb + 1) * P], ident)
                last.then_inc(v_t, 1)

            def attend(done, heads):
                s0, t0, b0, h0 = done[:4]
                steps = steps_of(heads)

                def scores(h, qt):
                    job = heads[h]
                    n = h * TT + qt
                    lo, hi = job["keys"](qt)
                    o = bank[S_BANKS[n % 2]]
                    if n >= 2:
                        pe.wait_ge(a_max, s0 + n - 1)
                    r, q, k = job["rows"], slice(qt * P, (qt + 1) * P), slice(lo * P, hi * P)
                    sums = [(job["q"][0][r, q], job["st"]["kh"][r, k], 0, (hi - lo) * P)]
                    if job["extra"]:
                        sums += job["extra"](job["e"], qt, lo, hi)
                    for i, (lhs, rhs, c0, c1) in enumerate(sums):
                        last = pe.matmul(o[:, c0:c1], lhs, rhs, start=i == 0, stop=i == len(sums) - 1)
                    last.then_inc(a_s, 1)

                def scores_t(h, i, kb, t):
                    job = heads[h]
                    q0, q1 = q_blocks(job["keys"], kb) if kb is not None else (0, TT)
                    n = (q1 - q0) * P
                    o = bank[T_BANKS[t % 3]][:, 0:n]
                    if t >= 3:
                        pe.wait_ge(a_e, t0 + t - 2)
                    if kb is not None:
                        r, k, q = job["rows"], slice(kb * P, (kb + 1) * P), slice(q0 * P, q1 * P)
                        (qh, ql), kh, kl = job["q"], job["st"]["kh"], job["st"]["kl"]
                        pe.matmul(o, kh[r, k], qh[r, q], start=True, stop=False)
                        if job["extra_t"]:
                            for lhs, rhs, c0, c1 in job["extra_t"](job["e"], kb, q0, q1):
                                pe.matmul(bank[T_BANKS[t % 3]][:, c0:c1], lhs, rhs, start=False, stop=False)
                        pe.matmul(o, kh[r, k], ql[r, q], start=False, stop=False)
                        pe.matmul(o, kl[r, k], qh[r, q], start=False, stop=False)
                    if i == 0:
                        pe.wait_ge(a_shift, h0 + h + 1)
                    pe.matmul(o, ones_r[:], shift[:, h % 2, q0 * P:q1 * P], start=kb is None, stop=True).then_inc(a_t, 1)

                def values_mm(h, i, kb, b):
                    job = heads[h]
                    st, keys = job["st"], job["keys"]
                    nk = keys(TT - 1)[1]
                    q0, q1 = q_blocks(keys, kb)
                    c = slice(q0 * P, q1 * P)
                    o = bank[O_BANKS[h % 2]]
                    if kb == 0 and h >= 2:
                        pe.wait_ge(a_o, h0 + h - 1)
                    pe.wait_ge(a_pl, b0 + b + 1)
                    slot = b % nk
                    ph, pl = st["ph"][:, slot, c], st["pl"][:, slot, c]
                    vh, vl = st["vh"][:, kb, job["v"]], st["vl"][:, kb, job["v"]]
                    ragged_first, ragged_last = kb == 0 and q1 < TT, kb == nk - 1 and q0 > 0
                    if ragged_first:
                        pe.matmul(o[:], zero_r[:], st["kh"][:], start=True, stop=False)
                    pe.matmul(o[:, c], vh, ph, start=kb == 0 and not ragged_first, stop=False)
                    pe.matmul(o[:, c], vh, pl, start=False, stop=False)
                    last = pe.matmul(o[:, c], vl, ph, start=False, stop=kb == nk - 1 and not ragged_last)
                    if ragged_last:
                        last = pe.matmul(o[:], zero_r[:], st["kh"][:], start=False, stop=True)
                    if job["den"] is None:
                        if kb == 0 and h:
                            pe.wait_ge(a_o, h0 + h)
                        pe.matmul(bank[DEN_BANK][:], ones_r[:], ph, start=kb == 0, stop=False)
                        last = pe.matmul(bank[DEN_BANK][:], ones_r[:], pl, start=False, stop=kb == nk - 1)
                    last.then_inc(a_pv, 1)

                for qt in range(TT):
                    scores(0, qt)
                for x, (h, i, kb, t, b) in enumerate(steps):
                    scores_t(h, i, kb, t)
                    if h + 1 < len(heads) and i < TT // 2:
                        scores(h + 1, 2 * i)
                        scores(h + 1, 2 * i + 1)
                    if x >= PV_LAG and steps[x - PV_LAG][2] is not None:
                        h_, i_, kb_, t_, b_ = steps[x - PV_LAG]
                        values_mm(h_, i_, kb_, b_)
                for h, i, kb, t, b in steps[-PV_LAG:]:
                    if kb is not None:
                        values_mm(h, i, kb, b)

            pe.wait_ge(ld_const, 16)
            pe.wait_ge(ld_x, 16)
            for c in range(KC):
                for i in range(TT):
                    last = pe.transpose(bank[c][:, i * P:(i + 1) * P], x_tok[:, i, c * P:(c + 1) * P], ident)
                last.then_inc(xt_done, 1)
            pe.wait_ge(x_ready, KC)

            pe.wait_ge(ld_gain, 16 * 25)
            pe.transpose(bank[1][:, 0:N_GAIN], gain_rows[:, :], ident[0:N_GAIN, 0:N_GAIN]).then_inc(gain_t, 1)
            pe.wait_ge(gain_ready, 1)
            ffn(0, U_GU1, N_F1)

            norm_sum(N_MIX)
            for k in range(4):
                pe.wait_ge(n_std, N_MIX + 1)
                panel(U_PREP + k, k % SPL, k, U, norm_wait(N_MIX) if k == 0 else None)
            head_sum(H_PREP, 4, W[0], blk64)
            pe.wait_ge(r_raw, RR_PREP + 2)
            rotate(6, W[2])
            for i in range(TT):
                last = pe.transpose(bank[5][:, i * HD:(i + 1) * HD], W[7][0:HD, i * P:(i + 1) * P], ident[0:HD, 0:HD])
            last.then_inc(iw_t, 1)
            pe.wait_ge(h_out, H_PREP + 1)
            rotate(7, W[1])
            pe.wait_ge(ld_mem, 16)
            pe.wait_ge(r_out, R_PREP + 2)
            pe.wait_ge(iw_ready, 1)
            pe.wait_ge(v_raw, VR_PREP + 1)
            for c in range(KC):
                for i in range(MT):
                    last = pe.transpose(bank[c][:, i * P:(i + 1) * P], m_tok[:, i, c * P:(c + 1) * P], ident)
                last.then_inc(mt_done, 1)
            pe.wait_ge(m_ready, KC)
            norm_sum(N_MEM, MEM)
            pe.wait_ge(n_std, N_MEM + 1)

            def mem_head(i, second, first):
                u, h = U_MEM + 4 * i, H_MEM + 2 * i
                panel(u, 0, 2, U)

                def sum_q():
                    if second:
                        pe.wait_ge(h_std, h - 1)
                    head_sum(h, 6, W[0], ones)

                def km_hook(c):
                    if first:
                        norm_wait(N_MEM)(c)
                    if c == 5:
                        sum_q()
                unit_mm(u + 1, bank[3], m_hi, m_lo, n=MEM, per=(1,), before=km_hook)

                def sum_k():
                    if second:
                        pe.wait_ge(h_std, h)
                    head_sum(h + 1, 7, W[2], ones, MEM)
                unit_mm(u + 2, bank[4], m_hi, m_lo, n=MEM, per=(0,), before=amid(6, sum_k))
                if second:
                    pe.wait_ge(r_raw, RR_MEM + i)

                def v():
                    if second:
                        pe.wait_ge(s_lo, S_MEM + 3 * i)
                    values(VR_MEM + i, 1, W[4], MT)
                panel(u + 3, 1, 5, U, amid(3, v))

            def mem_pair(i, first):
                if not first:
                    pe.wait_ge(a_o, 2 * i)
                mem_head(2 * i, False, first)
                mem_head(2 * i + 1, True, False)
                pe.wait_ge(r_raw, RR_MEM + 2 * i + 2)
                pe.wait_ge(s_lo, S_MEM + 6 * i + 6)
                attend(done_before(A_MEM, (8, 4, 4, 2, 2), i), mem_heads)
            mem_pair(0, True)
            with pe.Fori(1, 2) as i:
                mem_pair(i, False)

            def fox_pair(i, second):
                u, h = U_FOX + 4 * i, H_FOX + 2 * i
                if second:
                    pe.wait_ge(r_out, R_IQ + i)
                rotate(0, iq[:, bass.ds(i, 1), :].rearrange("p a n -> p (a n)"))
                panel(u, 0, 2, U)

                def sum_q():
                    if second:
                        pe.wait_ge(h_std, h - 1)
                    head_sum(h, 6, W[0], blk64)
                panel(u + 1, 1, 3, U, amid(3, sum_q))

                def sum_k():
                    if second:
                        pe.wait_ge(h_std, h)
                    head_sum(h + 1, 7, W[2], blk64)
                panel(u + 2, 0, 4, U, amid(3, sum_k))
                if second:
                    pe.wait_ge(r_raw, RR_FOX + i)

                def v():
                    if second:
                        pe.wait_ge(s_lo, S_FOX + 3 * i)
                    values(VR_FOX + i, 1, W[6])
                panel(u + 3, 1, 5, U, amid(3, v))

            with pe.Fori(0, 2) as i:
                pe.wait_ge(a_o, A_FOX[3] + 4 * i)
                fox_pair(2 * i, False)
                fox_pair(2 * i + 1, True)
                pe.wait_ge(s_lo, S_FOX + 6 * i + 6)
                pe.wait_ge(ld_c, 64 * (i + 1))
                pe.wait_ge(r_out, R_IQ + 2 * i + 2)
                attend(done_before(A_FOX, (16, 16, 16, 4, 2), i), fox_heads)

            def gates(i, first, hooks=(None,) * 4):
                for k in range(4):
                    if not first:
                        pe.wait_ge(g_sig, 4 * i + k - 3)
                    panel(U_GATE + 4 * i + k, k % SPL, 2 + k, U, hooks[k])

            def index_score(head, qt):
                i, e = head // 2, head % 2
                if e == 0 and qt == 1:
                    pe.wait_ge(s_lo, S_IDX + 2 + i)
                n = 3 * head + qt - 1
                if n >= 3:
                    pe.wait_ge(ix_relu, n - 2)
                b = bank[I_BANKS[n % 3]][:, 0:(qt + 1) * P]
                r, q, k = slice(e * HD, (e + 1) * HD), slice(qt * P, (qt + 1) * P), slice(0, (qt + 1) * P)
                pe.matmul(b, ist["qh"][r, i, q], ist["kh"][r, k], start=True, stop=False)
                pe.matmul(b, ist["qh"][r, i, q], ist["kl"][r, k], start=False, stop=False)
                pe.matmul(b, ist["ql"][r, i, q], ist["kh"][r, k], start=False, stop=True).then_inc(ix_s, 1)

            def index_head(head):
                def before(c):
                    if c >= KC + 1 - TT:
                        index_score(head, c - (KC - TT))
                return before
            pe.wait_ge(a_o, A_DSA[3])
            gates(0, True, [index_head(k) for k in range(4)])
            gates(1, False, [index_head(4 + k) for k in range(4)])
            with pe.Fori(2, 6) as i:
                gates(i, False, (None, amid(3, lambda: head_sum(H_DQ + i - 2, 6, W[4], blk64)), None, None))
                pe.wait_ge(h_out, H_DQ + i - 1)
                pe.wait_ge(r_out, R_DQ + i - 2)
                rotate(7, dq[:, bass.ds(i - 2, 1), :].rearrange("p a n -> p (a n)"))

            pe.wait_ge(ix_relu, 24)
            pe.wait_ge(g_sig, 24)
            values(VR_PREP, 1, dvT)
            pe.wait_ge(tk_mask, 3)

            pe.wait_ge(s_lo, S_DSA + 6)
            attend(A_DSA, dsa_heads)

            pe.wait_ge(a_o, A_B2[3])

            def branches(it, first):
                for kk in range(6):
                    k = 6 * it + kk
                    n = BRANCH_ORDER[kk % 3]
                    slot = kk % SPL
                    if not first or kk >= 3:
                        pe.wait_ge(b_mul, 2 * k - 4)
                    pe.wait_ge(split_ready, U_BR + k + 1)
                    if first and kk < 3:
                        pe.wait_ge(o_split, kk + 1)
                    for half in range(2):
                        o = bank[2 * n + half][:]
                        for c in range(4):
                            a = c * 2 * P + half * P
                            oc = 4 * n + c
                            pe.matmul(o, w_hi[:, slot, a:a + P], o_hi[:, oc, :], start=(c == 0), stop=False)
                            pe.matmul(o, w_hi[:, slot, a:a + P], o_lo[:, oc, :], start=False, stop=False)
                            last = pe.matmul(o, w_lo[:, slot, a:a + P], o_hi[:, oc, :], start=False, stop=(c == 3))
                    last.then_inc(unit_done, 1)
            branches(0, True)
            with pe.Fori(1, 2) as it:
                branches(it, False)

            def w_out(u0, rhs, r0, before=None, later=None):
                for i in range(2):
                    for k in range(4):
                        if i:
                            pe.wait_ge(res, r0 + k + 1)
                        m = 4 * i + k
                        panel(u0 + m, k % SPL, k, rhs, before if m == 0 else later(m) if later else None)
            pe.wait_ge(b_mul, 24)
            w_out(U_WO, (mix_hi, mix_lo), 0, lambda c: pe.wait_ge(b_lo, c + 1))

            pe.wait_ge(res, KC)
            ffn(1, U_GU2, N_F2)

            norm_sum(N_PRE)
            pe.wait_ge(n_std, N_PRE + 1)

            def key_head(i, first):
                u = U_B2 + 8 * i
                h, r, rr, s, vr = H_B2 + 3 * i, R_B2 + 6 * i, RR_B2 + 3 * i, S_B2 + 8 * i, VR_B2 + 2 * i
                pe.wait_ge(a_o, A_B2[3] + 8 * i)
                panel(u, 0, 2, U, norm_wait(N_PRE) if first else None)
                panel(u + 1, 1, 3, U, amid(3, lambda: head_sum(h, 6, W[0], blk64)))
                panel(u + 2, 0, 4, U, amid(3, lambda: head_sum(h + 1, 7, W[5], blk64)))

                def turn_ka():
                    pe.wait_ge(h_out, h + 1)
                    rotate(1, W[1])
                panel(u + 3, 1, 5, U, amid(3, lambda: head_sum(h + 2, 0, rtmp[:, 6, :], blk64), turn_ka))

                def turn_kb():
                    pe.wait_ge(r_raw, rr + 1)
                    rotate(6, W[3])
                panel(u + 4, 0, 2, U, amid(3, turn_kb))

                def turn_qa():
                    pe.wait_ge(h_out, h + 2)
                    rotate(7, W[6])
                panel(u + 5, 1, 3, U, amid(3, turn_qa))

                def turn_qb():
                    pe.wait_ge(h_std, h + 3)
                    pe.wait_ge(r_raw, rr + 2)
                    rotate(0, W[7])
                panel(u + 6, 0, 4, U, amid(3, turn_qb))

                def turn_second():
                    pe.wait_ge(h_out, h + 3)
                    pe.wait_ge(r_out, r + 1)
                    rotate(1, rtmp[:, 7, :])
                    pe.wait_ge(r_raw, rr + 3)
                    pe.wait_ge(r_out, r + 2)
                    rotate(6, rtmp[:, 8, :])
                panel(u + 7, 1, 5, U, amid(4, turn_second))
                pe.wait_ge(r_out, r + 4)
                values(vr, 7, W[2])
                values(vr + 1, 0, W[4])
                pe.wait_ge(s_lo, s + 8)
                attend(done_before(A_B2, (32, 36, 32, 8, 4), i), b2_heads)
            key_head(0, True)
            with pe.Fori(1, 2) as i:
                key_head(i, False)

            pe.wait_ge(a_o, A_B2[3] + 16)
            norm_sum(N_GRP, groups=2)
            pe.wait_ge(n_std, N_GRP + 2)
            w_out(U_WO2, U, 8, norm_wait(N_GRP), lambda m: amid(4, lambda: sum_chunk(N_POST, m - 1, SUM_BANK)))
            sum_chunk(N_POST, KC - 1, SUM_BANK)
            pe.wait_ge(n_std, N_POST + 2)

            ffn(2, U_GU3, N_FPRE)
            norm_sum(N_FPOST)
            pe.wait_ge(n_std, N_FPOST + 2)
            pe.wait_ge(x_ready, 3 * KC)
            for i in range(TT):
                if i >= 2:
                    pe.wait_ge(o_ready_a, i - 1)
                    pe.wait_ge(o_ready_b, i - 1)
                for half in range(2):
                    for c in range(4):
                        last = pe.transpose(bank[2 * (i % 2) + half][:, c * P:(c + 1) * P],
                                            hT[:, 4 * half + c, i * P:(i + 1) * P], ident)
                    last.then_inc(ot_done, 1)

        @block.scalar
        def _(act):
            def copy(out_, in_, s, **kw):
                act.activation(out_, in_, ACT.Copy, **kw).then_inc(s, 1)

            def squares(ni, src, ready, n=S):
                for c in range(KC):
                    ready(c)
                    if ni * KC + c >= 2:
                        act.wait_ge(n_acc, ni * KC + c - 1)
                    act.activation(W[c % 2][:, 0:n], src[:, c, :], ACT.Square).then_inc(n_sq, 1)

            def norm_std(ni, n=S, groups=1, b=0):
                act.wait_ge(n_acc, ni * KC + KC)
                for g in range(groups):
                    act.activation(W[2 + g][:, 0:n], bank[b + g][:, 0:n], ACT.Sqrt, scale=groups / D, bias=EPS).then_inc(n_std, 1)

            def norm_hi(ni, dst, n=S):
                for c in range(KC):
                    act.wait_ge(n_t, SCALED[ni] * KC + c + 1)
                    act.activation(dst[:, c, :], W[4 + c % 2][:, 0:n], ACT.Copy).then_inc(n_hi, 1)

            def gained_hi(ni, g0, ready):
                for c in range(KC):
                    ready(c)
                    act.activation(u_hi[:, c, :], hT[:, c, :], ACT.Identity, scale=gain[:, g0 + c:g0 + c + 1]).then_inc(n_hi, 1)
                squares(ni, hT, lambda c: None)
                norm_std(ni, b=SUM_BANK)

            def ffn(fi):
                def silu(f, k, first):
                    act.wait_ge(f_gate, fi * FT + f + 1)
                    if not first:
                        act.wait_ge(f_prod, fi * FT + f - 1)
                    act.activation(W[6 + k], W[k], ACT.Silu).then_inc(f_silu, 1)

                def high(f, k):
                    act.wait_ge(f_prod, fi * FT + f + 1)
                    act.activation(hid_hi[:, f, :], W[8 + k], ACT.Copy).then_inc(f_hi, 1)

                def two(it, first):
                    for k in range(2):
                        f = 2 * it + k
                        silu(f, k, first)
                        high(f, k)
                two(0, True)
                with act.Fori(1, FT // 2) as it:
                    two(it, False)

            def head_square(i, u, b, sq, rw, n=S):
                act.wait_ge(unit_done, u + 1)
                act.activation(sq[:, 0:n], bank[b][:, 0:n], ACT.Square).then_inc(h_sq, 1)
                copy(rw[:, 0:n], bank[b][:, 0:n], h_raw)

            def head_std(i, b, sq, width, n=S):
                act.wait_ge(h_sum, i + 1)
                act.activation(sq[:, 0:n], bank[b][:, 0:n], ACT.Sqrt, scale=1.0 / width, bias=EPS).then_inc(h_std, 1)

            def raw_copy(u, b, dst):
                act.wait_ge(unit_done, u + 1)
                copy(dst, bank[b][:], r_raw)

            def value_copy(u, b, dst, n=S):
                act.wait_ge(unit_done, u + 1)
                copy(dst[:, 0:n], bank[b][:, 0:n], v_raw)

            def attend(done, heads, put):
                s0, t0, b0, h0, g0 = done
                steps = steps_of(heads)

                def exps(h, i, kb, t, b):
                    job = heads[h]
                    o = bank[T_BANKS[t % 3]]
                    act.wait_ge(a_t, t0 + t + 1)
                    if kb is None:
                        r, k = job["rows"], job["sink"]
                        act.activation(sink_e[r], o[r, :], ACT.Exp, bias=sink_now[r, k:k + 1]).then_inc(a_e, 1)
                        return
                    nk = job["keys"](TT - 1)[1]
                    q0, q1 = q_blocks(job["keys"], kb)
                    c = slice(q0 * P, q1 * P)
                    if b >= nk:
                        act.wait_ge(a_pv, b0 + b - nk + 1)
                    act.activation(job["st"]["ph"][:, b % nk, c], o[:, 0:(q1 - q0) * P], ACT.Exp)
                    if b >= 3:
                        act.wait_ge(a_pl, b0 + b - 2)
                    act.activation(prob[b % 3][:, c], o[:, 0:(q1 - q0) * P], ACT.Exp).then_inc(a_e, 1)

                def output(h):
                    job = heads[h]
                    r, o = job["rows"], bank[O_BANKS[h % 2]]
                    act.wait_ge(a_pv, b0 + last_block(steps, h))
                    size = group(heads)
                    if h % size == 0 and not (isinstance(g0, int) and g0 + h == 0):
                        act.wait_ge(a_rec, g0 + h // size)
                    act.activation(put(r, h // size), o[r, :], ACT.Copy)
                    act.activation(den[r], bank[DEN_BANK][:] if job["den"] is None else o[job["den"], :],
                                   ACT.Copy).then_inc(a_o, 1)

                ends = {last_step(steps, h): h for h in range(len(heads))}
                for x in range(len(steps) + PV_LAG + 1):
                    if x < len(steps):
                        exps(*steps[x])
                    if x - PV_LAG - 1 in ends:
                        output(ends[x - PV_LAG - 1])

            def value_high(vt, b, st):
                act.wait_ge(v_t, vt + 1)
                for e in range(2):
                    last = act.activation(st["vh"][:, :, 2 * e * HD:(2 * e + 1) * HD],
                                          bank[b][:].rearrange("p (k n) -> p k n", k=TT)[:, :, e * HD:(e + 1) * HD],
                                          ACT.Copy)
                last.then_inc(s_hi, 1)

            act.dma_start(x_tok[:], t["x"][0].rearrange("(i p) d -> p i d", p=P)).then_inc(ld_x, 16)
            act.dma_start(const[:, 0:N_CONST], t["const"]).then_inc(ld_const, 16)
            act.wait_ge(gain_zero, 1)
            for row, name in ((G_F1, "ffn1_norm"), (G_MIX, "mix_norm"), (G_MEM, "mem_norm"), (G_F2, "ffn2_norm"),
                              (G_PRE2, "norm_mix_pre_2"), (G_POST2, "norm_mix_post_2"),
                              (G_FPRE2, "norm_ffn_pre_2"), (G_FPOST2, "norm_ffn_post_2")):
                act.dma_start(gain_rows[row:row + KC, :], t[name][0].rearrange("(c p) -> c p", p=P)).then_inc(ld_gain, 16)
            for k, name in enumerate(("group_norm_a_2", "group_norm_b_2")):
                act.dma_start(gain_rows[G_GN + 4 * k:G_GN + 4 * k + 4, :],
                              t[name][0].rearrange("(c p) -> c p", p=P)).then_inc(ld_gain, 16)
            for row, name in ((G_FQ, "fox_q_norm"), (G_FK, "fox_k_norm"), (G_DQ, "dsa_q_norm"), (G_DK, "dsa_k_norm"),
                              (G_QA, "q_norm_a_2"), (G_KA, "k_norm_a_2")):
                for h in range(2):
                    act.dma_start(gain_rows[row:row + 1, h * HD:(h + 1) * HD], t[name]).then_inc(ld_gain, 16)
            act.dma_start(gain_rows[G_MQ:G_MQ + 1, :], t["mem_q_norm"]).then_inc(ld_gain, 16)
            act.dma_start(gain_rows[G_MK:G_MK + 1, :], t["mem_k_norm"]).then_inc(ld_gain, 16)
            act.dma_start(gain_rows[G_BF:G_BF + 1, 0:HEADS], t["b_forget"]).then_inc(ld_gain, 16)
            act.dma_start(pos_i[:], t["positions"].to_broadcast([P, S])).then_inc(ld_pos, 16)
            act.dma_start(sink[:], t["sink_b_2"].to_broadcast([P, HEADS])).then_inc(ld_sink, 16)

            def x_here(c):
                act.wait_ge(x_ready, c + 1)
            act.wait_ge(gain_ready, 1)
            gained_hi(N_F1, G_F1, x_here)
            ffn(0)
            act.wait_ge(trig, N_ANGLE)
            act.activation(sin1[:], W[0], ACT.Sin).then_inc(trig_a, 1)
            act.activation(cos1[:], W[1], ACT.Sin).then_inc(trig_a, 1)

            def f_here(fi):
                return lambda c: act.wait_ge(f_out, fi * KC + c + 1)
            squares(N_MIX, hT, f_here(0))
            act.dma_start(m_tok[:], t["mem"][0].rearrange("(i p) d -> p i d", p=P)).then_inc(ld_mem, 16)
            norm_std(N_MIX)
            norm_hi(N_MIX, u_hi)
            act.wait_ge(n_lo, (N_MIX + 1) * KC)
            act.wait_ge(unit_done, U_PREP + 1)
            copy(W[7][0:HD], bank[0][0:HD, :], r_raw)
            raw_copy(U_PREP + 1, 1, W[2])
            head_square(H_PREP, U_PREP + 2, 2, W[0], W[1])
            value_copy(U_PREP + 3, 3, dvT[:])
            head_std(H_PREP, 4, W[0], HD)
            act.wait_ge(iw_t, 1)
            act.activation(iw_tok[:], bank[5][:, 0:TT * HD].rearrange("p (i n) -> p i n", i=TT)[:, :, 32:32 + HEADS],
                           ACT.Copy, scale=float(HEADS ** -0.5 * HD ** -0.5)).then_inc(iw_ready, 1)
            act.wait_ge(fg, 3)
            act.activation(W[9][0:HEADS], W[9][0:HEADS], ACT.Exp).then_inc(fg_a, 1)
            act.wait_ge(fg_a, 1)
            act.activation(W[9][0:HEADS], W[9][0:HEADS], ACT.Ln, bias=1.0).then_inc(fg_a, 1)
            for c in range(KC):
                act.wait_ge(mt_done, c + 1)
                copy(mT[:, c, :], bank[c][:, 0:MEM], m_ready)
            act.wait_ge(c_ready, 2)
            for part in range(2):
                act.dma_start(c_dram[part], c_sum[32 * part:32 * part + HEADS, :].bitcast(F32)).then_inc(c_stored, 16)
            squares(N_MEM, mT, lambda c: act.wait_ge(m_ready, c + 1), MEM)
            norm_std(N_MEM, MEM)
            norm_hi(N_MEM, m_hi, MEM)
            act.wait_ge(n_lo, (N_MEM + 1) * KC)

            def mem_head(i, st, second, first):
                u, h = U_MEM + 4 * i, H_MEM + 2 * i
                if second:
                    act.wait_ge(s_lo, S_MEM + 3 * i - 1)
                head_square(h, u, 2, W[0], W[1])
                if not first and not second:
                    act.wait_ge(a_out, i)
                head_square(h + 1, u + 1, 3, W[2], W[3], MEM)
                head_std(h, 6, W[0], P)
                value_copy(u + 2, 4, W[4], MEM)
                head_std(h + 1, 7, W[2], P, MEM)
                raw_copy(u + 3, 5, iq[:, bass.ds(i, 1), :].rearrange("p a n -> p (a n)"))
                act.wait_ge(h_out, h + 1)
                copy(st["qh"][:], W[1], s_hi)
                act.wait_ge(h_out, h + 2)
                copy(st["kh"][:], W[3][:, 0:MEM], s_hi)
                act.wait_ge(v_t, VT_MEM + i + 1)
                copy(st["vh"][:], bank[1][:, 0:MEM].rearrange("p (k n) -> p k n", k=MT), s_hi)

            def mem_pair(i, first):
                mem_head(2 * i, mst, False, first)
                mem_head(2 * i + 1, mst2, True, False)
                attend(done_before(A_MEM, (8, 4, 4, 2, 2), i), mem_heads, lambda r, g: oT[r, 8 + 2 * i + g, :])
            mem_pair(0, True)
            with act.Fori(1, 2) as i:
                mem_pair(i, False)

            def fox_pair(i, st, second):
                u, h = U_FOX + 4 * i, H_FOX + 2 * i
                if second:
                    act.wait_ge(s_lo, S_FOX + 3 * i - 1)
                head_square(h, u, 2, W[0], W[1])
                if not second:
                    act.wait_ge(a_out, A_FOX[4] + i)
                head_square(h + 1, u + 1, 3, W[2], W[3])
                head_std(h, 6, W[0], HD)
                value_copy(u + 2, 4, W[6])
                head_std(h + 1, 7, W[2], HD)
                act.wait_ge(h_out, h + 1)
                copy(st["qh"][:], W[1], s_hi)
                act.wait_ge(h_out, h + 2)
                copy(st["kh"][:], W[3], s_hi)
                value_high(VT_FOX + i, 1, st)
                raw_copy(u + 3, 5, dq[:, bass.ds(i, 1), :].rearrange("p a n -> p (a n)"))
            act.wait_ge(c_one, 2)
            act.wait_ge(c_stored, 32)
            with act.Fori(0, 2) as i:
                for k in range(2):
                    for dst_, r in ((c_q, 32 * k), (c_k, 32 * k + 2)):
                        act.dma_start(dst_[r:r + 2, :, :].bitcast(F32),
                                      c_dram[:, bass.ds(4 * i + 2 * k, 2), :]).then_inc(ld_c, 16)
                fox_pair(2 * i, fst, False)
                fox_pair(2 * i + 1, fst2, True)
                attend(done_before(A_FOX, (16, 16, 16, 4, 2), i), fox_heads, lambda r, g: oT[r, 2 * i + g, :])

            act.wait_ge(a_o, A_DSA[3])
            copy(ist["kh"][:], ik[:], s_hi)
            for i in range(4):
                copy(ist["qh"][:, i, :], iq[:, i, :], s_hi)

            def gate(i, k):
                act.wait_ge(unit_done, U_GATE + 4 * i + k + 1)
                act.activation(sig[:, 4 * i + k, :], bank[2 + k][:], ACT.Sigmoid).then_inc(g_sig, 1)
            for head in range(HEADS):
                for qt in range(1, TT):
                    n = 3 * head + qt - 1
                    act.wait_ge(ix_s, n + 1)
                    if n >= 3:
                        act.wait_ge(ix_acc, n - 2)
                    act.activation(W[n % 3][:, 0:(qt + 1) * P], bank[I_BANKS[n % 3]][:, 0:(qt + 1) * P],
                                   ACT.Relu).then_inc(ix_relu, 1)
                gate(head // 4, head % 4)
            act.wait_ge(a_out, A_DSA[4])
            with act.Fori(2, 6) as i:
                act.wait_ge(h_out, H_DQ + i - 2)
                act.activation(W[4], dq[:, bass.ds(i - 2, 1), :].rearrange("p a n -> p (a n)"), ACT.Square).then_inc(h_sq, 1)
                gate(i, 0)
                head_std(H_DQ + i - 2, 6, W[4], HD)
                for k in range(1, 4):
                    gate(i, k)

            act.wait_ge(r_out, R_DQ + 4)
            act.wait_ge(ix_acc, 24)
            copy(dst["kh"][:], dk[:], s_hi)
            value_high(VT_DSA, 1, dst)
            for k in range(4):
                copy((q_later[k - 1] if k else (dst["qh"],))[0][:], dq[:, k, :], s_hi)
            attend(A_DSA, dsa_heads, lambda r, g: oT[r, 4 + g, :])

            for n in BRANCH_ORDER:
                act.wait_ge(a_out, A_B2[4] if n == 1 else A_DSA[4])
                copy(o_hi[:, 4 * n:4 * n + 4, :], oT[:, 4 * n:4 * n + 4, :], o_split_hi)
            act.wait_ge(o_split, 3)
            with act.Fori(0, 4) as i:
                for k in range(2):
                    m = 2 * i + k
                    act.wait_ge(b_add, 4 * i + 3 + k)
                    act.activation(mix_hi[:, m, :], W[3 * k], ACT.Copy).then_inc(b_hi, 1)

            gained_hi(N_F2, G_F2, lambda c: act.wait_ge(res, c + 1))
            ffn(1)

            squares(N_PRE, hT, f_here(1))
            act.dma_start(tab2[:], t["rope2"]).then_inc(ld_tab, 16)
            norm_std(N_PRE)
            norm_hi(N_PRE, u_hi)
            act.wait_ge(n_lo, (N_PRE + 1) * KC)

            def key_head(i, first):
                u = U_B2 + 8 * i
                h, r, s, vt = H_B2 + 3 * i, R_B2 + 6 * i, S_B2 + 8 * i, VT_B2 + 2 * i
                head_square(h, u, 2, W[0], W[1])
                act.wait_ge(a_out, A_B2[4] + 4 * i)
                head_square(h + 1, u + 1, 3, W[5], W[6])
                head_std(h, 6, W[0], HD)
                head_square(h + 2, u + 2, 4, rtmp[:, 6, :], rtmp[:, 7, :])
                head_std(h + 1, 7, W[5], HD)
                raw_copy(u + 3, 5, W[3])
                head_std(h + 2, 0, rtmp[:, 6, :], HD)

                def high(k):
                    act.wait_ge(r_out, r + k + 1)
                    copy((ast["kh"], bst["kh"], *(q[0] for q in q2))[k][:], rtmp[:, k, :], s_hi,
                         scale=HD ** -0.5 if k in (3, 5) else 1.0)
                high(0)
                raw_copy(u + 4, 2, W[7])
                raw_copy(u + 5, 3, rtmp[:, 8, :])
                high(1)
                high(2)
                value_copy(u + 6, 4, W[2])
                high(3)
                value_copy(u + 7, 5, W[4])
                high(4)
                high(5)
                value_high(vt, 7, ast)
                value_high(vt + 1, 0, bst)
                copy(sink_now[:, 0:4], sink[:, bass.ds(4 * i, 4)], a_sink)
                attend(done_before(A_B2, (32, 36, 32, 8, 4), i), b2_heads,
                       lambda r, g: o2T[r, (g % 2) * 4 + 2 * i + g // 2, :])
            act.wait_ge(ld_sink, 16)
            key_head(0, True)
            with act.Fori(1, 2) as i:
                key_head(i, False)

            squares(N_GRP, o2T, lambda c: act.wait_ge(a_out, A_B2[4] + 8))
            norm_std(N_GRP, groups=2)
            norm_hi(N_GRP, u_hi)
            squares(N_POST, mo, lambda c: act.wait_ge(res, KC + c + 1))
            norm_std(N_POST, b=SUM_BANK)
            gained_hi(N_FPRE, G_FPRE2, lambda c: act.wait_ge(x_ready, KC + c + 1))
            ffn(2)
            squares(N_FPOST, fT, f_here(2))
            norm_std(N_FPOST)
            for i in range(TT):
                act.wait_ge(ot_done, 2 * i + 2)
                if i >= 2:
                    act.wait_ge(stored[i % 2], 16 * (i // 2))
                copy(out_tok[:, i % 2, 512:1024], bank[2 * (i % 2) + 1][:], o_ready_b)

        @block.vector
        def _(dve):
            def norm_recip(std_no, n=S, groups=1):
                for g in range(groups):
                    dve.wait_ge(n_std, std_no + g + 1)
                    dve.reciprocal(W[2 + g][:, 0:n], W[2 + g][:, 0:n]).then_inc(n_rec, 1)

            def norm_split(ni, std_no, src, g0, hi, lo, n=S, groups=1):
                norm_recip(std_no, n, groups)
                per = KC // groups

                def low(c):
                    dve.wait_ge(n_hi, SPLITS[ni] * KC + c + 1)
                    dve.tensor_tensor(lo[:, c, :], W[4 + c % 2][:, 0:n], hi[:, c, :].bitcast(F32),
                                      ALU.subtract).then_inc(n_lo, 1)
                dve.wait_ge(n_rec, std_no + groups)
                for c in range(KC):
                    if c >= 2:
                        dve.wait_ge(n_lo, SPLITS[ni] * KC + c - 1)
                    dve.scalar_tensor_tensor(out=W[4 + c % 2][:, 0:n], in0=src[:, c, :], scalar=gain[:, g0 + c:g0 + c + 1],
                                             in1=W[2 + c // per][:, 0:n], op0=ALU.mult, op1=ALU.mult).then_inc(n_t, 1)
                    if c:
                        low(c - 1)
                low(KC - 1)

            def gained_low(ni, g0, c):
                dve.wait_ge(n_hi, SPLITS[ni] * KC + c + 1)
                dve.scalar_tensor_tensor(out=u_lo[:, c, :], in0=hT[:, c, :], scalar=gain[:, g0 + c:g0 + c + 1],
                                         in1=u_hi[:, c, :].bitcast(F32), op0=ALU.mult, op1=ALU.subtract).then_inc(n_lo, 1)

            def ffn(fi, u0, ni, std_no, finish, between=None):
                norm_recip(std_no)
                dve.wait_ge(n_rec, std_no + 1)

                def two(it, first):
                    for k in range(2):
                        f = 2 * it + k
                        u = u0 + 4 * it + 2 * k
                        if not first:
                            dve.wait_ge(f_lo, fi * FT + f - 1)
                        dve.wait_ge(unit_done, u + 1)
                        dve.tensor_tensor(W[k], bank[2 * k][:], W[2], ALU.mult).then_inc(f_gate, 1)
                        dve.wait_ge(unit_done, u + 2)
                        dve.tensor_tensor(W[4 + k], bank[2 * k + 1][:], W[2], ALU.mult).then_inc(f_up, 1)
                        dve.wait_ge(f_up, fi * FT + f + 1)
                        dve.wait_ge(f_silu, fi * FT + f + 1)
                        dve.tensor_tensor(W[8 + k], W[6 + k], W[4 + k], ALU.mult).then_inc(f_prod, 1)
                        dve.wait_ge(f_hi, fi * FT + f + 1)
                        dve.tensor_tensor(hid_lo[:, f, :], W[8 + k], hid_hi[:, f, :].bitcast(F32),
                                          ALU.subtract).then_inc(f_lo, 1)
                two(0, True)
                with dve.Fori(1, FT // 2) as it:
                    two(it, False)
                if between:
                    between()
                for m in range(KC):
                    if m < KC - 1:
                        dve.wait_ge(f_tile, fi * (KC - 1) + m + 1)
                    else:
                        dve.wait_ge(unit_done, u0 + 3 * FT)
                    finish(m)

            def half_residual(m):
                dve.scalar_tensor_tensor(out=hT[:, m, :], in0=bank[m][:], scalar=0.5, in1=hT[:, m, :],
                                         op0=ALU.mult, op1=ALU.add).then_inc(f_out, 1)

            def head_norm(i, sq, rw, g, n=S):
                dve.wait_ge(h_std, i + 1)
                dve.reciprocal(sq[:, 0:n], sq[:, 0:n]).then_inc(h_rec, 1)
                dve.wait_ge(h_rec, i + 1)
                dve.scalar_tensor_tensor(out=rw[:, 0:n], in0=rw[:, 0:n], scalar=gain[:, g:g + 1], in1=sq[:, 0:n],
                                         op0=ALU.mult, op1=ALU.mult).then_inc(h_out, 1)

            def rope(j, src, b, cos, sin, tmp, dst_):
                if src is dst_:
                    dve.wait_ge(r_rot, j + 1)
                dve.tensor_tensor(dst_, src, cos, ALU.mult).then_inc(r_cos, 1)
                if not isinstance(j, int) or j:
                    dve.wait_ge(r_out, j)
                dve.wait_ge(r_rot, j + 1)
                dve.tensor_tensor(tmp, bank[b][:], sin, ALU.mult).then_inc(r_sin, 1)
                dve.wait_ge(r_cos, j + 1)
                dve.wait_ge(r_sin, j + 1)
                dve.tensor_tensor(dst_, dst_, tmp, ALU.add).then_inc(r_out, 1)

            def low(i, dst_, src, hi):
                dve.wait_ge(s_hi, i + 1)
                dve.tensor_tensor(dst_, src, hi.bitcast(F32), ALU.subtract).then_inc(s_lo, 1)

            def attend(done, heads, put, sink0=0):
                s0, t0, b0, h0, g0 = done
                steps = steps_of(heads)
                sunk = [h for h, job in enumerate(heads) if job["sink"] is not None]

                def maxes(h, qt):
                    lo, hi = heads[h]["keys"](qt)
                    n = h * TT + qt
                    dve.wait_ge(a_s, s0 + n + 1)
                    dve.tensor_reduce(rowmax[:, h % 2, qt:qt + 1], bank[S_BANKS[n % 2]][:, 0:(hi - lo) * P], AX.X,
                                      ALU.max, negate=h not in sunk).then_inc(a_max, 1)

                def diagonal(h):
                    dve.wait_ge(a_max, s0 + TT * (h + 1))
                    neg = rowmax
                    if h in sunk:
                        neg = negmax
                        k = heads[h]["sink"]
                        dve.tensor_scalar(negmax[:, h % 2, :], rowmax[:, h % 2, :], sink_now[:, k:k + 1], -1.0, ALU.max,
                                          ALU.mult).then_inc(a_neg, 1)
                        dve.wait_ge(a_neg, 2 * sink0 + sunk.index(h) + 1)
                    for qt in range(TT):
                        last = dve.tensor_scalar(shift[:, h % 2, qt * P:(qt + 1) * P], ident, neg[:, h % 2, qt:qt + 1],
                                                 None, ALU.mult)
                    last.then_inc(a_shift, 1)

                def low_part(h, i, kb, t, b):
                    job = heads[h]
                    nk = job["keys"](TT - 1)[1]
                    q0, q1 = q_blocks(job["keys"], kb)
                    c = slice(q0 * P, q1 * P)
                    dve.wait_ge(a_e, t0 + t + 1)
                    dve.tensor_tensor(job["st"]["pl"][:, b % nk, c], prob[b % 3][:, c],
                                      job["st"]["ph"][:, b % nk, c].bitcast(F32), ALU.subtract).then_inc(a_pl, 1)

                def output(g):
                    last = (g + 1) * group(heads) - 1
                    dve.wait_ge(a_o, h0 + last + 1)
                    if last in sunk:
                        k = sink0 + sunk.index(last) // 2 + 1
                        dve.wait_ge(a_e, t0 + max(x[3] for x in steps if x[0] == last) + 1)
                        dve.tensor_tensor(den, den, sink_e, ALU.add).then_inc(a_den, 1)
                        dve.wait_ge(a_den, k)
                    if g:
                        dve.wait_ge(a_out, g0 + g)
                    dve.reciprocal(inverse, den).then_inc(a_rec, 1)
                    dve.wait_ge(a_rec, g0 + g + 1)
                    o = put(slice(0, P), g)
                    dve.tensor_tensor(o, o, inverse, ALU.mult).then_inc(a_out, 1)

                for qt in range(TT):
                    maxes(0, qt)
                diagonal(0)
                size = group(heads)
                steps_in = max(i for h, i, *_ in steps if h == 0) + 1
                ends = {last_step(steps, (g + 1) * size - 1): g for g in range(len(heads) // size)}
                for x in range(len(steps) + PV_LAG + 3):
                    h, i = steps[x][:2] if x < len(steps) else (len(heads), 0)
                    if h + 1 < len(heads) and i < TT // 2:
                        maxes(h + 1, 2 * i)
                        maxes(h + 1, 2 * i + 1)
                    if h + 1 < len(heads) and i == min(TT // 2, steps_in - 1):
                        diagonal(h + 1)
                    if 1 <= x <= len(steps) and steps[x - 1][2] is not None:
                        low_part(*steps[x - 1])
                    if x - PV_LAG - 2 in ends:
                        output(ends[x - PV_LAG - 2])

            def value_low(i, st, b):
                dve.wait_ge(s_hi, i + 1)
                for e in range(2):
                    c = slice(2 * e * HD, (2 * e + 1) * HD)
                    last = dve.tensor_tensor(st["vl"][:, :, c],
                                             bank[b][:].rearrange("p (k n) -> p k n", k=TT)[:, :, e * HD:(e + 1) * HD],
                                             st["vh"][:, :, c].bitcast(F32), ALU.subtract)
                last.then_inc(s_lo, 1)

            def value_ones(st):
                dve.memset(st["vh"][:, :, HD:2 * HD].bitcast(F32), 1.0)
                dve.memset(st["vl"][:, :, HD:2 * HD].bitcast(F32), 0.0)

            def norm_add(ni, std_no, src, g0, x0, also=None):
                norm_recip(std_no)
                dve.wait_ge(n_rec, std_no + 1)

                def add(c):
                    dve.wait_ge(n_t, SCALED[ni] * KC + c + 1)
                    dve.tensor_tensor(hT[:, c, :], hT[:, c, :], W[4 + c % 2], ALU.add).then_inc(x_ready, 1)
                for c in range(KC):
                    if c >= 2:
                        dve.wait_ge(x_ready, x0 + c - 1)
                    dve.scalar_tensor_tensor(out=W[4 + c % 2], in0=src[:, c, :], scalar=gain[:, g0 + c:g0 + c + 1],
                                             in1=W[2], op0=ALU.mult, op1=ALU.mult).then_inc(n_t, 1)
                    if c:
                        add(c - 1)
                    if c >= 2 and also:
                        also(c - 2)
                add(KC - 1)
                if also:
                    also(KC - 2)
                    also(KC - 1)

            dve.memset(gain_rows[:], 0.0).then_inc(gain_zero, 1)
            for c in range(KC):
                dve.wait_ge(xt_done, c + 1)
                dve.tensor_copy(hT[:, c, :], bank[c][:]).then_inc(x_ready, 1)
            dve.wait_ge(gain_t, 1)
            dve.tensor_copy(gain[:, 0:N_GAIN], bank[1][:, 0:N_GAIN]).then_inc(const_r, 1)
            dve.wait_ge(const_r, 1)
            for g, scale in ((G_FQ, HD ** -0.5), (G_DQ, HD ** -0.5), (G_QA, HD ** -0.5), (G_MQ, P ** -0.5)):
                last = dve.tensor_scalar(gain[:, g:g + 1], bank[1][:, g:g + 1], float(scale), None, ALU.mult)
            last.then_inc(gain_ready, 1)
            dve.wait_ge(gain_ready, 1)
            for c in range(KC):
                gained_low(N_F1, G_F1, c)
            dve.wait_ge(ld_const, 16)
            dve.tensor_copy(ident_r[:], ident)
            dve.tensor_copy(ones_r[:], ones)
            dve.memset(zero_r[:].bitcast(F32), 0.0)
            dve.tensor_copy(masks_r[:], const[:, C_CAUSAL:C_CAUSAL + 3 * P].rearrange("p (m n) -> p m n", m=3))


            def angles():
                step = [0]

                def link(ins):
                    step[0] += 1
                    ins.then_inc(trig, 1)
                    dve.wait_ge(trig, step[0])
                ROUND = 12582912.0
                PI = 3.1415925
                TWO_PI = (6.28125, 0.0019350051879882812, 3.0199159819567e-07)
                a, n, m = W[3], W[4], W[5]
                dve.wait_ge(ld_pos, 16)
                link(dve.tensor_copy(a, pos_i[:]))
                link(dve.tensor_scalar(a, a, const[:, C_FREQ:C_FREQ + 1], None, ALU.mult))
                link(dve.tensor_scalar(n, a, 1.0 / 6.283185307179586, ROUND, ALU.mult, ALU.add))
                link(dve.tensor_scalar(n, n, ROUND, None, ALU.subtract))
                link(dve.tensor_scalar(m, a, 1.0 / 6.283185307179586, 0.25, ALU.mult, ALU.add))
                link(dve.tensor_scalar(m, m, ROUND, None, ALU.add))
                link(dve.tensor_scalar(m, m, ROUND, None, ALU.subtract))
                for dst_, turns, quarter in ((W[0], n, 0.0), (W[1], m, 1.5707963267948966)):
                    src = a
                    for part in TWO_PI:
                        link(dve.scalar_tensor_tensor(out=dst_, in0=turns, scalar=-part, in1=src,
                                                      op0=ALU.mult, op1=ALU.add))
                        src = dst_
                    link(dve.tensor_scalar(dst_, dst_, quarter, PI, ALU.add, ALU.min))
                    link(dve.tensor_scalar(dst_, dst_, -PI, None, ALU.max))
                assert step[0] == N_ANGLE
                dve.wait_ge(trig_a, 2)
                link(dve.tensor_scalar(sin1[:], sin1[:], const[:, C_SIGN:C_SIGN + 1], None, ALU.mult))

            ffn(0, U_GU1, N_F1, N_F1, half_residual, angles)

            norm_split(N_MIX, N_MIX, hT, G_MIX, u_hi, u_lo)
            dve.memset(W[6][0:HEADS], 1.0).then_inc(fg, 1)
            dve.wait_ge(r_raw, RR_PREP + 1)
            z, e = W[8][0:HEADS], W[9][0:HEADS]
            dve.tensor_scalar(z, W[7][0:HEADS], gain[0:HEADS, G_BF:G_BF + 1], None, ALU.add).then_inc(fg, 1)
            dve.wait_ge(fg, 2)
            dve.scalar_tensor_tensor(out=e, in0=z, scalar=-1.0, in1=z, op0=ALU.mult, op1=ALU.min).then_inc(fg, 1)
            head_norm(H_PREP, W[0], W[1], G_DK)
            rope(R_PREP, W[2], 6, cos1[:], sin1[:], W[4], ik[:])
            dve.wait_ge(h_out, H_PREP + 1)
            rope(R_PREP + 1, W[1], 7, cos1[:], sin1[:], W[5], dk[:])
            dve.wait_ge(fg_a, 2)
            dve.scalar_tensor_tensor(out=z, in0=z, scalar=0.0, in1=e, op0=ALU.min, op1=ALU.subtract).then_inc(fg, 1)
            dve.wait_ge(fg, 4)
            dve.tensor_tensor_scan(e, W[6][0:HEADS], z, 0.0, ALU.mult, ALU.add).then_inc(fg, 1)
            dve.wait_ge(fg, 5)
            dve.tensor_copy(c_sum[0:HEADS, :], e).then_inc(c_ready, 1)
            dve.wait_ge(c_ready, 1)
            dve.tensor_tensor(c_sum[32:32 + HEADS, :], e, c_sum[0:HEADS, :].bitcast(F32), ALU.subtract).then_inc(c_ready, 1)
            norm_split(N_MEM, N_MEM, mT, G_MEM, m_hi, m_lo, MEM)

            def mem_head(i, st):
                h, s = H_MEM + 2 * i, S_MEM + 3 * i
                head_norm(h, W[0], W[1], G_MQ)
                head_norm(h + 1, W[2], W[3], G_MK, MEM)
                low(s, st["ql"][:], W[1], st["qh"][:])
                low(s + 1, st["kl"][:], W[3][:, 0:MEM], st["kh"][:])
                low(s + 2, st["vl"][:], bank[1][:, 0:MEM].rearrange("p (k n) -> p k n", k=MT), st["vh"][:])
            with dve.Fori(0, 2) as i:
                mem_head(2 * i, mst)
                mem_head(2 * i + 1, mst2)
                attend(done_before(A_MEM, (8, 4, 4, 2, 2), i), mem_heads, lambda r, g: oT[r, 8 + 2 * i + g, :])

            value_ones(fst)
            value_ones(fst2)
            dve.memset(c_q[:].bitcast(F32), -1.0).then_inc(c_one, 1)
            dve.memset(c_k[:].bitcast(F32), 1.0).then_inc(c_one, 1)

            def fox_pair(i, st):
                h, s = H_FOX + 2 * i, S_FOX + 3 * i
                q = iq[:, bass.ds(i, 1), :].rearrange("p a n -> p (a n)")
                rope(R_IQ + i, q, 0, cos1[:], sin1[:], W[7], q)
                head_norm(h, W[0], W[1], G_FQ)
                head_norm(h + 1, W[2], W[3], G_FK)
                low(s, st["ql"][:], W[1], st["qh"][:])
                low(s + 1, st["kl"][:], W[3], st["kh"][:])
                value_low(s + 2, st, 1)
            with dve.Fori(0, 2) as i:
                fox_pair(2 * i, fst)
                fox_pair(2 * i + 1, fst2)
                attend(done_before(A_FOX, (16, 16, 16, 4, 2), i), fox_heads, lambda r, g: oT[r, 2 * i + g, :])

            low(S_IDX, ist["kl"][:], ik[:], ist["kh"][:])
            for i in range(4):
                low(S_IDX + 1 + i, ist["ql"][:, i, :], iq[:, i, :], ist["qh"][:, i, :])

            def index_pair(i, first):
                for k in range(6):
                    e, qt = k // 3, 1 + k % 3
                    n = (qt + 1) * P
                    sc, weight = score[:, qt, 0:n], iw_tok[:, qt, bass.ds(2 * i + e, 1)]
                    dve.wait_ge(ix_relu, 6 * i + k + 1)
                    if first and e == 0:
                        dve.tensor_scalar(sc, W[k % 3][:, 0:n], weight, None, ALU.mult).then_inc(ix_acc, 1)
                    else:
                        dve.wait_ge(ix_acc, 6 * i + k - 2)
                        dve.scalar_tensor_tensor(out=sc, in0=W[k % 3][:, 0:n], scalar=weight, in1=sc,
                                                 op0=ALU.mult, op1=ALU.add).then_inc(ix_acc, 1)
            index_pair(0, True)
            with dve.Fori(1, 4) as i:
                index_pair(i, False)
            dve.wait_ge(ix_acc, 24)
            for qt in range(1, TT):
                d = score[:, qt, qt * P:(qt + 1) * P]
                dve.tensor_tensor(d, d, const[:, C_CAUSAL:C_CAUSAL + P], ALU.add).then_inc(tk_rep, 1)
            dve.wait_ge(tk_rep, TT - 1)
            found = dve.alloc_register("found")

            def top_round(r):
                for qt in range(1, TT):
                    dve.max(best8[:, qt, :], score[:, qt, 0:(qt + 1) * P]).then_inc(tk_max, 1)
                for qt in range(1, TT):
                    sc = score[:, qt, 0:(qt + 1) * P]
                    dve.reg_mov(found, (TT - 1) * r + qt)
                    dve.wait_ge(ix_acc, 24)
                    dve.wait_ge(tk_max, found)
                    dve.match_replace(sc, best8[:, qt, :], sc, TAKEN).then_inc(tk_rep, 1)
                dve.reg_mov(found, (TT - 1) * r + 2 * (TT - 1))
                dve.wait_ge(ix_acc, 24)
                dve.wait_ge(tk_rep, found)
            with dve.Fori(0, 4) as i:
                q = dq[:, bass.ds(i, 1), :].rearrange("p a n -> p (a n)")
                for r in range(TOP_ROUNDS // 4):
                    top_round(TOP_ROUNDS // 4 * i + r)
                head_norm(H_DQ + i, W[4], q, G_DQ)
                dve.wait_ge(h_out, H_DQ + i + 1)
                rope(R_DQ + i, q, 7, cos1[:], sin1[:], W[5], q)
            for qt in range(1, TT):
                dve.tensor_scalar(topmask[:, qt, 0:(qt + 1) * P], score[:, qt, 0:(qt + 1) * P], TAKEN / 2, NEG,
                                  ALU.is_gt, ALU.mult).then_inc(tk_mask, 1)

            low(S_DSA, dst["kl"][:], dk[:], dst["kh"][:])
            value_ones(dst)
            value_low(S_DSA + 1, dst, 1)
            for k in range(4):
                hi, lo = q_later[k - 1] if k else (dst["qh"], dst["ql"])
                low(S_DSA + 2 + k, lo[:], dq[:, k, :], hi[:])
            attend(A_DSA, dsa_heads, lambda r, g: oT[r, 4 + g, :])

            for place, n in enumerate(BRANCH_ORDER):
                c = slice(4 * n, 4 * n + 4)
                dve.wait_ge(o_split_hi, place + 1)
                dve.tensor_tensor(o_lo[:, c, :], oT[:, c, :], o_hi[:, c, :].bitcast(F32), ALU.subtract).then_inc(o_split, 1)

            def mixed(mp, first):
                if not first:
                    dve.wait_ge(b_lo, 2 * mp)
                for place, n in enumerate(BRANCH_ORDER):
                    dve.wait_ge(unit_done, U_BR + 3 * mp + place + 1)
                    for half in range(2):
                        dve.tensor_tensor(W[3 * half + n], bank[2 * n + half][:], sig[:, KC * n + 2 * mp + half, :],
                                          ALU.mult).then_inc(b_mul, 1)
                for half in range(2):
                    dve.wait_ge(b_mul, 6 * mp + 5 + half)
                    dve.tensor_tensor(W[3 * half], W[3 * half], W[3 * half + 1], ALU.add).then_inc(b_add, 1)
                for half in range(2):
                    dve.wait_ge(b_add, 4 * mp + 1 + half)
                    dve.tensor_tensor(W[3 * half], W[3 * half], W[3 * half + 2], ALU.add).then_inc(b_add, 1)
                for half in range(2):
                    dve.wait_ge(b_hi, 2 * mp + half + 1)
                    dve.tensor_tensor(mix_lo[:, 2 * mp + half, :], W[3 * half], mix_hi[:, 2 * mp + half, :].bitcast(F32),
                                      ALU.subtract).then_inc(b_lo, 1)
            mixed(0, True)
            with dve.Fori(1, 4) as mp:
                mixed(mp, False)
            for m in range(KC):
                dve.wait_ge(unit_done, U_WO + m + 1)
                dve.tensor_tensor(hT[:, m, :], bank[m % 4][:], hT[:, m, :], ALU.add).then_inc(res, 1)
                if 1 <= m <= 4:
                    gained_low(N_F2, G_F2, m - 1)
            for c in range(4, KC):
                gained_low(N_F2, G_F2, c)

            ffn(1, U_GU2, N_F2, N_F2, half_residual)

            norm_split(N_PRE, N_PRE, hT, G_PRE2, u_hi, u_lo)
            dve.wait_ge(ld_tab, 16)
            value_ones(ast)
            value_ones(bst)

            def key_head(i):
                h, r, s = H_B2 + 3 * i, R_B2 + 6 * i, S_B2 + 8 * i
                tmp = W[8]

                def turn(k, src, b):
                    rope(r + k, src, b, tab2[:, 2 * (k % 2), :], tab2[:, 2 * (k % 2) + 1, :], tmp, rtmp[:, k, :])
                def low_of(k):
                    hi, lo = ((ast["kh"], ast["kl"]), (bst["kh"], bst["kl"]), *q2)[k]
                    dve.wait_ge(s_hi, s + k + 1)
                    if k in (3, 5):
                        dve.scalar_tensor_tensor(out=lo[:], in0=rtmp[:, k, :], scalar=float(HD ** -0.5),
                                                 in1=hi[:].bitcast(F32), op0=ALU.mult, op1=ALU.subtract).then_inc(s_lo, 1)
                    else:
                        dve.tensor_tensor(lo[:], rtmp[:, k, :], hi[:].bitcast(F32), ALU.subtract).then_inc(s_lo, 1)

                head_norm(h, W[0], W[1], G_KA)
                head_norm(h + 1, W[5], W[6], G_QA)
                dve.wait_ge(h_out, h + 1)
                turn(0, W[1], 1)
                dve.wait_ge(r_raw, RR_B2 + 3 * i + 1)
                turn(1, W[3], 6)
                low_of(0)
                head_norm(h + 2, rtmp[:, 6, :], rtmp[:, 7, :], G_QA)
                dve.wait_ge(h_out, h + 2)
                turn(2, W[6], 7)
                low_of(1)
                dve.wait_ge(r_raw, RR_B2 + 3 * i + 2)
                turn(3, W[7], 0)
                low_of(2)
                dve.wait_ge(h_out, h + 3)
                turn(4, rtmp[:, 7, :], 1)
                low_of(3)
                dve.wait_ge(r_raw, RR_B2 + 3 * i + 3)
                turn(5, rtmp[:, 8, :], 6)
                low_of(4)
                low_of(5)
                value_low(s + 6, ast, 7)
                value_low(s + 7, bst, 0)
                dve.wait_ge(a_sink, i + 1)
                attend(done_before(A_B2, (32, 36, 32, 8, 4), i), b2_heads, sink0=2 * i,
                       put=lambda r, g: o2T[r, (g % 2) * 4 + 2 * i + g // 2, :])
            with dve.Fori(0, 2) as i:
                key_head(i)

            norm_split(N_GRP, N_GRP, o2T, G_GN, u_hi, u_lo, groups=2)
            for m in range(KC):
                dve.wait_ge(unit_done, U_WO2 + m + 1)
                dve.tensor_copy(mo[:, m, :], bank[m % 4][:]).then_inc(res, 1)
            norm_add(N_POST, N_POST + 1, mo, G_POST2, KC, lambda c: gained_low(N_FPRE, G_FPRE2, c))


            def to_fT(m):
                dve.tensor_copy(fT[:, m, :], bank[m][:]).then_inc(f_out, 1)
            ffn(2, U_GU3, N_FPRE, N_FPRE + 1, to_fT)
            norm_add(N_FPOST, N_FPOST + 1, fT, G_FPOST2, 2 * KC)
            for i in range(TT):
                dve.wait_ge(ot_done, 2 * i + 1)
                if i >= 2:
                    dve.wait_ge(stored[i % 2], 16 * (i // 2))
                dve.tensor_copy(out_tok[:, i % 2, 0:512], bank[2 * (i % 2)][:]).then_inc(o_ready_a, 1)


def constants():
    import numpy as np

    c = np.zeros((P, N_CONST), np.float32)
    i = np.arange(P)
    c[:, C_ID:C_ID + P] = np.eye(P)
    c[:, C_ONE:C_ONE + P] = 1.0
    c[:, C_BLK:C_BLK + P] = i[:, None] // HD == i[None, :] // HD
    c[i, C_ROT + (i ^ 32)] = 1.0
    c[:, C_CAUSAL:C_CAUSAL + P] = np.where(i[None, :] > i[:, None], NEG, 0.0)
    c[:, C_UP:C_UP + P] = np.where(i[None, :] > i[:, None], NEG, 0.0)
    c[:, C_LOW:C_LOW + P] = np.where(i[None, :] < i[:, None], NEG, 0.0)
    pairs = np.arange(0, HD, 2, dtype=np.float32) / np.float32(HD)
    freq = np.power(np.float32(10000.0), -pairs).astype(np.float32)
    c[:, C_FREQ] = freq[i % 32]
    sign = np.where(i % HD < 32, -1.0, 1.0).astype(np.float32)
    c[:, C_SIGN] = sign
    t = np.arange(S)
    f16 = np.power(np.float32(10000.0), -(np.arange(16, dtype=np.float32) / np.float32(16))).astype(np.float32)
    axial = np.concatenate([(t // 64).astype(np.float32)[:, None] * f16, (t % 64).astype(np.float32)[:, None] * f16], 1)
    f32 = np.power(np.float32(10000.0), -(np.arange(32, dtype=np.float32) / np.float32(32))).astype(np.float32)
    token = t.astype(np.float32)[:, None] * f32
    rope2 = np.empty((P, 4, S), np.float32)
    for k, a in enumerate((axial, token)):
        rope2[:, 2 * k] = np.cos(a).T[i % 32]
        rope2[:, 2 * k + 1] = np.sin(a).T[i % 32] * sign[:, None]
    return {"const": c, "rope2": rope2}


_INS = [
    "x", "mem", "positions", "ffn1_norm", "ffn1_w_gate", "ffn1_w_up", "ffn1_w_down", "mix_norm", "mem_norm", "w_in",
    "b_forget", "fox_q_norm", "fox_k_norm", "dsa_q_norm", "dsa_k_norm", "mem_q_norm", "mem_k_norm", "w_mem_kv",
    "w_branch", "w_out", "ffn2_norm", "ffn2_w_gate", "ffn2_w_up", "ffn2_w_down", "norm_mix_pre_2", "w_in_2",
    "q_norm_a_2", "k_norm_a_2", "sink_b_2", "group_norm_a_2", "group_norm_b_2", "w_out_2", "norm_mix_post_2",
    "norm_ffn_pre_2", "w_gate_2", "w_up_2", "w_down_2", "norm_ffn_post_2",
]


def kernel(**inputs):
    import numpy as np
    import concourse.bacc as bacc
    from concourse.bass_utils import run_bass_kernel_spmd

    nc = bacc.Bacc("TRN2", target_bir_lowering=False, num_devices=1)
    arrays, args = {}, {}
    given = {name: np.ascontiguousarray(inputs[name]) for name in _INS}
    for name, a in {**given, **constants()}.items():
        arrays[f"in_{name}"] = a
        args[name] = nc.dram_tensor(f"in_{name}", a.shape, mybir.dt.from_np(a.dtype), kind="ExternalInput").ap()
    out = nc.dram_tensor("out_0", (1, S, D), F32, kind="ExternalOutput").ap()
    two_blocks(nc, args, out)
    r = run_bass_kernel_spmd(nc, [arrays], core_ids=[0])
    return r.results[0]["out_0"]
```
